# Optimizing a Trainium2 kernel written in Bass

```python
import math
import jax, jax.numpy as jnp
from jax import lax
import numpy as np

D_MODEL = 1024
BATCH = 1
SEQ = 256
DEPTH = 2

PLE_DIM = 256
DIFF_HEADS = 8
DIFF_HEAD_DIM = 64
DIFF_V_DIM = 2 * DIFF_HEAD_DIM
MLA_HEADS = 8
MLA_Q_RANK = 384
MLA_KV_RANK = 256
MLA_NOPE_DIM = 64
MLA_ROPE_DIM = 32
MLA_V_DIM = 64
ROPE_THETA = 10000.0
REL_BUCKETS = 32
REL_MAX_DIST = 128
DENSE_FF = 2816
N_EXPERTS = 8
TOP_K = 2
EXPERT_FF = 3584
EXPERT_BLOCK = 128
Q_BLOCK = 128
EPS = 1e-5
DEEPNORM_ALPHA = (2.0 * DEPTH) ** 0.25
DEEPNORM_BETA = (8.0 * DEPTH) ** -0.25
N_DENSE = (DEPTH + 1) // 2
N_MOE = DEPTH // 2

DIFF_Q_COLS = DIFF_HEADS * 2 * DIFF_HEAD_DIM
DIFF_K_COLS = DIFF_HEADS * 2 * DIFF_HEAD_DIM
DIFF_V_COLS = DIFF_HEADS * DIFF_V_DIM
GATE_COLS = 2 * D_MODEL
IN_SIZES = (DIFF_Q_COLS, DIFF_K_COLS, DIFF_V_COLS, MLA_Q_RANK, MLA_KV_RANK, MLA_ROPE_DIM, GATE_COLS)
IN_SPLIT_IDX = [sum(IN_SIZES[:j + 1]) for j in range(len(IN_SIZES) - 1)]
IN_COLS = sum(IN_SIZES)


def _layernorm(x, g, b):
    xf = x.astype(jnp.float32)
    mu = jnp.mean(xf, axis=-1, keepdims=True)
    var = jnp.mean(jnp.square(xf - mu), axis=-1, keepdims=True)
    y = (xf - mu) * lax.rsqrt(var + EPS) * g.astype(jnp.float32) + b.astype(jnp.float32)
    return y.astype(x.dtype)

def _rmsnorm(x, g):
    xf = x.astype(jnp.float32)
    y = xf * lax.rsqrt(jnp.mean(jnp.square(xf), axis=-1, keepdims=True) + EPS) * g.astype(jnp.float32)
    return y.astype(x.dtype)

def _rope(x, pos):
    half = x.shape[-1] // 2
    inv_freq = ROPE_THETA ** (-jnp.arange(half, dtype=jnp.float32) / half)
    ang = pos.astype(jnp.float32)[:, :, None] * inv_freq
    c = jnp.cos(ang)[:, :, None, :]
    s = jnp.sin(ang)[:, :, None, :]
    xf = x.astype(jnp.float32)
    x1, x2 = xf[..., :half], xf[..., half:]
    return jnp.concatenate([x1 * c - x2 * s, x1 * s + x2 * c], axis=-1).astype(x.dtype)

def _t5_bucket(dist):
    n = jnp.maximum(dist, 0)
    max_exact = REL_BUCKETS // 2
    large = max_exact + (jnp.log(jnp.maximum(n, 1).astype(jnp.float32) / max_exact)
                         / math.log(REL_MAX_DIST / max_exact) * (REL_BUCKETS - max_exact)).astype(jnp.int32)
    large = jnp.minimum(large, REL_BUCKETS - 1)
    return jnp.where(n < max_exact, n, large)

def _t5_bias(table, q_pos, k_pos):
    bucket = _t5_bucket(q_pos[:, :, None] - k_pos[:, None, :])
    return jnp.transpose(table[bucket].astype(jnp.float32), (0, 3, 1, 2))

def _causal_mask(q0, kend):
    return jnp.arange(kend)[None, :] <= (q0 + jnp.arange(Q_BLOCK))[:, None]

def _diff_attention(q, k, v, pos, rel_table, lam, lam_init, subln_g):
    B, S, H = q.shape[0], q.shape[1], q.shape[2]
    scale = DIFF_HEAD_DIM ** -0.5
    outs = []
    for q0 in range(0, S, Q_BLOCK):
        kend = q0 + Q_BLOCK
        s = jnp.einsum('bqhmd,bkhmd->bhmqk', q[:, q0:kend], k[:, :kend]).astype(jnp.float32) * scale
        s = s + _t5_bias(rel_table, pos[:, q0:kend], pos[:, :kend])[:, :, None]
        s = jnp.where(_causal_mask(q0, kend), s, -jnp.inf)
        a = jax.nn.softmax(s, axis=-1)
        w = a[:, :, 0] - lam * a[:, :, 1]
        outs.append(jnp.einsum('bhqk,bkhe->bqhe', w.astype(v.dtype), v[:, :kend]))
    o = jnp.concatenate(outs, axis=1)
    o = _rmsnorm(o, subln_g) * (1.0 - lam_init)
    return o.reshape(B, S, H * DIFF_V_DIM)

def _mla(c_q, c_kv, k_r, pos, q_norm_g, w_uq, kv_norm_g, w_ukv):
    B, S = c_q.shape[0], c_q.shape[1]
    q = (_rmsnorm(c_q, q_norm_g) @ w_uq).reshape(B, S, MLA_HEADS, MLA_NOPE_DIM + MLA_ROPE_DIM)
    q_nope, q_rope = q[..., :MLA_NOPE_DIM], _rope(q[..., MLA_NOPE_DIM:], pos)
    kv = (_rmsnorm(c_kv, kv_norm_g) @ w_ukv).reshape(B, S, MLA_HEADS, MLA_NOPE_DIM + MLA_V_DIM)
    k_nope, v = kv[..., :MLA_NOPE_DIM], kv[..., MLA_NOPE_DIM:]
    k_rope = _rope(k_r[:, :, None, :], pos)[:, :, 0]
    scale = (MLA_NOPE_DIM + MLA_ROPE_DIM) ** -0.5
    outs = []
    for q0 in range(0, S, Q_BLOCK):
        kend = q0 + Q_BLOCK
        s = (jnp.einsum('bqhd,bkhd->bhqk', q_nope[:, q0:kend], k_nope[:, :kend])
             + jnp.einsum('bqhr,bkr->bhqk', q_rope[:, q0:kend], k_rope[:, :kend])).astype(jnp.float32) * scale
        s = jnp.where(_causal_mask(q0, kend), s, -jnp.inf)
        a = jax.nn.softmax(s, axis=-1)
        outs.append(jnp.einsum('bhqk,bkhd->bqhd', a.astype(v.dtype), v[:, :kend]))
    return jnp.concatenate(outs, axis=1).reshape(B, S, MLA_HEADS * MLA_V_DIM)

def _mixer(h, pos, rel_table, w_in, b_gate, lq1, lk1, lq2, lk2, lam_init, diff_subln_g,
           mla_q_norm_g, w_uq, mla_kv_norm_g, w_ukv, w_branch_diff, w_branch_mla, w_out):
    B, S, _ = h.shape
    z = h @ w_in
    dq, dk, dv, cq, ckv, kr, gl = jnp.split(z, IN_SPLIT_IDX, axis=-1)
    lam = (jnp.exp(jnp.sum(lq1.astype(jnp.float32) * lk1.astype(jnp.float32)))
           - jnp.exp(jnp.sum(lq2.astype(jnp.float32) * lk2.astype(jnp.float32))) + lam_init)
    o_a = _diff_attention(dq.reshape(B, S, DIFF_HEADS, 2, DIFF_HEAD_DIM),
                          dk.reshape(B, S, DIFF_HEADS, 2, DIFF_HEAD_DIM),
                          dv.reshape(B, S, DIFF_HEADS, DIFF_V_DIM),
                          pos, rel_table, lam, lam_init, diff_subln_g)
    o_b = _mla(cq, ckv, kr, pos, mla_q_norm_g, w_uq, mla_kv_norm_g, w_ukv)
    g = jax.nn.sigmoid(gl + b_gate)
    g_a, g_b = g[..., :D_MODEL], g[..., D_MODEL:]
    m = g_a * (o_a @ w_branch_diff) + g_b * (o_b @ w_branch_mla)
    return m @ w_out

def _swiglu(x, w1, w3, w2):
    return (jax.nn.silu(x @ w1) * (x @ w3)) @ w2

def _moe(x, w_router, w1, w3, w2):
    B, S, D = x.shape
    xt = x.reshape(-1, D)
    T = xt.shape[0]
    M = T * TOP_K
    logits = (xt @ w_router).astype(jnp.float32)
    top_v, top_e = lax.top_k(logits, TOP_K)
    gates = jax.nn.softmax(top_v, axis=-1)
    flat_e = top_e.reshape(-1)
    flat_tok = jnp.repeat(jnp.arange(T, dtype=jnp.int32), TOP_K)
    order = jnp.argsort(flat_e, stable=True)
    se, stok, sg = flat_e[order], flat_tok[order], gates.reshape(-1)[order]
    counts = jnp.bincount(flat_e, length=N_EXPERTS)
    padded = ((counts + EXPERT_BLOCK - 1) // EXPERT_BLOCK) * EXPERT_BLOCK
    start = jnp.cumsum(counts) - counts
    pstart = jnp.cumsum(padded) - padded
    dest = pstart[se] + jnp.arange(M, dtype=jnp.int32) - start[se]
    n_blocks = -(-M // EXPERT_BLOCK) + N_EXPERTS
    P = n_blocks * EXPERT_BLOCK
    buf = jnp.zeros((P, D), x.dtype).at[dest].set(xt[stok])
    block_e = jnp.minimum(jnp.searchsorted(jnp.cumsum(padded), jnp.arange(n_blocks) * EXPERT_BLOCK,
                                           side='right'), N_EXPERTS - 1)

    def run(args):
        xb, e = args
        return _swiglu(xb, w1[e], w3[e], w2[e])

    yb = lax.map(run, (buf.reshape(n_blocks, EXPERT_BLOCK, D), block_e)).reshape(P, D)
    y = jnp.zeros((T, D), x.dtype).at[stok].add(yb[dest] * sg[:, None].astype(x.dtype))
    return y.reshape(B, S, D)

def first_inputs(seed: int = 0) -> dict:
    key = jax.random.key(seed)
    ks = jax.random.split(key, 32)
    f32 = jnp.float32

    def nrm(k, shape, scale):
        return jax.random.normal(k, shape, f32) * scale

    beta = DEEPNORM_BETA
    return {
        "x": nrm(ks[0], (BATCH, SEQ, D_MODEL), 1.0),
        "p": nrm(ks[1], (DEPTH, BATCH, SEQ, PLE_DIM), 1.0),
        "positions": jnp.broadcast_to(jnp.arange(SEQ, dtype=jnp.int32), (BATCH, SEQ)),
        "rel_bias_table": nrm(ks[2], (REL_BUCKETS, DIFF_HEADS), 0.5),
        "w_in": nrm(ks[3], (DEPTH, D_MODEL, IN_COLS), D_MODEL ** -0.5),
        "b_gate": nrm(ks[4], (DEPTH, GATE_COLS), 0.02),
        "lambda_q1": nrm(ks[5], (DEPTH, DIFF_HEAD_DIM), 0.1),
        "lambda_k1": nrm(ks[6], (DEPTH, DIFF_HEAD_DIM), 0.1),
        "lambda_q2": nrm(ks[7], (DEPTH, DIFF_HEAD_DIM), 0.1),
        "lambda_k2": nrm(ks[8], (DEPTH, DIFF_HEAD_DIM), 0.1),
        "diff_subln_g": 1.0 + nrm(ks[9], (DEPTH, DIFF_V_DIM), 0.02),
        "mla_q_norm_g": 1.0 + nrm(ks[10], (DEPTH, MLA_Q_RANK), 0.02),
        "w_uq": nrm(ks[11], (DEPTH, MLA_Q_RANK, MLA_HEADS * (MLA_NOPE_DIM + MLA_ROPE_DIM)), MLA_Q_RANK ** -0.5),
        "mla_kv_norm_g": 1.0 + nrm(ks[12], (DEPTH, MLA_KV_RANK), 0.02),
        "w_ukv": nrm(ks[13], (DEPTH, MLA_KV_RANK, MLA_HEADS * (MLA_NOPE_DIM + MLA_V_DIM)), MLA_KV_RANK ** -0.5),
        "w_branch_diff": nrm(ks[14], (DEPTH, DIFF_HEADS * DIFF_V_DIM, D_MODEL), (DIFF_HEADS * DIFF_V_DIM) ** -0.5),
        "w_branch_mla": nrm(ks[15], (DEPTH, MLA_HEADS * MLA_V_DIM, D_MODEL), (MLA_HEADS * MLA_V_DIM) ** -0.5),
        "w_out": nrm(ks[16], (DEPTH, D_MODEL, D_MODEL), beta * D_MODEL ** -0.5),
        "ln_mix_g": 1.0 + nrm(ks[17], (DEPTH, D_MODEL), 0.02),
        "ln_mix_b": nrm(ks[18], (DEPTH, D_MODEL), 0.02),
        "dense_w1": nrm(ks[19], (N_DENSE, D_MODEL, DENSE_FF), D_MODEL ** -0.5),
        "dense_w3": nrm(ks[20], (N_DENSE, D_MODEL, DENSE_FF), D_MODEL ** -0.5),
        "dense_w2": nrm(ks[21], (N_DENSE, DENSE_FF, D_MODEL), beta * DENSE_FF ** -0.5),
        "router_w": nrm(ks[22], (N_MOE, D_MODEL, N_EXPERTS), D_MODEL ** -0.5),
        "expert_w1": nrm(ks[23], (N_MOE, N_EXPERTS, D_MODEL, EXPERT_FF), D_MODEL ** -0.5),
        "expert_w3": nrm(ks[24], (N_MOE, N_EXPERTS, D_MODEL, EXPERT_FF), D_MODEL ** -0.5),
        "expert_w2": nrm(ks[25], (N_MOE, N_EXPERTS, EXPERT_FF, D_MODEL), beta * EXPERT_FF ** -0.5),
        "w_ple_gate": nrm(ks[26], (DEPTH, D_MODEL, D_MODEL), D_MODEL ** -0.5),
        "w_ple_proj": nrm(ks[27], (DEPTH, PLE_DIM, D_MODEL), beta * PLE_DIM ** -0.5),
        "ln_ffn_g": 1.0 + nrm(ks[28], (DEPTH, D_MODEL), 0.02),
        "ln_ffn_b": nrm(ks[29], (DEPTH, D_MODEL), 0.02),
    }

def first_block(x, p, positions, rel_bias_table, w_in, b_gate, lambda_q1, lambda_k1, lambda_q2, lambda_k2,
              diff_subln_g, mla_q_norm_g, w_uq, mla_kv_norm_g, w_ukv, w_branch_diff, w_branch_mla, w_out,
              ln_mix_g, ln_mix_b, dense_w1, dense_w3, dense_w2, router_w, expert_w1, expert_w3, expert_w2,
              w_ple_gate, w_ple_proj, ln_ffn_g, ln_ffn_b):
    for i in range(DEPTH):
        lam_init = 0.8 - 0.6 * math.exp(-0.3 * i)
        y = _mixer(x, positions, rel_bias_table, w_in[i], b_gate[i], lambda_q1[i], lambda_k1[i],
                   lambda_q2[i], lambda_k2[i], lam_init, diff_subln_g[i], mla_q_norm_g[i], w_uq[i],
                   mla_kv_norm_g[i], w_ukv[i], w_branch_diff[i], w_branch_mla[i], w_out[i])
        x = _layernorm(DEEPNORM_ALPHA * x + y, ln_mix_g[i], ln_mix_b[i])
        j = i // 2
        if i % 2 == 0:
            f = _swiglu(x, dense_w1[j], dense_w3[j], dense_w2[j])
        else:
            f = _moe(x, router_w[j], expert_w1[j], expert_w3[j], expert_w2[j])
        e = jax.nn.sigmoid(x @ w_ple_gate[i]) * (p[i] @ w_ple_proj[i])
        x = _layernorm(DEEPNORM_ALPHA * x + f + e, ln_ffn_g[i], ln_ffn_b[i])
    return x


D_FF = 2816
A_CHUNK = 128
A_GROUPS = 4
A_GROUP_DIM = 128
A_WIDTH = A_GROUPS * A_GROUP_DIM
B_WINDOW = 128
B_Q_HEADS = 8
B_KV_HEADS = 2
B_HEAD_DIM = 64
B_Q_PER_KV = B_Q_HEADS // B_KV_HEADS
B_WIDTH = B_Q_HEADS * B_HEAD_DIM
B_KV_WIDTH = B_KV_HEADS * B_HEAD_DIM
C_CHUNK = 128
C_HEADS = 4
C_QK_DIM = 128
C_V_DIM = 256
C_QK_WIDTH = C_HEADS * C_QK_DIM
C_V_WIDTH = C_HEADS * C_V_DIM
SPLIT_SIZES = (A_WIDTH, A_WIDTH,
               B_WIDTH, B_KV_WIDTH, B_KV_WIDTH,
               C_QK_WIDTH, C_QK_WIDTH, C_V_WIDTH, C_V_WIDTH,
               3 * D_MODEL)
IN_WIDTH = sum(SPLIT_SIZES)
NORM_EPS = 1e-6
GN_EPS = 1e-5


def rmsnorm(x, g):
    xf = x.astype(jnp.float32)
    y = xf * lax.rsqrt(jnp.mean(xf * xf, axis=-1, keepdims=True) + NORM_EPS)
    return (y * g.astype(jnp.float32)).astype(x.dtype)

def swiglu(h, w_in, w_out):
    a, b = jnp.split(h @ w_in, 2, axis=-1)
    return (jax.nn.silu(a) * b) @ w_out

def gmlp_spatial(z, v_norm, w_s, b_s):
    bsz, t_len, _ = z.shape
    u, v = jnp.split(z, 2, axis=-1)
    v = rmsnorm(v, v_norm)
    vc = v.reshape(bsz, t_len // A_CHUNK, A_CHUNK, A_GROUPS, A_GROUP_DIM)
    causal = jnp.tril(jnp.ones((A_CHUNK, A_CHUNK), dtype=bool))
    w = jnp.where(causal[None], w_s, jnp.zeros_like(w_s))
    s = jnp.einsum('gts,bcsgd->bctgd', w, vc) + b_s.T[None, None, :, :, None]
    return u * s.reshape(bsz, t_len, A_WIDTH)

def swa_attention(q, k, v, sinks):
    bsz, t_len, _ = q.shape
    n = t_len // B_WINDOW
    W = B_WINDOW
    qb = q.reshape(bsz, n, W, B_KV_HEADS, B_Q_PER_KV, B_HEAD_DIM)
    kb = k.reshape(bsz, n, W, B_KV_HEADS, B_HEAD_DIM)
    vb = v.reshape(bsz, n, W, B_KV_HEADS, B_HEAD_DIM)
    pad = ((0, 0), (1, 0), (0, 0), (0, 0), (0, 0))
    kk = jnp.concatenate([jnp.pad(kb, pad)[:, :-1], kb], axis=2)
    vv = jnp.concatenate([jnp.pad(vb, pad)[:, :-1], vb], axis=2)
    scores = jnp.einsum('bnqhgd,bnkhd->bnhgqk', qb, kk).astype(jnp.float32)
    scores = scores * (1.0 / math.sqrt(B_HEAD_DIM))
    qpos = jnp.arange(W)[:, None] + W
    kpos = jnp.arange(2 * W)[None, :]
    dist = (qpos - kpos).astype(jnp.float32)
    valid = (dist >= 0) & (dist < W)
    block_valid = valid[None] & ((jnp.arange(n) > 0)[:, None, None] | (kpos >= W)[None])
    slopes = jnp.exp2(-8.0 / B_Q_HEADS * (jnp.arange(B_Q_HEADS, dtype=jnp.float32) + 1.0))
    alibi = -slopes.reshape(B_KV_HEADS, B_Q_PER_KV)[:, :, None, None] * dist
    scores = jnp.where(block_valid[None, :, None, None], scores + alibi[None, None], -jnp.inf)
    sink = sinks.astype(jnp.float32).reshape(B_KV_HEADS, B_Q_PER_KV)[None, None, :, :, None, None]
    m = jnp.maximum(jnp.max(scores, axis=-1, keepdims=True), sink)
    p = jnp.exp(scores - m)
    probs = p / (jnp.sum(p, axis=-1, keepdims=True) + jnp.exp(sink - m))
    out = jnp.einsum('bnhgqk,bnkhd->bnqhgd', probs.astype(v.dtype), vv)
    return out.reshape(bsz, t_len, B_WIDTH)

def retention(q, k, v, g, gn_gain):
    bsz, t_len, _ = q.shape
    n = t_len // C_CHUNK
    dt = q.dtype
    log_gamma = jnp.log(1.0 - jnp.exp2(-5.0 - jnp.arange(C_HEADS, dtype=jnp.float32)))
    qc = q.reshape(bsz, n, C_CHUNK, C_HEADS, C_QK_DIM)
    kc = k.reshape(bsz, n, C_CHUNK, C_HEADS, C_QK_DIM) * (C_QK_DIM ** -0.5)
    vc = v.reshape(bsz, n, C_CHUNK, C_HEADS, C_V_DIM)
    idx = jnp.arange(C_CHUNK, dtype=jnp.float32)
    dist = idx[:, None] - idx[None, :]
    decay = jnp.where(dist[None] >= 0, jnp.exp(log_gamma[:, None, None] * jnp.maximum(dist, 0.0)[None]), 0.0)
    scores = jnp.einsum('bnthd,bnshd->bnhts', qc, kc) * decay.astype(dt)[None, None]
    inner = jnp.einsum('bnhts,bnshe->bnthe', scores, vc)
    k_w = jnp.exp(log_gamma[None, :] * (C_CHUNK - 1.0 - idx)[:, None]).astype(dt)
    kv = jnp.einsum('bnshd,bnshe->nbhde', kc * k_w[None, None, :, :, None], vc)
    chunk_decay = jnp.exp(log_gamma * C_CHUNK).astype(dt)[None, :, None, None]

    def step(state, kv_i):
        return chunk_decay * state + kv_i, state

    init = jnp.zeros((bsz, C_HEADS, C_QK_DIM, C_V_DIM), dtype=kv.dtype)
    _, s_prev = lax.scan(step, init, kv)
    q_w = jnp.exp(log_gamma[None, :] * (idx + 1.0)[:, None]).astype(dt)
    cross = jnp.einsum('bnthd,nbhde->bnthe', qc * q_w[None, None, :, :, None], s_prev)
    o = (inner + cross).astype(jnp.float32)
    mu = jnp.mean(o, axis=-1, keepdims=True)
    var = jnp.mean(jnp.square(o - mu), axis=-1, keepdims=True)
    o = ((o - mu) * lax.rsqrt(var + GN_EPS)).reshape(bsz, t_len, C_V_WIDTH)
    o = (o * gn_gain.astype(jnp.float32)).astype(dt)
    return o * jax.nn.silu(g)

def hybrid_layer(x, ffn1_norm, ffn1_w_in, ffn1_w_out, mix_norm, w_in, b_gate,
                 gmlp_v_norm, gmlp_w_s, gmlp_b_s, attn_sinks, ret_gn,
                 w_branch_a, w_branch_b, w_branch_c, w_out,
                 ffn2_norm, ffn2_w_in, ffn2_w_out):
    x = x + 0.5 * swiglu(rmsnorm(x, ffn1_norm), ffn1_w_in, ffn1_w_out)
    h = rmsnorm(x, mix_norm)
    p = h @ w_in
    cuts = list(np.cumsum(SPLIT_SIZES)[:-1])
    a_u, a_v, b_q, b_k, b_v, c_q, c_k, c_v, c_g, gate_pre = jnp.split(p, cuts, axis=-1)
    y_a = gmlp_spatial(jax.nn.gelu(jnp.concatenate([a_u, a_v], axis=-1)),
                       gmlp_v_norm, gmlp_w_s, gmlp_b_s) @ w_branch_a
    y_b = swa_attention(b_q, b_k, b_v, attn_sinks) @ w_branch_b
    y_c = retention(c_q, c_k, c_v, c_g, ret_gn) @ w_branch_c
    g_a, g_b, g_c = jnp.split(jax.nn.sigmoid(gate_pre + b_gate), 3, axis=-1)
    merged = g_a * y_a + g_b * y_b + g_c * y_c
    x = x + merged @ w_out
    x = x + 0.5 * swiglu(rmsnorm(x, ffn2_norm), ffn2_w_in, ffn2_w_out)
    return x

def second_inputs(seed: int = 0) -> dict:
    key = jax.random.key(seed)
    ks = jax.random.split(key, 24)
    L, D, F = DEPTH, D_MODEL, D_FF
    f32 = jnp.float32

    def nrm(k, shape, fan_in):
        return jax.random.normal(k, shape, f32) * (fan_in ** -0.5)

    def gain(k, shape):
        return 1.0 + 0.02 * jax.random.normal(k, shape, f32)

    return {
        "x": jax.random.normal(ks[0], (BATCH, SEQ, D), f32),
        "ffn1_norm": gain(ks[1], (L, D)),
        "ffn1_w_in": nrm(ks[2], (L, D, 2 * F), D),
        "ffn1_w_out": nrm(ks[3], (L, F, D), F),
        "mix_norm": gain(ks[4], (L, D)),
        "w_in": nrm(ks[5], (L, D, IN_WIDTH), D),
        "b_gate": 0.02 * jax.random.normal(ks[6], (L, 3 * D), f32),
        "gmlp_v_norm": gain(ks[7], (L, A_WIDTH)),
        "gmlp_w_s": nrm(ks[8], (L, A_GROUPS, A_CHUNK, A_CHUNK), A_CHUNK),
        "gmlp_b_s": 1.0 + 0.02 * jax.random.normal(ks[9], (L, A_GROUPS, A_CHUNK), f32),
        "attn_sinks": 0.5 * jax.random.normal(ks[10], (L, B_Q_HEADS), f32),
        "ret_gn": gain(ks[11], (L, C_V_WIDTH)),
        "w_branch_a": nrm(ks[12], (L, A_WIDTH, D), A_WIDTH),
        "w_branch_b": nrm(ks[13], (L, B_WIDTH, D), B_WIDTH),
        "w_branch_c": nrm(ks[14], (L, C_V_WIDTH, D), C_V_WIDTH),
        "w_out": nrm(ks[15], (L, D, D), D),
        "ffn2_norm": gain(ks[16], (L, D)),
        "ffn2_w_in": nrm(ks[17], (L, D, 2 * F), D),
        "ffn2_w_out": nrm(ks[18], (L, F, D), F),
        "final_norm": gain(ks[19], (D,)),
    }

def second_block(x, ffn1_norm, ffn1_w_in, ffn1_w_out, mix_norm, w_in, b_gate,
              gmlp_v_norm, gmlp_w_s, gmlp_b_s, attn_sinks, ret_gn,
              w_branch_a, w_branch_b, w_branch_c, w_out,
              ffn2_norm, ffn2_w_in, ffn2_w_out, final_norm):
    for l in range(DEPTH):
        x = hybrid_layer(x, ffn1_norm[l], ffn1_w_in[l], ffn1_w_out[l], mix_norm[l],
                         w_in[l], b_gate[l], gmlp_v_norm[l], gmlp_w_s[l], gmlp_b_s[l],
                         attn_sinks[l], ret_gn[l], w_branch_a[l], w_branch_b[l],
                         w_branch_c[l], w_out[l], ffn2_norm[l], ffn2_w_in[l], ffn2_w_out[l])
    return rmsnorm(x, final_norm)


_first_inputs = second_inputs


def second_inputs(seed=0):
    import zlib

    import numpy as np

    out = dict(_first_inputs(seed))
    spreads = {}
    factors = {'ffn1_norm': 3.946,
     'b_gate': 8.0,
     'gmlp_v_norm': 8.0,
     'gmlp_b_s': 6.391,
     'attn_sinks': 3.105,
     'ret_gn': 7.107,
     'ffn2_norm': 5.617,
     'final_norm': 2.845}
    for name, (base, spread) in spreads.items():
        noise = np.random.default_rng([zlib.crc32(name.encode()), seed]).standard_normal(out[name].shape)
        drawn = base * np.exp(spread * noise) if base else spread * noise
        out[name] = __import__('jax').numpy.asarray(drawn.astype(out[name].dtype))
    for name, factor in factors.items():
        out[name] = (out[name] * factor).astype(out[name].dtype)
    return out


_narrow_inputs = second_inputs


def second_inputs(seed=0):

    out = dict(_narrow_inputs(seed))
    wider = {'gmlp_v_norm': 5.91,
     'gmlp_b_s': 5.13,
     'attn_sinks': 4.95,
     'ret_gn': 5.2,
     'final_norm': 3.19}
    for name, times in wider.items():
        mean = out[name].mean()
        out[name] = (mean + times * (out[name] - mean)).astype(out[name].dtype)
    return out


def setup_inputs(seed=0):
    out = dict(first_inputs(seed))
    for name, value in second_inputs(seed + 1).items():
        if name != "x":
            out[name + "_2"] = value
    return out


def reference(
    x, p, positions, rel_bias_table, w_in, b_gate, lambda_q1, lambda_k1, lambda_q2, lambda_k2,
    diff_subln_g, mla_q_norm_g, w_uq, mla_kv_norm_g, w_ukv, w_branch_diff, w_branch_mla, w_out,
    ln_mix_g, ln_mix_b, dense_w1, dense_w3, dense_w2, router_w, expert_w1, expert_w3, expert_w2,
    w_ple_gate, w_ple_proj, ln_ffn_g, ln_ffn_b, ffn1_norm_2, ffn1_w_in_2, ffn1_w_out_2,
    mix_norm_2, w_in_2, b_gate_2, gmlp_v_norm_2, gmlp_w_s_2, gmlp_b_s_2, attn_sinks_2, ret_gn_2,
    w_branch_a_2, w_branch_b_2, w_branch_c_2, w_out_2, ffn2_norm_2, ffn2_w_in_2, ffn2_w_out_2,
    final_norm_2,
):
    x = first_block(
        x, p, positions, rel_bias_table, w_in, b_gate, lambda_q1, lambda_k1, lambda_q2,
        lambda_k2, diff_subln_g, mla_q_norm_g, w_uq, mla_kv_norm_g, w_ukv, w_branch_diff,
        w_branch_mla, w_out, ln_mix_g, ln_mix_b, dense_w1, dense_w3, dense_w2, router_w,
        expert_w1, expert_w3, expert_w2, w_ple_gate, w_ple_proj, ln_ffn_g, ln_ffn_b,
    )
    return second_block(
        x, ffn1_norm_2, ffn1_w_in_2, ffn1_w_out_2, mix_norm_2, w_in_2, b_gate_2, gmlp_v_norm_2,
        gmlp_w_s_2, gmlp_b_s_2, attn_sinks_2, ret_gn_2, w_branch_a_2, w_branch_b_2,
        w_branch_c_2, w_out_2, ffn2_norm_2, ffn2_w_in_2, ffn2_w_out_2, final_norm_2,
    )


_drawn_inputs = setup_inputs


def setup_inputs(seed=0):
    import zlib

    import numpy as np

    out = dict(_drawn_inputs(seed))
    spreads = {}
    factors = {'mla_kv_norm_g': 3.198, 'attn_sinks_2': 3.117, 'b_gate': 4.577}
    for name, (base, spread) in spreads.items():
        noise = np.random.default_rng([zlib.crc32(name.encode()), seed]).standard_normal(out[name].shape)
        drawn = base * np.exp(spread * noise) if base else spread * noise
        out[name] = __import__('jax').numpy.asarray(drawn.astype(out[name].dtype))
    for name, factor in factors.items():
        out[name] = (out[name] * factor).astype(out[name].dtype)
    return out
```

```python
import math
from contextlib import ExitStack

import numpy as np

import concourse.bass as bass
from concourse import mybir

F32 = mybir.dt.float32
I32 = mybir.dt.int32
U32 = mybir.dt.uint32
ALU = mybir.AluOpType
ACT = mybir.ActivationFunctionType
AX = mybir.AxisListType.X

P = 128
SEQ = 256
HALVES = SEQ // P
D = 1024
KT = D // P
LAYERS = 2
ALPHA = (2.0 * LAYERS) ** 0.25
LN_EPS, RMS_EPS = 1e-5, 1e-6

HEADS = 8
DENSE_FF, EXPERT_FF, EXPERTS = 2816, 3584, 8
Q_RANK, KV_RANK, ROPE, NOPE, MLA_V = 384, 256, 32, 64, 64
HALF_ROPE = ROPE // 2
MLA_QK = NOPE + ROPE
LATENT = Q_RANK + KV_RANK + ROPE
BUCKETS, MAX_DIST = 32, 128
LAM_INIT = [0.8 - 0.6 * math.exp(-0.3 * i) for i in range(LAYERS)]
MAGIC = 1.5 * 2.0 ** 23
TWO_PI = (6.28125, 0.0019350051879882812, 3.019916050561733e-07)
PI_DOWN = 3.1415925

D_FF = 2816
A_GROUPS = 4
C_HEADS, C_V = 4, 256
SWA_DIM = 64

FF_STEP = 256
UNIT = 3 * KT * FF_STEP
UP = 2 * KT * FF_STEP
GEMM = KT * 512
SLOTS = 4
DENSE_STEPS = DENSE_FF // FF_STEP
EXPERT_STEPS = EXPERT_FF // FF_STEP
FFN_STEPS = D_FF // FF_STEP
MIX1, PLE, MIX2 = 19, 3, 22
DENSE_START = MIX1 + PLE
MOE_START = DENSE_START + DENSE_STEPS + MIX1 + PLE
BLOCK2 = MOE_START + EXPERTS * EXPERT_STEPS
LAYER2 = 2 * FFN_STEPS + MIX2
FFN2_START = BLOCK2 + FFN_STEPS + MIX2
assert LAYER2 % SLOTS == 0 and 2 * EXPERT_STEPS % SLOTS == 0

MAP = P + 2 * P
NEG = -1e30
COLS1 = dict(b_gate=0, subln=16, q_norm=17, kv_norm=20)
COLS2 = dict(ffn1=0, mix=8, b_gate=16, v_norm=40, ret=44, ffn2=52)
N_COLS1, N_COLS2 = 22, 60
START_LOADS = 9


def t5_thresholds():
    n = np.arange(0, 4 * MAX_DIST)
    exact = BUCKETS // 2
    ratio = np.maximum(n, 1).astype(np.float32) / np.float32(exact)
    large = exact + (np.log(ratio) / np.float32(math.log(MAX_DIST / exact)) * np.float32(BUCKETS - exact)).astype(np.int32)
    bucket = np.where(n < exact, n, np.minimum(large, BUCKETS - 1))
    return [int(np.argmax(bucket >= b)) for b in range(1, BUCKETS)]


def order(*names):
    return {name: i for i, name in enumerate(names)}


def attention_order(maps, name):
    out = []
    for i in range(maps + 2):
        if i < maps:
            out.append(f"{name}_scores{i}")
        if 0 <= i - 1 < maps:
            out.append(f"{name}_turn{i - 1}")
        if 0 <= i - 2 < maps:
            out.append(f"{name}_values{i - 2}")
    return out


JOBS1 = order(
    "latent0", "latent1", "dq0", "dq1", "dk0", "dk1", "dv0", "dv1",
    "cq_turn", "ckv_turn", "uq0", "uq1", "ukv0", "ukv1", "q_turn0", "q_turn1", "k_turn0", "k_turn1",
    *attention_order(HEADS, "diff"), *attention_order(HEADS // 2, "mla"),
    "gate_a0", "gate_a1", "o_turn0", "o_turn1", "branch_a0", "branch_a1",
    "gate_b0", "gate_b1", "branch_b0", "branch_b1", "mix0", "mix1",
    "x_turn0", "x_turn1", "ple_gate0", "ple_gate1", "ple_proj0", "ple_proj1",
    "end_turn0", "end_turn1")
JOBS2 = order(
    "ffn1_turn0", "ffn1_turn1", "mix_turn0", "mix_turn1",
    "a_v", "a_u", "b_q", "b_kv", "c_q", "c_k", "c_krow", "a_mix",
    "c_v0", "c_v1", *attention_order(HEADS // 2, "swa"),
    "c_g0", "c_g1", "c_scores", "c_state", "c_out0", "c_out1",
    "gate_a0", "gate_a1", "branch_a0", "branch_a1",
    "gate_b0", "gate_b1", "branch_b0", "branch_b1",
    "gate_c0", "gate_c1", "c_turn0", "c_turn1", "branch_c0", "branch_c1",
    "mix0", "mix1", "ffn2_turn0", "ffn2_turn1")

FREED1 = dict(
    latent0=("latent", 1), latent1=("latent", 2), dq0=("dq", 1), dq1=("dq", 2), dk0=("dk", 1), dk1=("dk", 2),
    dv0=("dv", 1), dv1=("dv", 2), cq_turn=("cqT", 3), ckv_turn=("ckvT", 2), uq0=("q_rows", 1), uq1=("q_rows", 2),
    ukv0=("kv_rows", 2), ukv1=("kv_rows", 4), q_turn0=("qT", 1), q_turn1=("qT", 2), k_turn0=("kT", 1), k_turn1=("kT", 2),
    **{f"diff_scores{h}": ("biased", 2 * h + 2) for h in range(HEADS)},
    **{f"diff_turn{h}": ("turned", h + 1) for h in range(HEADS)},
    **{f"diff_values{h}": ("values", h + 1) for h in range(HEADS)},
    **{f"mla_scores{i}": ("biased", 2 * (HEADS + i) + 2) for i in range(HEADS // 2)},
    **{f"mla_turn{i}": ("turned", HEADS + i + 1) for i in range(HEADS // 2)},
    **{f"mla_values{i}": ("values", HEADS + i + 1) for i in range(HEADS // 2)},
    gate_a0=("gate", 4), gate_a1=("gate", 8), o_turn0=("oT", 1), o_turn1=("oT", 2),
    branch_a0=("mT", 1), branch_a1=("mT", 2), gate_b0=("gate", 12), gate_b1=("gate", 16),
    branch_b0=("m_tmp", 1), branch_b1=("m_tmp", 2), mix0=("mix", 1), mix1=("mix", 2),
    x_turn0=("turned_x", 1), x_turn1=("turned_x", 2), ple_gate0=("ple_sig", 1), ple_gate1=("ple_sig", 2),
    ple_proj0=("ple_e", 1), ple_proj1=("ple_e", 2), end_turn0=("turned_x", 3), end_turn1=("turned_x", 4))
FREED2 = dict(
    ffn1_turn0=("turned_act", 4), ffn1_turn1=("turned_dve", 4), mix_turn0=("turned_act", 8), mix_turn1=("turned_dve", 8),
    a_v=("av", 1), a_u=("uT", 1), b_q=("bq", 1), b_kv=("bkv", 2), c_q=("cq", 1), c_k=("ck", 1), c_krow=("ckw", 1),
    a_mix=("ya_tmp", 4), c_v0=("cv", 1), c_v1=("cv", 2),
    **{f"swa_scores{i}": ("biased", 2 * i + 2) for i in range(HEADS // 2)},
    **{f"swa_turn{i}": ("turned", i + 1) for i in range(HEADS // 2)},
    **{f"swa_values{i}": ("values", i + 1) for i in range(HEADS // 2)},
    c_g0=("cg", 1), c_g1=("cg", 2), c_scores=("scT", 4), c_state=("state", 1), c_out0=("o_n", 4), c_out1=("o_n", 8),
    gate_a0=("gate", 4), gate_a1=("gate", 8), branch_a0=("mT", 1), branch_a1=("mT", 2),
    gate_b0=("gate", 12), gate_b1=("gate", 16), branch_b0=("m_tmp", 1), branch_b1=("m_tmp", 2),
    gate_c0=("gate", 20), gate_c1=("gate", 24), c_turn0=("ycT", 4), c_turn1=("ycT", 8),
    branch_c0=("m_tmp", 3), branch_c1=("m_tmp", 4), mix0=("mix", 1), mix1=("mix", 2),
    ffn2_turn0=("turned_act", 12), ffn2_turn1=("turned_dve", 12))


class Signal:

    def __init__(self, sem, per):
        self.sem, self.per = sem, per

    def by(self, layer, n=None):
        return self.sem, layer * self.per + (self.per if n is None else n)


class Signals:

    def __init__(self, new, prefix, **per):
        self.named = {name: Signal(new(prefix + name), n) for name, n in per.items()}

    def __getitem__(self, name):
        return self.named[name]


def build(nc, a, out):
    with ExitStack() as ctx:
        def sb(name, words, dtype=F32):
            return ctx.enter_context(nc.sbuf_tensor(name, [P, words], dtype))

        ring = sb("weight_ring", SLOTS * UNIT)
        arena = sb("arena", 99 * 256)
        x_rows = sb("x_rows", HALVES * D)
        ident = sb("identity", P)
        cols1 = sb("columns_first", LAYERS * N_COLS1)
        cols2 = sb("columns_second", LAYERS * N_COLS2)
        stat = sb("statistics", 256)
        consts = sb("constants", 3 * 2 * HEADS)
        att = sb("softmax_statistics", 12 * 20)
        routing = sb("routing", HALVES * EXPERTS * 4)
        top_idx = sb("top_experts", HALVES * 8, U32)
        psum = ctx.enter_context(nc.psum_tensor("psum", [P, 8, 512], F32))

        def view(kb, words, pattern=None, **sizes):
            v = arena[:, int(kb * 256):int(kb * 256) + words]
            return v.rearrange(pattern, **sizes) if pattern else v

        X = x_rows[:].rearrange("p (h d) -> p h d", h=HALVES)

        xT = view(0, KT * SEQ, "p (k t) -> p k t", k=KT)
        xn = view(8, HALVES * D, "p (h d) -> p h d", h=HALVES)
        T = view(16, 2 * 2 * MAP, "p (b m k) -> p b m k", b=2, m=2)
        PT = view(22, 2 * 2 * MAP, "p (b m k) -> p b m k", b=2, m=2)
        hT = view(16, 4 * SEQ, "p (n t) -> p n t", n=4)
        sil = view(20, 2 * SEQ, "p (n t) -> p n t", n=2)
        latent = view(16, HALVES * LATENT, "p (h c) -> p h c", h=HALVES)
        qrow = view(22, HALVES * HEADS * MLA_QK, "p (h n c) -> p h n c", h=HALVES, n=HEADS)
        kcat = view(8, HALVES * HEADS * MLA_QK, "p (h n c) -> p h n c", h=HALVES, n=HEADS)
        squares = view(16, HALVES * D, "p (h d) -> p h d", h=HALVES)
        bias = view(28, HEADS * MAP, "p (h k) -> p h k", h=HEADS)
        dqT = view(40, HEADS * SEQ, "p (h t) -> p h t", h=HEADS)
        dkT = view(48, HEADS * SEQ, "p (h t) -> p h t", h=HEADS)
        dv = view(56, HALVES * D, "p (h c) -> p h c", h=HALVES)
        qT = view(64, HEADS * SEQ, "p (h t) -> p h t", h=HEADS)
        kT = view(72, HEADS * SEQ, "p (h t) -> p h t", h=HEADS)
        cqT = view(80, 3 * SEQ, "p (k t) -> p k t", k=3)
        ckvT = view(83, 2 * SEQ, "p (k t) -> p k t", k=2)
        obT = view(80, 4 * SEQ, "p (k t) -> p k t", k=4)
        vrow = view(85, HALVES * HEADS * MLA_V, "p (h n c) -> p h n c", h=HALVES, n=HEADS)
        norm_rows = view(89, 2 * D, "p (n d) -> p n d", n=2)
        rope_tmp = view(74, 4 * HEADS * HALF_ROPE, "p (n h c) -> p n h c", n=4, h=HEADS)
        neg_dist = view(89, MAP)
        at_least = view(90.5, MAP)
        delta = view(94, BUCKETS * HEADS)
        table_rows = view(95, BUCKETS * HEADS)
        thresholds = view(96, BUCKETS)
        causal = view(97, MAP)
        trig = view(98.5, HALVES * 2 * HALF_ROPE, "p (n h c) -> p n h c", n=2, h=HALVES)
        lambdas = view(64, LAYERS * 4 * 64, "p (n q c) -> p n q c", n=2 * LAYERS, q=2)
        positions = view(66, SEQ + HALVES).bitcast(I32)
        pos = view(68, SEQ + HALVES)
        inv_freq = view(70, HALF_ROPE)
        angle = view(71, 6 * HALVES * HALF_ROPE, "p (n h c) -> p n h c", n=6, h=HALVES)
        oT = view(40, KT * SEQ, "p (k t) -> p k t", k=KT)
        gate1 = view(64, 2 * KT * SEQ, "p (n k t) -> p n k t", n=2, k=KT)
        m1T = view(48, KT * SEQ, "p (k t) -> p k t", k=KT)
        R = view(40, HALVES * D, "p (h d) -> p h d", h=HALVES)
        E = view(64, HALVES * D, "p (h d) -> p h d", h=HALVES)
        pT = view(56, 2 * SEQ, "p (k t) -> p k t", k=2)
        router = view(60, KT * EXPERTS + EXPERTS)
        v2 = view(28, HALVES * 512, "p (h c) -> p h c", h=HALVES)
        uT = view(32, 4 * SEQ, "p (k t) -> p k t", k=4)
        m2T = view(28, KT * SEQ, "p (k t) -> p k t", k=KT)
        yaT = view(36, 4 * SEQ, "p (k t) -> p k t", k=4)
        bqT = view(40, 4 * SEQ, "p (k t) -> p k t", k=4)
        bkT = view(44, 2 * SEQ, "p (n t) -> p n t", n=2)
        bv = view(46, HALVES * P, "p (h c) -> p h c", h=HALVES)
        ybT = view(47, 4 * SEQ, "p (k t) -> p k t", k=4)
        c_qT = view(51, C_HEADS * SEQ, "p (h t) -> p h t", h=C_HEADS)
        c_kT = view(55, C_HEADS * SEQ, "p (h t) -> p h t", h=C_HEADS)
        c_qw = view(59, C_HEADS * P, "p (h t) -> p h t", h=C_HEADS)
        c_kw = view(61, C_HEADS * P, "p (h t) -> p h t", h=C_HEADS)
        cv = view(63, HALVES * D, "p (h c) -> p h c", h=HALVES)
        cg = view(71, HALVES * D, "p (h c) -> p h c", h=HALVES)
        scT = view(79, C_HEADS * SEQ, "p (h t) -> p h t", h=C_HEADS)
        state = view(83, C_HEADS * C_V, "p (h e) -> p h e", h=C_HEADS)
        ycT = view(16, KT * SEQ, "p (k t) -> p k t", k=KT)
        wsT = view(87, A_GROUPS * P, "p (g t) -> p g t", g=A_GROUPS)
        bs = view(89, A_GROUPS * P, "p (g t) -> p g t", g=A_GROUPS)
        tables = view(91, 2 * C_HEADS * P + MAP + C_HEADS + LAYERS * 2 * HEADS)
        t0 = 91 + 2 * C_HEADS * P / 256
        decayT = view(91, C_HEADS * P, "p (h t) -> p h t", h=C_HEADS)
        q_decay = view(93, C_HEADS * P, "p (h t) -> p h t", h=C_HEADS)
        swa_dist = view(t0, MAP)
        k_decay = view(t0 + 1.5, C_HEADS)
        neg_sinks = view(t0 + 1.5 + C_HEADS / 256, LAYERS * 2 * HEADS)
        gate2 = dict(a=view(63, KT * SEQ, "p (k t) -> p k t", k=KT),
                     b=view(51, KT * SEQ, "p (k t) -> p k t", k=KT),
                     c=view(63, KT * SEQ, "p (k t) -> p k t", k=KT))
        last_row = view(28, D)

        MAXS, NEGM, SUMS, INV, SINK = range(5)
        attv = att[:].rearrange("p (n s m b) -> p n s m b", n=12, s=5, m=2)
        neg_lambda = stat[:, 0:LAYERS]
        lam_work = stat[:, 4:4 + 4 * LAYERS]
        sq = stat[:, 16:32]
        rs = stat[:, 32:48]
        mean_var = stat[:, 48:80].rearrange("p (n v) -> p n v", v=2)
        bn = stat[:, 80:176].rearrange("p (n s) -> p n s", s=6)
        logit = routing[:, 0:16].rearrange("p (h e) -> p h e", h=HALVES)
        tops = routing[:, 16:32].rearrange("p (h e) -> p h e", h=HALVES)
        pick = routing[:, 32:48].rearrange("p (h e) -> p h e", h=HALVES)
        top_gate = routing[:, 48:64].rearrange("p (h e) -> p h e", h=HALVES)

        def new(name):
            return ctx.enter_context(nc.semaphore(name))

        loaded = [new(f"slot{i}_loaded") for i in range(SLOTS)]
        unit_used = new("unit_used")
        start_loaded = new("start_loaded")
        x_loaded = new("x_loaded")
        once = Signals(new, "once_", consts=3, eps_added=1, setup=21, lam_sum=1, lam_exp=1, angles=1, trig=2, bias=HEADS * BUCKETS, ind=BUCKETS - 1,
                       tables_loaded=16, sinks=1, routed=1, logits=1, tops=4, top_diff=1, top_exp=1, pick=9,
                       row_loaded=16, sq=2, rs=1, n=2, g=2, stored=16)

        def attention(jobs):
            return dict(biased=2 * jobs, maxed=2 * jobs, negated=jobs, exped=4 * jobs, inverse=jobs,
                        weighed=4 * jobs, turned=jobs, values=jobs)

        f = Signals(new, "first_", full=len(JOBS1), eps_added=5, **attention(12), lam_weight=8,
                    latent=2, latent_sq=4, latent_rs=2, latent_n=4, cqT=3, ckvT=2, q_rows=2, kv_rows=4, kr_tmp=8,
                    kcat=4, q_tmp=8, q_rot=4, qT=2, kT=2, dq=2, dk=2, dv=2, o_sq=2, o_sum=2, o_rs=1, o_n=2, oT=2,
                    gate=16, m_tmp=2, mT=4, mix=2, ln_stats=8, ln_aggr=4, ln_rs=2, ln_n=4, ln_g=2, x=2,
                    norm_rows=32, turned_x=4, ple_loaded=32, ple_sig=2, ple_e=2, residual=1)
        s = Signals(new, "second_", full=len(JOBS2), eps_added=6, **attention(4), sink_diff=4, sink_exp=4, sink_added=4,
                    params=32, sq=6, rs=3, n=6, turned_act=12, turned_dve=12, av=1, av_sq=2, av_rs=1, av_n=2, ws=1, uT=1,
                    ya_tmp=4, yaT=1, bq=1, bkv=2, cq=1, cqw=1, ck=1, ckw=1, cv=2, cg=2, scT=4, state=1,
                    o_stats=8, o_aggr=8, o_rs=2, o_n=8, yc=2, ycT=8, gate=24, m_tmp=4, mT=6, mix=2)

        def ffn_signals(prefix, steps):
            return Signals(new, prefix, hidden=2 * steps, silu=2 * steps, gated=2 * steps, taken=4)

        dense, moe = ffn_signals("dense_", DENSE_STEPS), ffn_signals("expert_", EXPERT_STEPS)
        ffn1, ffn2 = ffn_signals("ffn1_", FFN_STEPS), ffn_signals("ffn2_", FFN_STEPS)

        def slot(c, k_tiles, width):
            base = (c % SLOTS) * UNIT
            return ring[:, base:base + k_tiles * width].rearrange("p (k n) -> p k n", k=k_tiles)

        def landed(c, turns):
            return loaded[c % SLOTS], 16 * (c // SLOTS + 1) + 16 * turns

        def pair(jobs, name):
            b = 2 * (jobs[name] % 4)
            return psum[:, b:b + 2].rearrange("p b n -> p (b n)")

        def banks(jobs, name):
            b = 2 * (jobs[name] % 4)
            return psum[:, b:b + 2]

        block = ctx.enter_context(nc.Block())

        @block.sync
        def _(sp):
            def load(c, turns, source, words=GEMM):
                if not (isinstance(turns, int) and c + SLOTS * turns < SLOTS):
                    sp.wait_ge(unit_used, c - SLOTS + 1 + SLOTS * turns)
                base = (c % SLOTS) * UNIT
                sp.dma_start(ring[:, base:base + words], source).then_inc(loaded[c % SLOTS], 16)

            def load_ffn(packed, first, steps, c0, turns):
                whole = steps // SLOTS
                with sp.Fori(0, whole) as g:
                    for q in range(SLOTS):
                        load(c0 + q, turns + g, packed[bass.ds((first + SLOTS * g + q) * P, P), :], UNIT)
                for q in range(SLOTS * whole, steps):
                    load(c0 + q, turns, packed[bass.ds((first + q) * P, P), :], UNIT)

            sp.dma_start(xT, a["xT"].rearrange("p (k t) -> p k t", k=KT)).then_inc(x_loaded, 16)
            narrow = {1: ("latent1", KT * (LATENT - 512)), 8: ("w_uq", 3 * 768), 9: ("w_ukv", 2 * D), 21: ("ple_proj", 2 * D)}
            c = 0
            for l in range(LAYERS):
                wide = 0
                for u in range(MIX1 + PLE):
                    if u in narrow:
                        name, words = narrow[u]
                        load(c, 0, a[name][l * P:(l + 1) * P, :], words)
                    else:
                        load(c, 0, a["first_wide"][(l * 18 + wide) * P:(l * 18 + wide + 1) * P, :])
                        wide += 1
                    c += 1
                if l == 0:
                    load_ffn(a["dense"], 0, DENSE_STEPS, c, 0)
                    c += DENSE_STEPS
            with sp.Fori(0, EXPERTS * EXPERT_STEPS // SLOTS) as g:
                for q in range(SLOTS):
                    load(MOE_START + q, g, a["experts"][bass.ds((SLOTS * g + q) * P, P), :], UNIT)
            with sp.Fori(0, LAYERS) as l:
                turns = l * (LAYER2 // SLOTS)
                load_ffn(a["ffn1"], l * FFN_STEPS, FFN_STEPS, BLOCK2, turns)
                for view_, name in ((wsT, "spatial_w"), (bs, "spatial_b")):
                    sp.dma_start(view_, a[name][bass.ds(l * P, P), :].rearrange("p (g t) -> p g t", g=A_GROUPS)).then_inc(s["params"].sem, 16)
                wide = 0
                for u in range(MIX2):
                    c = BLOCK2 + FFN_STEPS + u
                    if u == 3:
                        load(c, turns, a["swa_kv"][bass.ds(l * P, P), :], KT * 256)
                    else:
                        load(c, turns, a["second_wide"][bass.ds((l * (MIX2 - 1) + wide) * P, P), :])
                        wide += 1
                load_ffn(a["ffn2"], l * FFN_STEPS, FFN_STEPS, FFN2_START, turns)
            sp.wait_ge(*once["g"].by(0))
            sp.dma_start(out.rearrange("(h p) d -> p h d", p=P), xn).then_inc(once["stored"].sem, 16)
            sp.wait_ge(*once["stored"].by(0))

        @block.gpsimd
        def _(pool):
            def root(sig, l, name, added, o, mean, eps):
                at = 2 * HEADS * (1 if eps == LN_EPS else 2)
                nc.gpsimd.tensor_tensor(out=o, in0=mean, in1=consts[:, at:at + o.shape[1]], op=ALU.add).then_inc(sig["eps_added"].sem, 1)
                pool.wait_ge(*sig["eps_added"].by(l, added))
                nc.gpsimd.tensor_tensor(out=o, in0=o, in1=consts[:, 0:o.shape[1]], op=ALU.pow).then_inc(sig[name].sem, 1)

            for n, value in enumerate((-0.5, LN_EPS, RMS_EPS)):
                nc.gpsimd.memset(consts[:, 2 * HEADS * n:2 * HEADS * (n + 1)], value).then_inc(once["consts"].sem, 1)
            pool.wait_ge(*once["consts"].by(0))
            for l in range(LAYERS):
                for n in range(2):
                    pool.wait_ge(*f["latent_sq"].by(l, 2 * n + 2))
                    root(f, l, "latent_rs", n + 1, rs[:, 2 * n:2 * n + 2], sq[:, 2 * n:2 * n + 2], LN_EPS)
                if l == 0:
                    pool.wait_ge(*once["bias"].by(0))
                else:
                    pool.wait_ge(*f["x"].by(0))
                pool.dma_start(norm_rows, a["ln_mix"][l * P:(l + 1) * P, :].rearrange("p (n d) -> p n d", n=2)).then_inc(f["norm_rows"].sem, 16)
                pool.wait_ge(*f["o_sum"].by(l))
                root(f, l, "o_rs", 3, rs[:, 0:2 * HEADS], sq[:, 0:2 * HEADS], LN_EPS)
                pool.wait_ge(*f["mix"].by(l))
                pool.dma_start(pT, a["pT"][l * P:(l + 1) * P, :].rearrange("p (k t) -> p k t", k=2)).then_inc(f["ple_loaded"].sem, 16)
                pool.dma_start(router, a["router"][:, :]).then_inc(f["ple_loaded"].sem, 16)
                pool.wait_ge(*f["ln_aggr"].by(l, 2))
                root(f, l, "ln_rs", 4, rs[:, 0:2], mean_var[:, 0:2, 1], LN_EPS)
                pool.wait_ge(*f["x"].by(l, 1))
                pool.dma_start(norm_rows, a["ln_ffn"][l * P:(l + 1) * P, :].rearrange("p (n d) -> p n d", n=2)).then_inc(f["norm_rows"].sem, 16)
                pool.wait_ge(*f["ln_aggr"].by(l))
                root(f, l, "ln_rs", 5, rs[:, 0:2], mean_var[:, 0:2, 1], LN_EPS)
            pool.wait_ge(*f["x"].by(1))
            pool.dma_start(tables, a["tables2"][:, :]).then_inc(once["tables_loaded"].sem, 16)
            with pool.Fori(0, LAYERS) as l:
                for n in range(2):
                    if n == 1:
                        pool.wait_ge(*s["params"].by(l))
                    pool.wait_ge(*s["sq"].by(l, 2 * n + 2))
                    root(s, l, "rs", n + 1, rs[:, 0:2], sq[:, 0:2], RMS_EPS)
                nc.gpsimd.affine_select(out=wsT, in_=wsT, compare_op=ALU.is_ge, fill=0.0, base=0,
                                        pattern=[[0, A_GROUPS], [1, P]], channel_multiplier=-1).then_inc(s["ws"].sem, 1)
                pool.wait_ge(*s["av_sq"].by(l))
                root(s, l, "av_rs", 3, rs[:, 4:6], sq[:, 4:6], RMS_EPS)
                for n in range(2):
                    pool.wait_ge(*s["o_aggr"].by(l, 4 * n + 4))
                    root(s, l, "o_rs", 4 + n, rs[:, 8 + 4 * n:12 + 4 * n], mean_var[:, 4 + 4 * n:8 + 4 * n, 1], LN_EPS)
                pool.wait_ge(*s["sq"].by(l))
                root(s, l, "rs", 6, rs[:, 0:2], sq[:, 0:2], RMS_EPS)
            pool.wait_ge(*s["mix"].by(1))
            pool.dma_start(last_row, a["final_norm"][:, :]).then_inc(once["row_loaded"].sem, 16)
            pool.wait_ge(*once["sq"].by(0))
            root(once, 0, "rs", 1, rs[:, 0:2], sq[:, 0:2], RMS_EPS)

        @block.tensor
        def _(pe):
            unit_open = [False]

            def count_unit(m):
                if unit_open[0]:
                    m.then_inc(unit_used, 1)
                    unit_open[0] = False

            def end_unit():
                unit_open[0] = True

            def product(terms):
                for i, (o, lhs, rhs) in enumerate(terms):
                    m = pe.matmul(o, lhs, rhs, start=i == 0, stop=i == len(terms) - 1)
                    if i == 0 and len(terms) > 1:
                        count_unit(m)
                return m

            def row_product(o, w, k_tiles, width, lhs, half, column=0):
                return product([(o, lhs[:, k, half * P:(half + 1) * P], w[:, k, column:column + width]) for k in range(k_tiles)])

            def rows(jobs, name, w, k_tiles, width, lhs=xT, column=0):
                for h in range(HALVES):
                    m = row_product(banks(jobs, name)[:, h, 0:width], w, k_tiles, width, lhs, h, column)
                return m

            def columns(jobs, name, w, k_tiles, rhs=xT, column=0):
                for n in range(4):
                    at = column + n * P
                    m = product([(pair(jobs, name)[:, n * SEQ:(n + 1) * SEQ], w[:, k, at:at + P], rhs[:, k, :]) for k in range(k_tiles)])
                return m

            def turn_rows(jobs, name, source, tiles, first):
                for n in range(tiles):
                    for h in range(HALVES):
                        m = pe.transpose(pair(jobs, name)[:, n * SEQ + h * P:n * SEQ + (h + 1) * P],
                                         source[:, h, first + n * P:first + (n + 1) * P], ident[:])
                        if n == 0 and h == 0:
                            count_unit(m)
                return m

            def map_scores(o, q, k):
                count_unit(pe.matmul(o[:, 0:P], q[:, 0:P], k[:, 0:P], start=True, stop=True))
                return pe.matmul(o[:, P:MAP], q[:, P:SEQ], k, start=True, stop=True)

            def turn_map(o, weights):
                for n in range(3):
                    m = pe.transpose(o[:, n * P:(n + 1) * P], weights[:, n * P:(n + 1) * P], ident[:])
                return m

            def pair_values(o, turned, values):
                for m in range(2):
                    om = o[64 * m:64 * m + 64]
                    pe.matmul(om[:, 0:P], values(m, 0), turned[:, m, 0:P], start=True, stop=True)
                    mm = product([(om[:, P:SEQ], values(m, 0), turned[:, m, P:2 * P]),
                                  (om[:, P:SEQ], values(m, 1), turned[:, m, 2 * P:MAP])])
                return mm

            def network(sig, l, steps, c0, turns):
                def up(step, q, t, guarded=True):
                    pe.wait_ge(*landed(c0 + q, t))
                    w = slot(c0 + q, 2 * KT, FF_STEP)
                    for i in range(2):
                        bank = (2 * q + i) % 4
                        if guarded:
                            pe.wait_ge(*sig["gated"].by(l, 2 * step + i - 3))
                        for m in range(2):
                            mm = product([(psum[:, bank, m * SEQ:(m + 1) * SEQ], w[:, m * KT + k, i * P:(i + 1) * P], xT[:, k, :])
                                          for k in range(KT)])
                        mm.then_inc(sig["hidden"].sem, 1)

                def down(step, q, first=False, last=False):
                    base = ((c0 + q) % SLOTS) * UNIT + UP
                    w = ring[:, base:base + 2 * D].rearrange("p (f n) -> p f n", f=2)
                    for i in range(2):
                        pe.wait_ge(*sig["gated"].by(l, 2 * step + i + 1))
                        for h in range(HALVES):
                            for n in range(2):
                                mm = pe.matmul(psum[:, 4 + 2 * h + n], hT[:, (2 * q + i) % 4, h * P:(h + 1) * P],
                                               w[:, i, n * 512:(n + 1) * 512], start=first and i == 0, stop=last and i == 1,
                                               skip_group_check=True)
                    mm.then_inc(unit_used, 1)

                up(0, 0, turns, guarded=False)
                up(1, 1, turns, guarded=False)
                down(0, 0, first=True)
                whole = (steps - 2) // SLOTS
                with pe.Fori(0, whole) as g:
                    for q in range(1, 1 + SLOTS):
                        up(SLOTS * g + q + 1, q + 1, turns + g)
                        down(SLOTS * g + q, q)
                for step in range(SLOTS * whole + 1, steps - 1):
                    up(step + 1, step + 1, turns)
                    down(step, step)
                down(steps - 1, steps - 1, last=True)

            pe.wait_ge(x_loaded, 16)
            pe.wait_ge(start_loaded, 16 * START_LOADS)
            c = 0

            for l in range(LAYERS):
                J = JOBS1

                def banks_free(name, l):
                    signal, count = FREED1[list(J)[J[name] - 4]]
                    return f[signal].by(l, count)

                if l == 1:
                    pe.wait_ge(*f["turned_x"].by(0))
                for i, width in enumerate((512, LATENT - 512)):
                    pe.wait_ge(*landed(c, 0))
                    rows(J, f"latent{i}", slot(c, KT, width), KT, width).then_inc(f["full"].sem, 1)
                    end_unit()
                    c += 1
                for name in ("dq0", "dq1", "dk0", "dk1", "dv0", "dv1"):
                    if J[name] >= 4:
                        pe.wait_ge(*banks_free(name, l))
                    pe.wait_ge(*landed(c, 0))
                    w = slot(c, KT, 512)
                    (rows(J, name, w, KT, 512) if name[:2] == "dv" else columns(J, name, w, KT)).then_inc(f["full"].sem, 1)
                    end_unit()
                    c += 1
                pe.wait_ge(*banks_free("cq_turn", l))
                pe.wait_ge(*f["latent_n"].by(l))
                turn_rows(J, "cq_turn", latent, 3, 0).then_inc(f["full"].sem, 1)
                pe.wait_ge(*banks_free("ckv_turn", l))
                turn_rows(J, "ckv_turn", latent, 2, Q_RANK).then_inc(f["full"].sem, 1)
                for name, k_tiles, width, source in (("uq", 3, 384, cqT), ("ukv", 2, 512, ckvT)):
                    pe.wait_ge(*landed(c, 0))
                    w = slot(c, k_tiles, 2 * width)
                    for h in range(HALVES):
                        pe.wait_ge(*banks_free(f"{name}{h}", l))
                        pe.wait_ge(*f["cqT" if name == "uq" else "ckvT"].by(l))
                        for n in range(2):
                            m = row_product(banks(J, f"{name}{h}")[:, n, 0:width], w, k_tiles, width, source, h, n * width)
                        m.then_inc(f["full"].sem, 1)
                    end_unit()
                    c += 1
                for name, source, ready in (("q", qrow, "q_rot"), ("k", kcat, "kcat")):
                    if name == "k":
                        pe.wait_ge(*f["kv_rows"].by(l))
                    for i in range(2):
                        o = pair(J, f"{name}_turn{i}")
                        pe.wait_ge(*banks_free(f"{name}_turn{i}", l))
                        pe.wait_ge(*f[ready].by(l))
                        for n in range(4):
                            for h in range(HALVES):
                                m = pe.transpose(o[0:MLA_QK, n * SEQ + h * P:n * SEQ + (h + 1) * P], source[:, h, 4 * i + n, :], ident[:])
                                if n == h == 0:
                                    count_unit(m)
                        m.then_inc(f["full"].sem, 1)

                pe.wait_ge(*f["dv"].by(l))
                pe.wait_ge(*f["dk"].by(l))
                pe.wait_ge(*f["dq"].by(l))
                for i in range(HEADS + 2):
                    if i < HEADS:
                        pe.wait_ge(*banks_free(f"diff_scores{i}", l))
                        for m in range(2):
                            mm = map_scores(banks(J, f"diff_scores{i}")[:, m], dqT[64 * m:64 * m + 64, i, :], dkT[64 * m:64 * m + 64, i, :])
                        mm.then_inc(f["full"].sem, 1)
                    if 0 <= i - 1 < HEADS:
                        h = i - 1
                        o = pair(J, f"diff_turn{h}")
                        pe.wait_ge(*banks_free(f"diff_turn{h}", l))
                        pe.wait_ge(*f["weighed"].by(l, 4 * h + 4))
                        turn_map(o, T[:, h % 2, 0]).then_inc(f["full"].sem, 1)
                    if 0 <= i - 2 < HEADS:
                        h = i - 2
                        o = pair(J, f"diff_values{h}")
                        pe.wait_ge(*banks_free(f"diff_values{h}", l))
                        pe.wait_ge(*f["turned"].by(l, h + 1))
                        w, vh = PT[:, h % 2, 0], dv[:, :, h * P:(h + 1) * P]
                        pe.matmul(o[:, 0:P], w[:, 0:P], vh[:, 0], start=True, stop=True)
                        product([(o[:, P:2 * P], w[:, P:2 * P], vh[:, 0]), (o[:, P:2 * P], w[:, 2 * P:MAP], vh[:, 1])]).then_inc(f["full"].sem, 1)

                pe.wait_ge(*f["qT"].by(l))
                pe.wait_ge(*f["kT"].by(l))
                for i in range(HEADS // 2 + 2):
                    if i < HEADS // 2:
                        pe.wait_ge(*banks_free(f"mla_scores{i}", l))
                        for m in range(2):
                            mm = map_scores(banks(J, f"mla_scores{i}")[:, m], qT[0:MLA_QK, 2 * i + m, :], kT[0:MLA_QK, 2 * i + m, :])
                        mm.then_inc(f["full"].sem, 1)
                    if 0 <= i - 1 < HEADS // 2:
                        h = i - 1
                        pe.wait_ge(*banks_free(f"mla_turn{h}", l))
                        pe.wait_ge(*f["weighed"].by(l, 4 * (HEADS + h) + 4))
                        for m in range(2):
                            mm = turn_map(banks(J, f"mla_turn{h}")[:, m], T[:, h % 2, m])
                        mm.then_inc(f["full"].sem, 1)
                    if 0 <= i - 2 < HEADS // 2:
                        h = i - 2
                        o = pair(J, f"mla_values{h}")
                        pe.wait_ge(*banks_free(f"mla_values{h}", l))
                        pe.wait_ge(*f["turned"].by(l, HEADS + h + 1))
                        pair_values(o, PT[:, h % 2], lambda m, half: vrow[:, half, 2 * h + m, :]).then_inc(f["full"].sem, 1)

                for i in range(2):
                    pe.wait_ge(*banks_free(f"gate_a{i}", l))
                    pe.wait_ge(*landed(c, 0))
                    columns(J, f"gate_a{i}", slot(c, KT, 512), KT).then_inc(f["full"].sem, 1)
                    end_unit()
                    c += 1
                for i in range(2):
                    pe.wait_ge(*banks_free(f"o_turn{i}", l))
                    pe.wait_ge(*f["o_n"].by(l))
                    turn_rows(J, f"o_turn{i}", xn, 4, 4 * i * P).then_inc(f["full"].sem, 1)
                for i in range(2):
                    pe.wait_ge(*banks_free(f"branch_a{i}", l))
                    pe.wait_ge(*f["oT"].by(l))
                    pe.wait_ge(*landed(c, 0))
                    columns(J, f"branch_a{i}", slot(c, KT, 512), KT, oT).then_inc(f["full"].sem, 1)
                    end_unit()
                    c += 1
                for i in range(2):
                    pe.wait_ge(*banks_free(f"gate_b{i}", l))
                    pe.wait_ge(*landed(c, 0))
                    columns(J, f"gate_b{i}", slot(c, KT, 512), KT).then_inc(f["full"].sem, 1)
                    end_unit()
                    c += 1
                pe.wait_ge(*landed(c, 0))
                for i in range(2):
                    pe.wait_ge(*banks_free(f"branch_b{i}", l))
                    pe.wait_ge(*f["values"].by(l))
                    columns(J, f"branch_b{i}", slot(c, 4, D), 4, obT, 512 * i).then_inc(f["full"].sem, 1)
                end_unit()
                c += 1
                for i in range(2):
                    pe.wait_ge(*banks_free(f"mix{i}", l))
                    pe.wait_ge(*f["mT"].by(l))
                    pe.wait_ge(*landed(c, 0))
                    rows(J, f"mix{i}", slot(c, KT, 512), KT, 512, m1T).then_inc(f["full"].sem, 1)
                    end_unit()
                    c += 1
                for i in range(2):
                    pe.wait_ge(*banks_free(f"x_turn{i}", l))
                    pe.wait_ge(*f["x"].by(l, 1))
                    turn_rows(J, f"x_turn{i}", X, 4, 4 * i * P).then_inc(f["full"].sem, 1)
                for i in range(2):
                    pe.wait_ge(*banks_free(f"ple_gate{i}", l))
                    pe.wait_ge(*f["turned_x"].by(l, 2))
                    pe.wait_ge(*landed(c, 0))
                    rows(J, f"ple_gate{i}", slot(c, KT, 512), KT, 512).then_inc(f["full"].sem, 1)
                    end_unit()
                    c += 1
                pe.wait_ge(*f["ple_loaded"].by(l))
                pe.wait_ge(*landed(c, 0))
                for i in range(2):
                    pe.wait_ge(*banks_free(f"ple_proj{i}", l))
                    rows(J, f"ple_proj{i}", slot(c, 2, D), 2, 512, pT, 512 * i).then_inc(f["full"].sem, 1)
                end_unit()
                c += 1
                pe.wait_ge(*f["ple_e"].by(l))
                if l == 0:
                    assert c == DENSE_START
                    network(dense, 0, DENSE_STEPS, c, 0)
                    c += DENSE_STEPS
                    for i in range(2):
                        pe.wait_ge(*banks_free(f"end_turn{i}", l))
                        pe.wait_ge(*f["x"].by(l))
                        turn_rows(J, f"end_turn{i}", X, 4, 4 * i * P).then_inc(f["full"].sem, 1)
                else:
                    assert c == MOE_START
                    r = router[:, 0:KT * EXPERTS].rearrange("p (k e) -> p k e", k=KT)
                    for h in range(HALVES):
                        m = row_product(psum[:, 6, h * EXPERTS:(h + 1) * EXPERTS], r, KT, EXPERTS, xT, h)
                    m.then_inc(once["routed"].sem, 1)
                    with pe.Fori(0, EXPERTS // 2) as couple:
                        for e in range(2):
                            network(moe, couple * 2 + e, EXPERT_STEPS, MOE_START + e * EXPERT_STEPS, couple * (2 * EXPERT_STEPS // SLOTS))

            pe.wait_ge(*once["tables_loaded"].by(0))
            with pe.Fori(0, LAYERS) as l:
                J = JOBS2
                turns = l * (LAYER2 // SLOTS)
                unit = [BLOCK2 + FFN_STEPS]

                def banks_free(name, l):
                    signal, count = FREED2[list(J)[J[name] - 4]]
                    return s[signal].by(l, count)

                def weights(k_tiles, width):
                    pe.wait_ge(*landed(unit[0], turns))
                    return slot(unit[0], k_tiles, width)

                def end_of_unit():
                    end_unit()
                    unit[0] += 1

                def turn_normed(name, n):
                    for i in range(2):
                        if J[f"{name}_turn{i}"] >= 4:
                            pe.wait_ge(*banks_free(f"{name}_turn{i}", l))
                        pe.wait_ge(*s["n"].by(l, 2 * n))
                        turn_rows(J, f"{name}_turn{i}", xn, 4, 4 * i * P).then_inc(s["full"].sem, 1)
                    pe.wait_ge(*s["turned_act"].by(l, 4 * n))
                    pe.wait_ge(*s["turned_dve"].by(l, 4 * n))

                turn_normed("ffn1", 1)
                network(ffn1, l, FFN_STEPS, BLOCK2, turns)
                turn_normed("mix", 2)
                for name in ("a_v", "a_u", "b_q"):
                    if J[name] >= 4:
                        pe.wait_ge(*banks_free(name, l))
                    w = weights(KT, 512)
                    (rows(J, name, w, KT, 512) if name == "a_v" else columns(J, name, w, KT)).then_inc(s["full"].sem, 1)
                    end_of_unit()
                pe.wait_ge(*banks_free("b_kv", l))
                w = weights(KT, 256)
                for n in range(2):
                    for half in range(2):
                        product([(banks(J, "b_kv")[64 * half:64 * half + 64, 0, n * SEQ:(n + 1) * SEQ],
                                  w[:, k, n * SWA_DIM:(n + 1) * SWA_DIM], xT[:, k, :]) for k in range(KT)])
                for h in range(HALVES):
                    m = row_product(banks(J, "b_kv")[:, 1, h * P:(h + 1) * P], w, KT, P, xT, h, P)
                m.then_inc(s["full"].sem, 1)
                end_of_unit()
                pe.wait_ge(*banks_free("c_q", l))
                columns(J, "c_q", weights(KT, 512), KT).then_inc(s["full"].sem, 1)
                end_of_unit()
                pe.wait_ge(*banks_free("c_k", l))
                w = weights(KT, 512)
                columns(J, "c_k", w, KT).then_inc(s["full"].sem, 1)
                o = pair(J, "c_krow")
                pe.wait_ge(*banks_free("c_krow", l))
                row_product(o[:, 0:512], w, KT, 512, xT, 0).then_inc(s["full"].sem, 1)
                end_of_unit()
                o = pair(J, "a_mix")
                pe.wait_ge(*banks_free("a_mix", l))
                pe.wait_ge(*s["av_n"].by(l))
                pe.wait_ge(*s["ws"].by(l))
                for g in range(A_GROUPS):
                    for h in range(HALVES):
                        m = pe.matmul(o[:, g * SEQ + h * P:g * SEQ + (h + 1) * P], v2[:, h, g * P:(g + 1) * P], wsT[:, g, :], start=True, stop=True)
                        if g == h == 0:
                            count_unit(m)
                m.then_inc(s["full"].sem, 1)
                for i in range(2):
                    pe.wait_ge(*banks_free(f"c_v{i}", l))
                    rows(J, f"c_v{i}", weights(KT, 512), KT, 512).then_inc(s["full"].sem, 1)
                    end_of_unit()
                pe.wait_ge(*s["bq"].by(l))
                pe.wait_ge(*s["bkv"].by(l))
                for i in range(HEADS // 2 + 2):
                    if i < HEADS // 2:
                        pe.wait_ge(*banks_free(f"swa_scores{i}", l))
                        for m in range(2):
                            mm = map_scores(banks(J, f"swa_scores{i}")[:, m], bqT[64 * m:64 * m + 64, i, :], bkT[64 * m:64 * m + 64, i // 2, :])
                        mm.then_inc(s["full"].sem, 1)
                    if 0 <= i - 1 < HEADS // 2:
                        h = i - 1
                        pe.wait_ge(*banks_free(f"swa_turn{h}", l))
                        pe.wait_ge(*s["weighed"].by(l, 4 * h + 4))
                        for m in range(2):
                            mm = turn_map(banks(J, f"swa_turn{h}")[:, m], T[:, h % 2, m])
                        mm.then_inc(s["full"].sem, 1)
                    if 0 <= i - 2 < HEADS // 2:
                        h = i - 2
                        o = pair(J, f"swa_values{h}")
                        pe.wait_ge(*banks_free(f"swa_values{h}", l))
                        pe.wait_ge(*s["turned"].by(l, h + 1))
                        pair_values(o, PT[:, h % 2], lambda m, half: bv[:, half, (h // 2) * 64:(h // 2) * 64 + 64]).then_inc(s["full"].sem, 1)
                for i in range(2):
                    pe.wait_ge(*banks_free(f"c_g{i}", l))
                    rows(J, f"c_g{i}", weights(KT, 512), KT, 512).then_inc(s["full"].sem, 1)
                    end_of_unit()
                o = pair(J, "c_scores")
                pe.wait_ge(*banks_free("c_scores", l))
                pe.wait_ge(*s["ck"].by(l))
                for h in range(C_HEADS):
                    for n in range(HALVES):
                        m = pe.matmul(o[:, h * SEQ + n * P:h * SEQ + (n + 1) * P], c_kT[:, h, n * P:(n + 1) * P], c_qT[:, h, n * P:(n + 1) * P], start=True, stop=True)
                        if h == n == 0:
                            count_unit(m)
                m.then_inc(s["full"].sem, 1)
                o = pair(J, "c_state")
                pe.wait_ge(*banks_free("c_state", l))
                pe.wait_ge(*s["ckw"].by(l))
                pe.wait_ge(*s["cv"].by(l))
                for h in range(C_HEADS):
                    m = pe.matmul(o[:, h * C_V:(h + 1) * C_V], c_kw[:, h, :], cv[:, 0, h * C_V:(h + 1) * C_V], start=True, stop=True)
                m.then_inc(s["full"].sem, 1)
                for n in range(HALVES):
                    o = pair(J, f"c_out{n}")
                    pe.wait_ge(*banks_free(f"c_out{n}", l))
                    pe.wait_ge(*s["scT"].by(l))
                    if n == 1:
                        pe.wait_ge(*s["state"].by(l))
                        pe.wait_ge(*s["cqw"].by(l))
                    for h in range(C_HEADS):
                        terms = [(o[:, h * C_V:(h + 1) * C_V], scT[:, h, n * P:(n + 1) * P], cv[:, n, h * C_V:(h + 1) * C_V])]
                        if n == 1:
                            terms.append((o[:, h * C_V:(h + 1) * C_V], c_qw[:, h, :], state[:, h, :]))
                        m = product(terms)
                    m.then_inc(s["full"].sem, 1)
                for branch, k_tiles, source, ready in (("a", 4, yaT, "yaT"), ("b", 4, ybT, "values"), ("c", KT, ycT, "ycT")):
                    for i in range(2):
                        pe.wait_ge(*banks_free(f"gate_{branch}{i}", l))
                        columns(J, f"gate_{branch}{i}", weights(KT, 512), KT).then_inc(s["full"].sem, 1)
                        end_of_unit()
                    if branch == "c":
                        for i in range(2):
                            pe.wait_ge(*banks_free(f"c_turn{i}", l))
                            pe.wait_ge(*s["yc"].by(l))
                            turn_rows(J, f"c_turn{i}", xn, 4, 4 * i * P).then_inc(s["full"].sem, 1)
                    for i in range(2):
                        pe.wait_ge(*banks_free(f"branch_{branch}{i}", l))
                        pe.wait_ge(*s[ready].by(l))
                        if branch == "c":
                            columns(J, f"branch_c{i}", weights(KT, 512), KT, source).then_inc(s["full"].sem, 1)
                            end_of_unit()
                        else:
                            columns(J, f"branch_{branch}{i}", weights(4, D), 4, source, 512 * i).then_inc(s["full"].sem, 1)
                            if i == 1:
                                end_of_unit()
                for i in range(2):
                    pe.wait_ge(*banks_free(f"mix{i}", l))
                    pe.wait_ge(*s["mT"].by(l))
                    rows(J, f"mix{i}", weights(KT, 512), KT, 512, m2T).then_inc(s["full"].sem, 1)
                    end_of_unit()
                assert unit[0] == FFN2_START
                turn_normed("ffn2", 3)
                network(ffn2, l, FFN_STEPS, FFN2_START, turns)

        @block.scalar
        def _(act):
            def exps(sig, l, i, b, scale):
                act.wait_ge(*sig["negated"].by(l, i + 1))
                for m in range(2):
                    for q, (lo, hi) in enumerate(((0, P), (P, MAP))):
                        nc.scalar.activation(T[:, b, m, lo:hi], T[:, b, m, lo:hi], ACT.Exp, bias=attv[:, i, NEGM, m, q:q + 1],
                                             scale=scale, accum_out=attv[:, i, SUMS, m, q:q + 1]).then_inc(sig["exped"].sem, 1)

            def silus(sig, l, steps):
                def tile(step, parity, i, guarded=True):
                    act.wait_ge(*sig["hidden"].by(l, 2 * step + i + 1))
                    if guarded:
                        act.wait_ge(*sig["gated"].by(l, 2 * step + i - 1))
                    nc.scalar.activation(sil[:, i, :], psum[:, 2 * parity + i, 0:SEQ], ACT.Silu).then_inc(sig["silu"].sem, 1)
                for step in range(2):
                    for i in range(2):
                        tile(step, step, i, guarded=step > 0)
                with act.Fori(1, steps // 2) as g:
                    for parity in range(2):
                        for i in range(2):
                            tile(2 * g + parity, parity, i)
                if steps % 2:
                    for i in range(2):
                        tile(steps - 1, 0, i)

            for place, name in ((ident[:], "identity"), (cols1[:], "columns_first"), (cols2[:], "columns_second"),
                                (causal, "causal"), (lambdas.rearrange("p n q c -> p (n q c)"), "lambdas"), (positions, "positions"),
                                (x_rows[:], "x_rows"), (view(95, BUCKETS * HEADS + BUCKETS), "bias_tables"), (inv_freq, "inv_freq")):
                act.dma_start(place, a[name][:, :]).then_inc(start_loaded, 16)

            act.wait_ge(start_loaded, 16 * START_LOADS)
            for l in range(LAYERS):
                J = JOBS1
                for i, (lo, hi) in enumerate(((0, 512), (512, LATENT))):
                    act.wait_ge(*f["full"].by(l, J[f"latent{i}"] + 1))
                    nc.scalar.copy(latent[:, :, lo:hi], banks(J, f"latent{i}")[:, :, 0:hi - lo]).then_inc(f["latent"].sem, 1)
                act.wait_ge(*f["latent"].by(l))
                for n, (lo, hi) in enumerate(((0, Q_RANK), (Q_RANK, Q_RANK + KV_RANK))):
                    for h in range(HALVES):
                        nc.scalar.activation(xn[:, h, lo:hi], latent[:, h, lo:hi], ACT.Square, scale=(hi - lo) ** -0.5,
                                             accum_out=sq[:, 2 * n + h:2 * n + h + 1]).then_inc(f["latent_sq"].sem, 1)
                if l == 0:
                    act.wait_ge(*once["lam_sum"].by(0))
                    nc.scalar.activation(lam_work[:, 4:4 + 2 * LAYERS], lam_work[:, 0:2 * LAYERS], ACT.Exp).then_inc(once["lam_exp"].sem, 1)
                    act.wait_ge(*once["angles"].by(0))
                    for q in range(2):
                        nc.scalar.activation(trig[:, q], angle[:, 3 + q], ACT.Sin).then_inc(once["trig"].sem, 1)
                for name, place in (("dq", dqT), ("dk", dkT)):
                    for i in range(2):
                        act.wait_ge(*f["full"].by(l, J[f"{name}{i}"] + 1))
                        nc.scalar.copy(place[:, 4 * i:4 * i + 4, :], pair(J, f"{name}{i}").rearrange("p (h t) -> p h t", h=4)).then_inc(f[name].sem, 1)
                for i in range(2):
                    act.wait_ge(*f["full"].by(l, J[f"dv{i}"] + 1))
                    nc.scalar.copy(dv[:, :, 512 * i:512 * i + 512], banks(J, f"dv{i}")).then_inc(f["dv"].sem, 1)
                for h in range(HALVES):
                    act.wait_ge(*f["full"].by(l, J[f"uq{h}"] + 1))
                    nc.scalar.copy(qrow[:, h].rearrange("p (b n) c -> p b (n c)", b=2), banks(J, f"uq{h}")[:, :, 0:384]).then_inc(f["q_rows"].sem, 1)
                act.wait_ge(*f["latent_n"].by(l))
                for h in range(HALVES):
                    act.wait_ge(*f["full"].by(l, J[f"ukv{h}"] + 1))
                    o = pair(J, f"ukv{h}").rearrange("p (n c) -> p n c", n=HEADS)
                    nc.scalar.copy(kcat[:, h, :, 0:NOPE], o[:, :, 0:NOPE]).then_inc(f["kv_rows"].sem, 1)
                    nc.scalar.copy(vrow[:, h], o[:, :, NOPE:]).then_inc(f["kv_rows"].sem, 1)
                for name, place in (("q", qT), ("k", kT)):
                    for i in range(2):
                        act.wait_ge(*f["full"].by(l, J[f"{name}_turn{i}"] + 1))
                        nc.scalar.copy(place[0:MLA_QK, 4 * i:4 * i + 4, :], pair(J, f"{name}_turn{i}")[0:MLA_QK].rearrange("p (h t) -> p h t", h=4)).then_inc(f[name + "T"].sem, 1)
                for i in range(HEADS + 2):
                    if i < HEADS:
                        exps(f, l, i, i % 2, 1.0)
                    if 0 <= i - 1 < HEADS:
                        h = i - 1
                        act.wait_ge(*f["full"].by(l, J[f"diff_turn{h}"] + 1))
                        nc.scalar.copy(PT[:, h % 2, 0], pair(J, f"diff_turn{h}")[:, 0:MAP]).then_inc(f["turned"].sem, 1)
                    if 0 <= i - 2 < HEADS:
                        h = i - 2
                        act.wait_ge(*f["full"].by(l, J[f"diff_values{h}"] + 1))
                        nc.scalar.copy(xn[:, :, h * P:(h + 1) * P], pair(J, f"diff_values{h}")[:, 0:SEQ].rearrange("p (h c) -> p h c", h=2)).then_inc(f["values"].sem, 1)
                for i in range(HEADS // 2 + 2):
                    if i < HEADS // 2:
                        exps(f, l, HEADS + i, i % 2, 1.0)
                    if 0 <= i - 1 < HEADS // 2:
                        h = i - 1
                        act.wait_ge(*f["full"].by(l, J[f"mla_turn{h}"] + 1))
                        nc.scalar.copy(PT[:, h % 2], banks(J, f"mla_turn{h}")[:, :, 0:MAP]).then_inc(f["turned"].sem, 1)
                    if 0 <= i - 2 < HEADS // 2:
                        h = i - 2
                        act.wait_ge(*f["full"].by(l, J[f"mla_values{h}"] + 1))
                        nc.scalar.copy(obT[:, h, :], pair(J, f"mla_values{h}")[:, 0:SEQ]).then_inc(f["values"].sem, 1)

                def gate_tiles(n):
                    for i in range(2):
                        name = f"gate_{'ab'[n]}{i}"
                        act.wait_ge(*f["full"].by(l, J[name] + 1))
                        for t in range(4):
                            col = l * N_COLS1 + COLS1["b_gate"] + KT * n + 4 * i + t
                            nc.scalar.activation(gate1[:, n, 4 * i + t, :], pair(J, name)[:, t * SEQ:(t + 1) * SEQ], ACT.Sigmoid,
                                                 bias=cols1[:, col:col + 1]).then_inc(f["gate"].sem, 1)
                gate_tiles(0)
                gate_tiles(1)
                for i in range(2):
                    act.wait_ge(*f["full"].by(l, J[f"x_turn{i}"] + 1))
                    nc.scalar.copy(xT[:, 4 * i:4 * i + 4, :], pair(J, f"x_turn{i}").rearrange("p (k t) -> p k t", k=4)).then_inc(f["turned_x"].sem, 1)
                for i in range(2):
                    act.wait_ge(*f["full"].by(l, J[f"ple_gate{i}"] + 1))
                    nc.scalar.activation(E[:, :, 512 * i:512 * i + 512], banks(J, f"ple_gate{i}"), ACT.Sigmoid).then_inc(f["ple_sig"].sem, 1)
                if l == 0:
                    silus(dense, 0, DENSE_STEPS)
                    for i in range(2):
                        act.wait_ge(*f["full"].by(l, J[f"end_turn{i}"] + 1))
                        nc.scalar.copy(xT[:, 4 * i:4 * i + 4, :], pair(J, f"end_turn{i}").rearrange("p (k t) -> p k t", k=4)).then_inc(f["turned_x"].sem, 1)
                else:
                    act.wait_ge(*once["top_diff"].by(0))
                    nc.scalar.activation(top_gate[:, :, 0:1], top_gate[:, :, 1:2], ACT.Exp).then_inc(once["top_exp"].sem, 1)
                    with act.Fori(0, EXPERTS // 2) as couple:
                        for e in range(2):
                            silus(moe, couple * 2 + e, EXPERT_STEPS)

            def square_rows(sig, l, n):
                for h in range(HALVES):
                    nc.scalar.activation(xn[:, h], X[:, h], ACT.Square, scale=D ** -0.5, accum_out=sq[:, h:h + 1]).then_inc(sig["sq"].sem, 1)

            act.wait_ge(*f["x"].by(1))
            with act.Fori(0, LAYERS) as l:
                J = JOBS2

                def column(name, k):
                    return cols2[:, bass.ds(l * N_COLS2 + COLS2[name] + k, 1)]

                def turn_in(name, gain, n):
                    act.wait_ge(*s["full"].by(l, J[f"{name}_turn0"] + 1))
                    for k in range(4):
                        nc.scalar.activation(xT[:, k, :], pair(J, f"{name}_turn0")[:, k * SEQ:(k + 1) * SEQ], ACT.Copy,
                                             scale=column(gain, k)).then_inc(s["turned_act"].sem, 1)

                square_rows(s, l, 0)
                turn_in("ffn1", "ffn1", 0)
                silus(ffn1, l, FFN_STEPS)
                act.wait_ge(*ffn1["taken"].by(l))
                square_rows(s, l, 1)
                turn_in("mix", "mix", 1)
                act.wait_ge(*s["full"].by(l, J["a_v"] + 1))
                nc.scalar.activation(v2, banks(J, "a_v"), ACT.Gelu_apprx_tanh).then_inc(s["av"].sem, 1)
                act.wait_ge(*s["av"].by(l))
                for h in range(HALVES):
                    nc.scalar.activation(T[:, h, 0:2].rearrange("p m k -> p (m k)")[:, 0:512], v2[:, h], ACT.Square, scale=512 ** -0.5,
                                         accum_out=sq[:, 4 + h:5 + h]).then_inc(s["av_sq"].sem, 1)
                act.wait_ge(*s["full"].by(l, J["a_u"] + 1))
                nc.scalar.activation(uT, pair(J, "a_u").rearrange("p (k t) -> p k t", k=4), ACT.Gelu_apprx_tanh).then_inc(s["uT"].sem, 1)
                for name, place, sig in (("b_q", bqT, "bq"), ("c_q", c_qT, "cq"), ("c_k", c_kT, "ck")):
                    act.wait_ge(*s["full"].by(l, J[name] + 1))
                    nc.scalar.copy(place, pair(J, name).rearrange("p (k t) -> p k t", k=4)).then_inc(s[sig].sem, 1)
                for i in range(2):
                    act.wait_ge(*s["full"].by(l, J[f"c_v{i}"] + 1))
                    nc.scalar.copy(cv[:, :, 512 * i:512 * i + 512], banks(J, f"c_v{i}")).then_inc(s["cv"].sem, 1)
                for i in range(HEADS // 2 + 2):
                    if i < HEADS // 2:
                        exps(s, l, i, i % 2, SWA_DIM ** -0.5)
                        act.wait_ge(*s["sink_diff"].by(l, i + 1))
                        nc.scalar.activation(attv[:, i, SINK], attv[:, i, SINK], ACT.Exp).then_inc(s["sink_exp"].sem, 1)
                    if 0 <= i - 1 < HEADS // 2:
                        h = i - 1
                        act.wait_ge(*s["full"].by(l, J[f"swa_turn{h}"] + 1))
                        nc.scalar.copy(PT[:, h % 2], banks(J, f"swa_turn{h}")[:, :, 0:MAP]).then_inc(s["turned"].sem, 1)
                    if 0 <= i - 2 < HEADS // 2:
                        h = i - 2
                        act.wait_ge(*s["full"].by(l, J[f"swa_values{h}"] + 1))
                        nc.scalar.copy(ybT[:, h, :], pair(J, f"swa_values{h}")[:, 0:SEQ]).then_inc(s["values"].sem, 1)
                for i in range(2):
                    act.wait_ge(*s["full"].by(l, J[f"c_g{i}"] + 1))
                    nc.scalar.activation(cg[:, :, 512 * i:512 * i + 512], banks(J, f"c_g{i}"), ACT.Silu).then_inc(s["cg"].sem, 1)
                act.wait_ge(*s["full"].by(l, J["c_state"] + 1))
                nc.scalar.copy(state, pair(J, "c_state").rearrange("p (h e) -> p h e", h=C_HEADS)).then_inc(s["state"].sem, 1)
                for n, branch in enumerate("abc"):
                    if branch == "c":
                        act.wait_ge(*s["mT"].by(l, 2))
                    for i in range(2):
                        name = f"gate_{branch}{i}"
                        act.wait_ge(*s["full"].by(l, J[name] + 1))
                        for t in range(4):
                            nc.scalar.activation(gate2[branch][:, 4 * i + t, :], pair(J, name)[:, t * SEQ:(t + 1) * SEQ], ACT.Sigmoid,
                                                 bias=column("b_gate", KT * n + 4 * i + t)).then_inc(s["gate"].sem, 1)
                for i in range(2):
                    act.wait_ge(*s["full"].by(l, J[f"c_turn{i}"] + 1))
                    for t in range(4):
                        nc.scalar.activation(ycT[:, 4 * i + t, :], pair(J, f"c_turn{i}")[:, t * SEQ:(t + 1) * SEQ], ACT.Copy,
                                             scale=column("ret", 4 * i + t)).then_inc(s["ycT"].sem, 1)
                act.wait_ge(*s["mix"].by(l))
                square_rows(s, l, 2)
                turn_in("ffn2", "ffn2", 2)
                silus(ffn2, l, FFN_STEPS)
                act.wait_ge(*ffn2["taken"].by(l))
            square_rows(once, 0, 0)

        @block.vector
        def _(dve):
            v = nc.vector

            def score_max(sig, l, i, b, name, jobs, biased):
                dve.wait_ge(*sig["full"].by(l, jobs[name] + 1))
                if i >= 2:
                    dve.wait_ge(*sig["turned"].by(l, i - 1))
                for m in range(2):
                    biased(T[:, b, m], banks(jobs, name)[:, m, 0:MAP], m).then_inc(sig["biased"].sem, 1)
                dve.wait_ge(*sig["biased"].by(l, 2 * i + 2))
                for q, (lo, hi) in enumerate(((0, P), (P, MAP))):
                    v.tensor_reduce(attv[:, i, MAXS, :, q], T[:, b, :, lo:hi], AX, ALU.max).then_inc(sig["maxed"].sem, 1)
                dve.wait_ge(*sig["maxed"].by(l, 2 * i + 2))

            def divide(sig, l, i, b):
                dve.wait_ge(*sig["inverse"].by(l, i + 1))
                for m in range(2):
                    for q, (lo, hi) in enumerate(((0, P), (P, MAP))):
                        v.tensor_scalar(T[:, b, m, lo:hi], T[:, b, m, lo:hi], attv[:, i, INV, m, q:q + 1], None, ALU.mult).then_inc(sig["weighed"].sem, 1)

            def gated_tiles(sig, l, steps, c0, turns):
                def tile(step, parity, i, guarded=True):
                    dve.wait_ge(*sig["silu"].by(l, 2 * step + i + 1))
                    if guarded:
                        dve.wait_ge(unit_used, c0 - 1 + step + SLOTS * turns)
                    v.tensor_tensor(hT[:, 2 * parity + i, :], sil[:, i, :], psum[:, 2 * parity + i, SEQ:2 * SEQ], ALU.mult).then_inc(sig["gated"].sem, 1)
                for step in range(2):
                    for i in range(2):
                        tile(step, step, i, guarded=False)
                with dve.Fori(1, steps // 2) as g:
                    for parity in range(2):
                        for i in range(2):
                            tile(2 * g + parity, parity, i)
                if steps % 2:
                    for i in range(2):
                        tile(steps - 1, 0, i)
                dve.wait_ge(unit_used, c0 + steps + SLOTS * turns)

            dve.wait_ge(start_loaded, 16 * START_LOADS)
            v.tensor_copy(pos, positions).then_inc(once["setup"].sem, 1)
            v.tensor_tensor(lambdas[:, :, 0, :], lambdas[:, :, 0, :], lambdas[:, :, 1, :], ALU.mult).then_inc(once["setup"].sem, 1)
            dve.wait_ge(once["setup"].sem, 2)
            v.tensor_reduce(lam_work[:, 0:2 * LAYERS], lambdas[:, :, 0, :], AX, ALU.add).then_inc(once["lam_sum"].sem, 1)
            dve.wait_ge(*once["lam_exp"].by(0))
            powers = lam_work[:, 4:4 + 2 * LAYERS].rearrange("p (l w) -> p l w", w=2)
            v.tensor_tensor(neg_lambda, powers[:, :, 1], powers[:, :, 0], ALU.subtract).then_inc(once["setup"].sem, 1)
            dve.wait_ge(once["setup"].sem, 3)
            for l in range(LAYERS):
                v.tensor_scalar(neg_lambda[:, l:l + 1], neg_lambda[:, l:l + 1], -LAM_INIT[l], None, ALU.add).then_inc(once["setup"].sem, 1)
            for h in range(HALVES):
                v.tensor_scalar(angle[:, 0, h], inv_freq, pos[:, SEQ + h:SEQ + h + 1], None, ALU.mult).then_inc(once["setup"].sem, 1)
            dve.wait_ge(once["setup"].sem, 7)
            for q in range(2):
                v.tensor_scalar(angle[:, 1 + q], angle[:, 0], 0.5 / math.pi, 0.25 * q, ALU.mult, ALU.add).then_inc(once["setup"].sem, 1)
            dve.wait_ge(once["setup"].sem, 9)
            for sign in (MAGIC, -MAGIC):
                v.tensor_scalar(angle[:, 1:3], angle[:, 1:3], sign, None, ALU.add).then_inc(once["setup"].sem, 1)
                dve.wait_ge(once["setup"].sem, 10 + (sign < 0))
            for part, term in enumerate(TWO_PI):
                for q in range(2):
                    v.scalar_tensor_tensor(out=angle[:, 3 + q], in0=angle[:, 1 + q], scalar=-term,
                                              in1=angle[:, 3 + q] if part else angle[:, 0], op0=ALU.mult, op1=ALU.add).then_inc(once["setup"].sem, 1)
                dve.wait_ge(once["setup"].sem, 13 + 2 * part)
            v.tensor_scalar(angle[:, 4], angle[:, 4], 0.5 * math.pi, None, ALU.add).then_inc(once["setup"].sem, 1)
            dve.wait_ge(once["setup"].sem, 18)
            v.tensor_scalar(angle[:, 3:5], angle[:, 3:5], PI_DOWN, -PI_DOWN, ALU.min, ALU.max).then_inc(once["angles"].sem, 1)
            for h in range(HALVES):
                lo, hi = (0, P) if h == 0 else (P, MAP)
                v.tensor_scalar(neg_dist[:, lo:hi], pos[:, 0:hi - lo], pos[:, SEQ + h:SEQ + h + 1], 0.0, ALU.subtract, ALU.min).then_inc(once["setup"].sem, 1)
            v.tensor_tensor(delta[:, 0:(BUCKETS - 1) * HEADS], table_rows[:, HEADS:], table_rows[:, 0:(BUCKETS - 1) * HEADS], ALU.subtract).then_inc(once["setup"].sem, 1)
            for h in range(HEADS):
                v.tensor_scalar(bias[:, h], causal, table_rows[:, h:h + 1], None, ALU.add).then_inc(once["bias"].sem, 1)
            dve.wait_ge(once["setup"].sem, 21)

            def add_buckets(first, last):
                with dve.Fori(first, last) as b:
                    dve.wait_ge(*once["bias"].by(0, b * HEADS + HEADS))
                    v.tensor_scalar(at_least, neg_dist, thresholds[:, bass.ds(b, 1)], None, ALU.is_le).then_inc(once["ind"].sem, 1)
                    dve.wait_ge(*once["ind"].by(0, b + 1))
                    for h in range(HEADS):
                        v.scalar_tensor_tensor(out=bias[:, h], in0=at_least, scalar=delta[:, bass.ds(b * HEADS + h, 1)],
                                                      in1=bias[:, h], op0=ALU.mult, op1=ALU.add).then_inc(once["bias"].sem, 1)

            for l in range(LAYERS):
                J = JOBS1

                def rotate(x1, x2, y1, y2, h, tmp, base, rotated):
                    if h:
                        dve.wait_ge(*f[rotated].by(l, 2))
                    for n, (x, t) in enumerate(((x1, 1), (x2, 0), (x1, 0), (x2, 1))):
                        t_ = trig[:, t, h].unsqueeze(1).broadcast_to([P, HEADS, HALF_ROPE])
                        v.tensor_tensor(rope_tmp[:, n], x, t_, ALU.mult).then_inc(f[tmp].sem, 1)
                    dve.wait_ge(*f[tmp].by(l, base + 4))
                    return ((y1, rope_tmp[:, 0], rope_tmp[:, 1], ALU.subtract), (y2, rope_tmp[:, 2], rope_tmp[:, 3], ALU.add))

                dve.wait_ge(*f["latent_rs"].by(l))
                for n, (lo, hi) in enumerate(((0, Q_RANK), (Q_RANK, Q_RANK + KV_RANK))):
                    for h in range(HALVES):
                        v.tensor_scalar(latent[:, h, lo:hi], latent[:, h, lo:hi], rs[:, 2 * n + h:2 * n + h + 1], None, ALU.mult).then_inc(f["latent_n"].sem, 1)
                dve.wait_ge(*once["trig"].by(0))
                for h in range(HALVES):
                    lo = Q_RANK + KV_RANK
                    x1, x2 = (latent[:, h, lo + i:lo + i + HALF_ROPE].unsqueeze(1).broadcast_to([P, HEADS, HALF_ROPE]) for i in (0, HALF_ROPE))
                    y1, y2 = (kcat[:, h, :, NOPE + i:NOPE + i + HALF_ROPE] for i in (0, HALF_ROPE))
                    for y, t0_, t1_, op in rotate(x1, x2, y1, y2, h, "kr_tmp", 4 * h, "kcat"):
                        v.tensor_tensor(y, t0_, t1_, op).then_inc(f["kcat"].sem, 1)
                if l == 0:
                    add_buckets(0, 12)
                dve.wait_ge(*f["full"].by(l, J["cq_turn"] + 1))
                for k in range(3):
                    col = l * N_COLS1 + COLS1["q_norm"] + k
                    v.tensor_scalar(cqT[:, k, :], pair(J, "cq_turn")[:, k * SEQ:(k + 1) * SEQ], cols1[:, col:col + 1], None, ALU.mult).then_inc(f["cqT"].sem, 1)
                dve.wait_ge(*f["full"].by(l, J["ckv_turn"] + 1))
                for k in range(2):
                    col = l * N_COLS1 + COLS1["kv_norm"] + k
                    v.tensor_scalar(ckvT[:, k, :], pair(J, "ckv_turn")[:, k * SEQ:(k + 1) * SEQ], cols1[:, col:col + 1], None, ALU.mult).then_inc(f["ckvT"].sem, 1)
                dve.wait_ge(*f["kcat"].by(l))
                for h in range(HALVES):
                    dve.wait_ge(*f["q_rows"].by(l, h + 1))
                    x1, x2 = (qrow[:, h, :, NOPE + i:NOPE + i + HALF_ROPE] for i in (0, HALF_ROPE))
                    for y, t0_, t1_, op in rotate(x1, x2, x1, x2, h, "q_tmp", 4 * h, "q_rot"):
                        v.tensor_tensor(y, t0_, t1_, op).then_inc(f["q_rot"].sem, 1)
                if l == 0:
                    add_buckets(12, BUCKETS - 1)
                    dve.wait_ge(*once["bias"].by(0))

                def weigh_diff(h):
                    dve.wait_ge(*f["exped"].by(l, 4 * h + 4))
                    v.reciprocal(attv[:, h, INV], attv[:, h, SUMS]).then_inc(f["inverse"].sem, 1)
                    dve.wait_ge(*f["inverse"].by(l, h + 1))
                    v.tensor_scalar(attv[:, h, INV, 1], attv[:, h, INV, 1], neg_lambda[:, l:l + 1], None, ALU.mult).then_inc(f["lam_weight"].sem, 1)
                    for q, (lo, hi) in enumerate(((0, P), (P, MAP))):
                        v.tensor_scalar(T[:, h % 2, 0, lo:hi], T[:, h % 2, 0, lo:hi], attv[:, h, INV, 0, q:q + 1], None, ALU.mult).then_inc(f["weighed"].sem, 1)
                    dve.wait_ge(*f["lam_weight"].by(l, h + 1))
                    dve.wait_ge(*f["weighed"].by(l, 4 * h + 2))
                    for q, (lo, hi) in enumerate(((0, P), (P, MAP))):
                        v.scalar_tensor_tensor(out=T[:, h % 2, 0, lo:hi], in0=T[:, h % 2, 1, lo:hi], scalar=attv[:, h, INV, 1, q:q + 1],
                                                      in1=T[:, h % 2, 0, lo:hi], op0=ALU.mult, op1=ALU.add).then_inc(f["weighed"].sem, 1)

                for i in range(HEADS + 1):
                    if i < HEADS:
                        score_max(f, l, i, i % 2, f"diff_scores{i}", J, lambda o, x, m: v.scalar_tensor_tensor(
                            out=o, in0=x, scalar=64 ** -0.5, in1=bias[:, i], op0=ALU.mult, op1=ALU.add))
                        v.tensor_scalar(attv[:, i, NEGM], attv[:, i, MAXS], -1.0, None, ALU.mult).then_inc(f["negated"].sem, 1)
                    if i >= 1:
                        weigh_diff(i - 1)
                for i in range(HEADS // 2 + 1):
                    if i < HEADS // 2:
                        score_max(f, l, HEADS + i, i % 2, f"mla_scores{i}", J, lambda o, x, m: v.scalar_tensor_tensor(
                            out=o, in0=x, scalar=MLA_QK ** -0.5, in1=causal, op0=ALU.mult, op1=ALU.add))
                        v.tensor_scalar(attv[:, HEADS + i, NEGM], attv[:, HEADS + i, MAXS], -1.0, None, ALU.mult).then_inc(f["negated"].sem, 1)
                    if i >= 1:
                        h = HEADS + i - 1
                        dve.wait_ge(*f["exped"].by(l, 4 * h + 4))
                        v.reciprocal(attv[:, h, INV], attv[:, h, SUMS]).then_inc(f["inverse"].sem, 1)
                        divide(f, l, h, (i - 1) % 2)

                dve.wait_ge(*f["values"].by(l))
                heads = xn.rearrange("p h (n c) -> p h n c", n=HEADS)
                for h in range(HALVES):
                    v.scalar_tensor_tensor(out=squares[:, h], in0=xn[:, h], scalar=1.0 / P, in1=xn[:, h], op0=ALU.mult, op1=ALU.mult).then_inc(f["o_sq"].sem, 1)
                dve.wait_ge(*f["o_sq"].by(l))
                for h in range(HALVES):
                    v.tensor_reduce(sq[:, HEADS * h:HEADS * h + HEADS], squares[:, h].rearrange("p (n c) -> p n c", n=HEADS), AX, ALU.add).then_inc(f["o_sum"].sem, 1)
                dve.wait_ge(*f["o_rs"].by(l))
                for h in range(HALVES):
                    v.tensor_tensor(heads[:, h], heads[:, h], rs[:, HEADS * h:HEADS * h + HEADS].unsqueeze(2).broadcast_to([P, HEADS, P]), ALU.mult).then_inc(f["o_n"].sem, 1)
                col = l * N_COLS1 + COLS1["subln"]
                for i in range(2):
                    dve.wait_ge(*f["full"].by(l, J[f"o_turn{i}"] + 1))
                    v.tensor_scalar(oT[:, 4 * i:4 * i + 4, :], pair(J, f"o_turn{i}").rearrange("p (k t) -> p k t", k=4),
                                           cols1[:, col:col + 1], 1.0 - LAM_INIT[l], ALU.mult, ALU.mult).then_inc(f["oT"].sem, 1)
                for i in range(2):
                    dve.wait_ge(*f["full"].by(l, J[f"branch_a{i}"] + 1))
                    dve.wait_ge(*f["gate"].by(l, 4 * i + 4))
                    v.tensor_tensor(m1T[:, 4 * i:4 * i + 4, :], pair(J, f"branch_a{i}").rearrange("p (k t) -> p k t", k=4),
                                           gate1[:, 0, 4 * i:4 * i + 4, :], ALU.mult).then_inc(f["mT"].sem, 1)
                for i in range(2):
                    dve.wait_ge(*f["full"].by(l, J[f"branch_b{i}"] + 1))
                    dve.wait_ge(*f["gate"].by(l, 12 + 4 * i))
                    g = gate1[:, 1, 4 * i:4 * i + 4, :]
                    v.tensor_tensor(g, pair(J, f"branch_b{i}").rearrange("p (k t) -> p k t", k=4), g, ALU.mult).then_inc(f["m_tmp"].sem, 1)
                    dve.wait_ge(*f["m_tmp"].by(l, i + 1))
                    dve.wait_ge(*f["mT"].by(l, i + 1))
                    m = m1T[:, 4 * i:4 * i + 4, :]
                    v.tensor_tensor(m, m, g, ALU.add).then_inc(f["mT"].sem, 1)
                for i in range(2):
                    dve.wait_ge(*f["full"].by(l, J[f"mix{i}"] + 1))
                    part = slice(512 * i, 512 * i + 512)
                    v.scalar_tensor_tensor(out=R[:, :, part], in0=X[:, :, part], scalar=ALPHA, in1=banks(J, f"mix{i}"),
                                                  op0=ALU.mult, op1=ALU.add).then_inc(f["mix"].sem, 1)
                dve.wait_ge(*f["mix"].by(l))

                def layernorm(n):
                    for h in range(HALVES):
                        for j in range(2):
                            v.bn_stats(bn[:, 2 * h + j, :], R[:, h, 512 * j:512 * j + 512]).then_inc(f["ln_stats"].sem, 1)
                    dve.wait_ge(*f["ln_stats"].by(l, 4 * n + 4))
                    for h in range(HALVES):
                        v.bn_aggr(mean_var[:, h], bn[:, 2 * h:2 * h + 2, :]).then_inc(f["ln_aggr"].sem, 1)
                    dve.wait_ge(*f["ln_rs"].by(l, n + 1))
                    for h in range(HALVES):
                        v.tensor_scalar(xn[:, h], R[:, h], mean_var[:, h, 0:1], rs[:, h:h + 1], ALU.subtract, ALU.mult).then_inc(f["ln_n"].sem, 1)
                    dve.wait_ge(*f["ln_n"].by(l, 2 * n + 2))
                    dve.wait_ge(*f["norm_rows"].by(l, 16 * (n + 1)))
                    v.tensor_tensor(xn, xn, norm_rows[:, 0:1, :].broadcast_to([P, HALVES, D]), ALU.mult).then_inc(f["ln_g"].sem, 1)
                    dve.wait_ge(*f["ln_g"].by(l, n + 1))
                    v.tensor_tensor(X, xn, norm_rows[:, 1:2, :].broadcast_to([P, HALVES, D]), ALU.add).then_inc(f["x"].sem, 1)
                    dve.wait_ge(*f["x"].by(l, n + 1))

                layernorm(0)
                for i in range(2):
                    dve.wait_ge(*f["full"].by(l, J[f"ple_proj{i}"] + 1))
                    dve.wait_ge(*f["ple_sig"].by(l, i + 1))
                    e = E[:, :, 512 * i:512 * i + 512]
                    v.tensor_tensor(e, banks(J, f"ple_proj{i}"), e, ALU.mult).then_inc(f["ple_e"].sem, 1)
                dve.wait_ge(*f["ple_e"].by(l))
                v.scalar_tensor_tensor(out=R, in0=X, scalar=ALPHA, in1=E, op0=ALU.mult, op1=ALU.add).then_inc(f["residual"].sem, 1)
                dve.wait_ge(*f["residual"].by(l))
                if l == 0:
                    gated_tiles(dense, 0, DENSE_STEPS, DENSE_START, 0)
                    for h in range(HALVES):
                        for n in range(2):
                            part = R[:, h, 512 * n:512 * n + 512]
                            v.tensor_tensor(part, psum[:, 4 + 2 * h + n], part, ALU.add).then_inc(dense["taken"].sem, 1)
                    dve.wait_ge(*dense["taken"].by(0))
                else:
                    dve.wait_ge(*once["routed"].by(0))
                    v.tensor_copy(logit, psum[:, 6, 0:HALVES * EXPERTS].rearrange("p (h e) -> p h e", h=HALVES)).then_inc(once["logits"].sem, 1)
                    dve.wait_ge(*once["logits"].by(0))
                    for h in range(HALVES):
                        v.max(tops[:, h], logit[:, h]).then_inc(once["tops"].sem, 1)
                    dve.wait_ge(*once["tops"].by(0, 2))
                    for h in range(HALVES):
                        v.max_index(top_idx[:, h * 8:h * 8 + 8], tops[:, h], logit[:, h]).then_inc(once["tops"].sem, 1)
                    v.tensor_tensor(top_gate[:, :, 1:2], tops[:, :, 1:2], tops[:, :, 0:1], ALU.subtract).then_inc(once["top_diff"].sem, 1)
                    dve.wait_ge(*once["tops"].by(0))
                    dve.wait_ge(*once["top_exp"].by(0))
                    v.tensor_copy(top_gate[:, :, 4:6], top_idx[:].rearrange("p (h e) -> p h e", h=HALVES)[:, :, 0:2]).then_inc(once["pick"].sem, 1)
                    v.tensor_scalar(top_gate[:, :, 1:2], top_gate[:, :, 0:1], 1.0, None, ALU.add).then_inc(once["pick"].sem, 1)
                    dve.wait_ge(*once["pick"].by(0, 2))
                    v.reciprocal(top_gate[:, :, 2:3], top_gate[:, :, 1:2]).then_inc(once["pick"].sem, 1)
                    dve.wait_ge(*once["pick"].by(0, 3))
                    v.tensor_tensor(top_gate[:, :, 3:4], top_gate[:, :, 0:1], top_gate[:, :, 2:3], ALU.mult).then_inc(once["pick"].sem, 1)
                    dve.wait_ge(*once["pick"].by(0, 4))
                    iota = router[:, KT * EXPERTS:]
                    for h in range(HALVES):
                        for which, o in ((0, pick[:, h]), (1, logit[:, h])):
                            v.tensor_scalar(o, iota, top_gate[:, h, 4 + which:5 + which], top_gate[:, h, 2 + which:3 + which],
                                                   ALU.is_equal, ALU.mult).then_inc(once["pick"].sem, 1)
                    dve.wait_ge(*once["pick"].by(0, 8))
                    v.tensor_tensor(pick, pick, logit, ALU.add).then_inc(once["pick"].sem, 1)
                    dve.wait_ge(*once["pick"].by(0))
                    with dve.Fori(0, EXPERTS // 2) as couple:
                        for e in range(2):
                            expert = couple * 2 + e
                            gated_tiles(moe, expert, EXPERT_STEPS, MOE_START + e * EXPERT_STEPS, couple * (2 * EXPERT_STEPS // SLOTS))
                            for h in range(HALVES):
                                for n in range(2):
                                    part = R[:, h, 512 * n:512 * n + 512]
                                    v.scalar_tensor_tensor(out=part, in0=psum[:, 4 + 2 * h + n], scalar=pick[:, h, bass.ds(expert, 1)],
                                                                  in1=part, op0=ALU.mult, op1=ALU.add).then_inc(moe["taken"].sem, 1)
                            dve.wait_ge(*moe["taken"].by(expert))
                layernorm(1)

            dve.wait_ge(*once["tables_loaded"].by(0))
            v.tensor_scalar(neg_sinks, neg_sinks, -1.0, None, ALU.mult).then_inc(once["sinks"].sem, 1)
            dve.wait_ge(*once["sinks"].by(0))

            def norm_rows_of(sig, l, n):
                dve.wait_ge(*sig["rs"].by(l, n + 1))
                for h in range(HALVES):
                    v.tensor_scalar(xn[:, h], X[:, h], rs[:, h:h + 1], None, ALU.mult).then_inc(sig["n"].sem, 1)

            with dve.Fori(0, LAYERS) as l:
                J = JOBS2
                turns = l * (LAYER2 // SLOTS)

                def column(name, k):
                    return cols2[:, bass.ds(l * N_COLS2 + COLS2[name] + k, 1)]

                def turn_in(name, gain):
                    dve.wait_ge(*s["full"].by(l, J[f"{name}_turn1"] + 1))
                    for k in range(4):
                        v.tensor_scalar(xT[:, 4 + k, :], pair(J, f"{name}_turn1")[:, k * SEQ:(k + 1) * SEQ], column(gain, 4 + k), None, ALU.mult).then_inc(s["turned_dve"].sem, 1)

                def add_network(sig, c0):
                    gated_tiles(sig, l, FFN_STEPS, c0, turns)
                    for h in range(HALVES):
                        for n in range(2):
                            part = X[:, h, 512 * n:512 * n + 512]
                            v.scalar_tensor_tensor(out=part, in0=psum[:, 4 + 2 * h + n], scalar=0.5, in1=part, op0=ALU.mult, op1=ALU.add).then_inc(sig["taken"].sem, 1)
                    dve.wait_ge(*sig["taken"].by(l))

                norm_rows_of(s, l, 0)
                turn_in("ffn1", "ffn1")
                add_network(ffn1, BLOCK2)
                norm_rows_of(s, l, 1)
                turn_in("mix", "mix")
                dve.wait_ge(*s["av_rs"].by(l))
                for h in range(HALVES):
                    v.tensor_scalar(v2[:, h], v2[:, h], rs[:, 4 + h:5 + h], None, ALU.mult).then_inc(s["av_n"].sem, 1)
                dve.wait_ge(*s["full"].by(l, J["b_kv"] + 1))
                v.tensor_copy(bkT, banks(J, "b_kv")[:, 0].rearrange("p (n t) -> p n t", n=2)).then_inc(s["bkv"].sem, 1)
                v.tensor_copy(bv, banks(J, "b_kv")[:, 1, 0:SEQ].rearrange("p (h c) -> p h c", h=2)).then_inc(s["bkv"].sem, 1)
                dve.wait_ge(*s["cq"].by(l))
                v.tensor_tensor(c_qw, c_qT[:, :, P:SEQ], q_decay, ALU.mult).then_inc(s["cqw"].sem, 1)
                dve.wait_ge(*s["full"].by(l, J["c_krow"] + 1))
                v.tensor_tensor(c_kw, pair(J, "c_krow")[:, 0:512].rearrange("p (h d) -> p h d", h=C_HEADS),
                                       k_decay.unsqueeze(2).broadcast_to([P, C_HEADS, P]), ALU.mult).then_inc(s["ckw"].sem, 1)
                dve.wait_ge(*s["full"].by(l, J["a_mix"] + 1))
                for g in range(A_GROUPS):
                    v.scalar_tensor_tensor(out=yaT[:, g].rearrange("p (h t) -> p h t", h=2),
                                                  in0=pair(J, "a_mix")[:, g * SEQ:(g + 1) * SEQ].rearrange("p (h t) -> p h t", h=2),
                                                  scalar=column("v_norm", g), in1=bs[:, g:g + 1, :].broadcast_to([P, 2, P]),
                                                  op0=ALU.mult, op1=ALU.add).then_inc(s["ya_tmp"].sem, 1)
                dve.wait_ge(*s["ya_tmp"].by(l))
                dve.wait_ge(*s["uT"].by(l))
                v.tensor_tensor(yaT, yaT, uT, ALU.mult).then_inc(s["yaT"].sem, 1)
                for i in range(HEADS // 2 + 1):
                    if i < HEADS // 2:
                        score_max(s, l, i, i % 2, f"swa_scores{i}", J, lambda o, x, m: v.scalar_tensor_tensor(
                            out=o, in0=swa_dist, scalar=-(2.0 ** -(2 * i + m + 1)) * SWA_DIM ** 0.5, in1=x, op0=ALU.mult, op1=ALU.add))
                        negs = neg_sinks[:, bass.ds(l * 2 * HEADS + 4 * i, 4)].rearrange("p (m b) -> p m b", m=2)
                        v.scalar_tensor_tensor(out=attv[:, i, NEGM], in0=attv[:, i, MAXS], scalar=-SWA_DIM ** -0.5, in1=negs,
                                                      op0=ALU.mult, op1=ALU.min).then_inc(s["negated"].sem, 1)
                        dve.wait_ge(*s["negated"].by(l, i + 1))
                        v.tensor_tensor(attv[:, i, SINK], attv[:, i, NEGM], negs, ALU.subtract).then_inc(s["sink_diff"].sem, 1)
                    if i >= 1:
                        h = i - 1
                        dve.wait_ge(*s["exped"].by(l, 4 * h + 4))
                        dve.wait_ge(*s["sink_exp"].by(l, h + 1))
                        v.tensor_tensor(attv[:, h, SUMS], attv[:, h, SUMS], attv[:, h, SINK], ALU.add).then_inc(s["sink_added"].sem, 1)
                        dve.wait_ge(*s["sink_added"].by(l, h + 1))
                        v.reciprocal(attv[:, h, INV], attv[:, h, SUMS]).then_inc(s["inverse"].sem, 1)
                        divide(s, l, h, h % 2)
                dve.wait_ge(*s["full"].by(l, J["c_scores"] + 1))
                for h in range(C_HEADS):
                    v.tensor_tensor(scT[:, h].rearrange("p (c t) -> p c t", c=2), pair(J, "c_scores")[:, h * SEQ:(h + 1) * SEQ].rearrange("p (c t) -> p c t", c=2),
                                           decayT[:, h:h + 1, :].broadcast_to([P, 2, P]), ALU.mult).then_inc(s["scT"].sem, 1)
                for n in range(HALVES):
                    o = pair(J, f"c_out{n}").rearrange("p (h e) -> p h e", h=C_HEADS)
                    dve.wait_ge(*s["full"].by(l, J[f"c_out{n}"] + 1))
                    for h in range(C_HEADS):
                        v.bn_stats(bn[:, 4 + 4 * n + h, :], o[:, h]).then_inc(s["o_stats"].sem, 1)
                    dve.wait_ge(*once["sinks"].by(0))
                    dve.wait_ge(*s["o_stats"].by(l, 4 * n + 4))
                    for h in range(C_HEADS):
                        v.bn_aggr(mean_var[:, 4 + 4 * n + h], bn[:, 4 + 4 * n + h:5 + 4 * n + h, :]).then_inc(s["o_aggr"].sem, 1)
                    at = 8 + 4 * n
                    dve.wait_ge(*s["o_rs"].by(l, n + 1))
                    for h in range(C_HEADS):
                        v.tensor_scalar(xn[:, n, h * C_V:(h + 1) * C_V], o[:, h], mean_var[:, 4 + 4 * n + h, 0:1], rs[:, at + h:at + h + 1],
                                               ALU.subtract, ALU.mult).then_inc(s["o_n"].sem, 1)
                    dve.wait_ge(*s["o_n"].by(l, 4 * n + 4))
                    dve.wait_ge(*s["cg"].by(l))
                    v.tensor_tensor(xn[:, n], xn[:, n], cg[:, n], ALU.mult).then_inc(s["yc"].sem, 1)
                for n, branch in enumerate("abc"):
                    for i in range(2):
                        dve.wait_ge(*s["full"].by(l, J[f"branch_{branch}{i}"] + 1))
                        dve.wait_ge(*s["gate"].by(l, 8 * n + 4 * i + 4))
                        g = gate2[branch][:, 4 * i:4 * i + 4, :]
                        m = m2T[:, 4 * i:4 * i + 4, :]
                        o = pair(J, f"branch_{branch}{i}").rearrange("p (k t) -> p k t", k=4)
                        if n == 0:
                            v.tensor_tensor(m, o, g, ALU.mult).then_inc(s["mT"].sem, 1)
                        else:
                            v.tensor_tensor(g, o, g, ALU.mult).then_inc(s["m_tmp"].sem, 1)
                            dve.wait_ge(*s["m_tmp"].by(l, 2 * (n - 1) + i + 1))
                            dve.wait_ge(*s["mT"].by(l, 2 * (n - 1) + i + 1))
                            v.tensor_tensor(m, m, g, ALU.add).then_inc(s["mT"].sem, 1)
                for i in range(2):
                    dve.wait_ge(*s["full"].by(l, J[f"mix{i}"] + 1))
                    part = X[:, :, 512 * i:512 * i + 512]
                    v.tensor_tensor(part, banks(J, f"mix{i}"), part, ALU.add).then_inc(s["mix"].sem, 1)
                dve.wait_ge(*s["mix"].by(l))
                norm_rows_of(s, l, 2)
                turn_in("ffn2", "ffn2")
                add_network(ffn2, FFN2_START)

            norm_rows_of(once, 0, 0)
            dve.wait_ge(*once["n"].by(0))
            dve.wait_ge(*once["row_loaded"].by(0))
            for h in range(HALVES):
                v.tensor_tensor(xn[:, h], xn[:, h], last_row, ALU.mult).then_inc(once["g"].sem, 1)


def causal_map():
    q, k = np.arange(P)[:, None], np.arange(P)[None, :]
    own = np.where(k <= q, 0.0, NEG)
    return np.concatenate([own, np.zeros((P, P)), own], axis=1).astype(np.float32)


def window_map():
    q, k = np.arange(P)[:, None], np.arange(P)[None, :]
    own = np.where(k <= q, q - k, -NEG)
    before = np.where(q + P - k < P, q + P - k, -NEG)
    return np.concatenate([own, before, own], axis=1).astype(np.float32)


def retention_tables():
    log_gamma = np.log(1.0 - np.exp2(-5.0 - np.arange(C_HEADS, dtype=np.float32))).astype(np.float32)
    i = np.arange(P, dtype=np.float32)
    dist = i[None, :] - i[:, None]
    scale = P ** -0.5
    decay = np.where(dist[:, None, :] >= 0, np.exp(log_gamma[None, :, None] * np.maximum(dist, 0)[:, None, :]), 0.0) * scale
    queries = np.broadcast_to(np.exp(log_gamma[:, None] * (i + 1.0)[None, :]), (P, C_HEADS, P))
    keys = np.exp(log_gamma[None, :] * (P - 1.0 - i)[:, None]) * scale
    return [x.reshape(P, -1).astype(np.float32) for x in (decay, queries, keys)]


def tiles(w):
    k, n = w.shape
    return w.reshape(k // P, P, n).transpose(1, 0, 2).reshape(P, -1)


def column_blocks(w, width=512):
    return [tiles(w[:, i:i + width]) for i in range(0, w.shape[1], width)]


def network_units(w1, w3, w2):
    out = []
    for i in range(0, w1.shape[1], FF_STEP):
        out.append(np.concatenate([tiles(w1[:, i:i + FF_STEP]), tiles(w3[:, i:i + FF_STEP]), tiles(w2[i:i + FF_STEP])], axis=1))
    return out


def on_columns(vector):
    return vector.reshape(-1, P).T


def repeated(vector):
    return np.broadcast_to(np.asarray(vector).reshape(1, -1), (P, np.asarray(vector).size))


def arrange(i):
    x = i["x"][0]
    w_in, wide, latent1, uq, ukv = i["w_in"], [], [], [], []
    qkv = 3 * D
    for l in range(LAYERS):
        w = w_in[l]
        latent_cols = w[:, qkv:qkv + LATENT]
        gate = w[:, qkv + LATENT:]
        wide += [tiles(latent_cols[:, :512])] + column_blocks(w[:, :qkv])
        latent1.append(tiles(latent_cols[:, 512:]))
        uq.append(tiles(i["w_uq"][l]))
        ukv.append(tiles(i["w_ukv"][l]))
        wide += column_blocks(gate[:, :D]) + column_blocks(i["w_branch_diff"][l]) + column_blocks(gate[:, D:])
        wide += [tiles(i["w_branch_mla"][l])] + column_blocks(i["w_out"][l]) + column_blocks(i["w_ple_gate"][l])
    a = dict(
        xT=tiles(np.ascontiguousarray(x.T)), x_rows=tiles(x),
        first_wide=np.concatenate(wide), latent1=np.concatenate(latent1), w_uq=np.concatenate(uq), w_ukv=np.concatenate(ukv),
        ple_proj=np.concatenate([tiles(w) for w in i["w_ple_proj"]]),
        dense=np.concatenate(network_units(i["dense_w1"][0], i["dense_w3"][0], i["dense_w2"][0])),
        experts=np.concatenate([u for e in range(EXPERTS) for u in network_units(i["expert_w1"][0, e], i["expert_w3"][0, e], i["expert_w2"][0, e])]),
        pT=np.concatenate([tiles(np.ascontiguousarray(p[0].T)) for p in i["p"]]),
        ln_mix=np.concatenate([np.concatenate([repeated(i["ln_mix_g"][l]), repeated(i["ln_mix_b"][l])], axis=1) for l in range(LAYERS)]),
        ln_ffn=np.concatenate([np.concatenate([repeated(i["ln_ffn_g"][l]), repeated(i["ln_ffn_b"][l])], axis=1) for l in range(LAYERS)]),
        router=np.concatenate([tiles(i["router_w"][0]), repeated(np.arange(EXPERTS, dtype=np.float32))], axis=1),
        lambdas=np.concatenate([repeated(i[n][l]) for l in range(LAYERS) for n in ("lambda_q1", "lambda_k1", "lambda_q2", "lambda_k2")], axis=1),
        positions=np.concatenate([repeated(i["positions"][0]), on_columns(i["positions"][0])], axis=1),
        bias_tables=np.concatenate([repeated(i["rel_bias_table"]), repeated(np.array([-t for t in t5_thresholds()] + [0], np.float32))], axis=1),
        inv_freq=repeated(np.float32(10000.0) ** (-np.arange(HALF_ROPE, dtype=np.float32) / np.float32(HALF_ROPE))),
        columns_first=np.concatenate([on_columns(i[n][l]) for l in range(LAYERS) for n in ("b_gate", "diff_subln_g", "mla_q_norm_g", "mla_kv_norm_g")], axis=1),
        identity=np.eye(P, dtype=np.float32), causal=causal_map())

    wide, kv = [], []
    cuts = np.cumsum([512, 512, 512, 128, 128, 512, 512, 1024, 1024, 3072])[:-1]
    for l in range(LAYERS):
        a_u, a_v, b_q, b_k, b_v, c_q, c_k, c_v, c_g, gate = np.split(i["w_in_2"][l], cuts, axis=1)
        kv.append(tiles(np.concatenate([b_k, b_v], axis=1)))
        for w in (a_v, a_u, b_q, c_q, c_k, c_v, c_g, gate[:, :D]):
            wide += column_blocks(w)
        wide += [tiles(i["w_branch_a_2"][l])] + column_blocks(gate[:, D:2 * D]) + [tiles(i["w_branch_b_2"][l])]
        wide += column_blocks(gate[:, 2 * D:]) + column_blocks(i["w_branch_c_2"][l]) + column_blocks(i["w_out_2"][l])
    decay, queries, keys = retention_tables()
    a.update(
        second_wide=np.concatenate(wide), swa_kv=np.concatenate(kv),
        ffn1=np.concatenate([u for l in range(LAYERS) for u in network_units(i["ffn1_w_in_2"][l][:, :D_FF], i["ffn1_w_in_2"][l][:, D_FF:], i["ffn1_w_out_2"][l])]),
        ffn2=np.concatenate([u for l in range(LAYERS) for u in network_units(i["ffn2_w_in_2"][l][:, :D_FF], i["ffn2_w_in_2"][l][:, D_FF:], i["ffn2_w_out_2"][l])]),
        spatial_w=np.concatenate([np.ascontiguousarray(w.transpose(2, 0, 1)).reshape(P, -1) for w in i["gmlp_w_s_2"]]),
        spatial_b=np.concatenate([repeated(b) for b in i["gmlp_b_s_2"]]),
        columns_second=np.concatenate([on_columns(i[n][l]) for l in range(LAYERS) for n in ("ffn1_norm_2", "mix_norm_2", "b_gate_2", "gmlp_v_norm_2", "ret_gn_2", "ffn2_norm_2")], axis=1),
        tables2=np.concatenate([decay, queries, window_map(), keys, repeated(np.repeat(i["attn_sinks_2"].reshape(-1), 2))], axis=1),
        final_norm=repeated(i["final_norm_2"]))
    return {name: np.ascontiguousarray(array) for name, array in a.items()}


def kernel(**inputs):
    import concourse.bacc as bacc
    from concourse.bass_utils import run_bass_kernel_spmd

    arrays = arrange({name: np.asarray(value) for name, value in inputs.items()})
    nc = bacc.Bacc("TRN2", target_bir_lowering=False, num_devices=1)
    places = {name: nc.dram_tensor(f"in_{name}", x.shape, mybir.dt.from_np(x.dtype), kind="ExternalInput").ap() for name, x in arrays.items()}
    out = nc.dram_tensor("out", (SEQ, D), F32, kind="ExternalOutput").ap()
    build(nc, places, out)
    result = run_bass_kernel_spmd(nc, [{f"in_{name}": x for name, x in arrays.items()}], core_ids=[0])
    return result.results[0]["out"].reshape(1, SEQ, D)
```

```python
import math
from contextlib import ExitStack

import numpy as np

import concourse.bass as bass
from concourse import mybir

F32 = mybir.dt.float32
I32 = mybir.dt.int32
U32 = mybir.dt.uint32
ALU = mybir.AluOpType
ACT = mybir.ActivationFunctionType
AX = mybir.AxisListType.X

P = 128
SEQ = 256
HALVES = SEQ // P
D = 1024
KT = D // P
LAYERS = 2
ALPHA = (2.0 * LAYERS) ** 0.25
LN_EPS, RMS_EPS = 1e-5, 1e-6

HEADS = 8
DENSE_FF, EXPERT_FF, EXPERTS = 2816, 3584, 8
Q_RANK, KV_RANK, ROPE, NOPE, MLA_V = 384, 256, 32, 64, 64
HALF_ROPE = ROPE // 2
MLA_QK = NOPE + ROPE
LATENT = Q_RANK + KV_RANK + ROPE
BUCKETS, MAX_DIST = 32, 128
MAPS1 = HEADS + HEADS // 2
MAPS2 = HEADS // 2
DVE_HEADS = 7
LATENT_BUCKET = 9
QUERY_BUCKET = 25
LAM_INIT = [0.8 - 0.6 * math.exp(-0.3 * i) for i in range(LAYERS)]
MAGIC = 1.5 * 2.0 ** 23
TWO_PI = (6.28125, 0.0019350051879882812, 3.019916050561733e-07)
PI_DOWN = 3.1415925

D_FF = 2816
A_GROUPS = 4
C_HEADS, C_V = 4, 256
SWA_DIM = 64

FF_STEP = 256
UNIT = 3 * KT * FF_STEP
UP = 2 * KT * FF_STEP
GEMM = KT * 512
SLOTS = 4
DENSE_STEPS = DENSE_FF // FF_STEP
EXPERT_STEPS = EXPERT_FF // FF_STEP
FFN_STEPS = D_FF // FF_STEP
MIX1, PLE, MIX2 = 19, 3, 22
DENSE_START = MIX1 + PLE
MOE_START = DENSE_START + DENSE_STEPS + MIX1 + PLE
BLOCK2 = MOE_START + EXPERTS * EXPERT_STEPS
LAYER2 = 2 * FFN_STEPS + MIX2
FFN2_START = BLOCK2 + FFN_STEPS + MIX2
assert LAYER2 % SLOTS == 0 and 2 * EXPERT_STEPS % SLOTS == 0

MAP = P + 2 * P
NEG = -1e30
COLS1 = dict(b_gate=0, subln=16, q_norm=17, kv_norm=20)
COLS2 = dict(ffn1=0, mix=8, b_gate=16, v_norm=40, ret=44, ffn2=52)
N_COLS1, N_COLS2 = 22, 60
START_LOADS = 8


def t5_thresholds():
    n = np.arange(0, 4 * MAX_DIST)
    exact = BUCKETS // 2
    ratio = np.maximum(n, 1).astype(np.float32) / np.float32(exact)
    large = exact + (np.log(ratio) / np.float32(math.log(MAX_DIST / exact)) * np.float32(BUCKETS - exact)).astype(np.int32)
    bucket = np.where(n < exact, n, np.minimum(large, BUCKETS - 1))
    return [int(np.argmax(bucket >= b)) for b in range(1, BUCKETS)]


def order(*names):
    return {name: i for i, name in enumerate(names)}


def attention_order(maps):
    out = []
    for i in range(maps + 3):
        if i < maps:
            out.append(f"scores{i}")
        if 0 <= i - 2 < maps:
            out.append(f"turn{i - 2}")
        if 0 <= i - 3 < maps:
            out.append(f"values{i - 3}")
    return out


JOBS1 = order(
    "latent0", "latent1", "dq0", "dq1", "dk0", "dk1", "dv0", "dv1",
    "cq_turn", "ckv_turn", "uq0", "uq1", "ukv0", "ukv1", "q_turn0", "q_turn1", "k_turn0", "k_turn1",
    *attention_order(MAPS1),
    "gate_a0", "gate_a1", "o_turn0", "o_turn1", "branch_a0", "branch_a1",
    "gate_b0", "gate_b1", "branch_b0", "branch_b1", "mix0", "mix1",
    "ple_proj0", "ple_proj1", "x_turn0", "x_turn1", "ple_gate0", "ple_gate1",
    "end_turn0", "end_turn1")
JOBS2 = order(
    "ffn1_turn0", "ffn1_turn1", "mix_turn0", "mix_turn1",
    "a_v", "a_u", "b_q", "b_kv", "c_q", "c_k", "c_krow", "a_mix",
    "c_v0", "c_v1", *attention_order(MAPS2),
    "c_g0", "c_g1", "c_scores", "c_state", "c_out0", "c_out1",
    "gate_a0", "gate_a1", "branch_a0", "branch_a1",
    "gate_b0", "gate_b1", "branch_b0", "branch_b1",
    "gate_c0", "gate_c1", "c_turn0", "c_turn1", "branch_c0", "branch_c1",
    "mix0", "mix1", "ffn2_turn0", "ffn2_turn1")

FREED1 = dict(
    latent0=("latent", 1), latent1=("latent", 2), dq0=("dq", 1), dq1=("dq", 2), dk0=("dk", 1), dk1=("dk", 2),
    dv0=("dv", 1), dv1=("dv", 2), cq_turn=("cqT", 3), ckv_turn=("ckvT", 2), uq0=("q_rows", 1), uq1=("q_rows", 2),
    ukv0=("kv_rows", 2), ukv1=("kv_rows", 4), q_turn0=("qT", 1), q_turn1=("qT", 2), k_turn0=("kT", 1), k_turn1=("kT", 2),
    **{f"scores{i}": ("biased", 2 * i + 2) for i in range(MAPS1)},
    **{f"turn{i}": ("turned", i + 1) for i in range(MAPS1)},
    **{f"values{i}": ("values", i + 1) for i in range(MAPS1)},
    gate_a0=("gate", 4), gate_a1=("gate", 8), o_turn0=("oT", 1), o_turn1=("oT", 2),
    branch_a0=("mT", 1), branch_a1=("mT", 2), gate_b0=("gate", 12), gate_b1=("gate", 16),
    branch_b0=("m_tmp", 1), branch_b1=("m_tmp", 2), mix0=("mix", 1), mix1=("mix", 2),
    x_turn0=("turned_x", 1), x_turn1=("turned_x", 2), ple_gate0=("ple_sig", 1), ple_gate1=("ple_sig", 2),
    ple_proj0=("ple_rows", 1), ple_proj1=("ple_rows", 2), end_turn0=("turned_x", 3), end_turn1=("turned_x", 4))
FREED2 = dict(
    ffn1_turn0=("turned_act", 4), ffn1_turn1=("turned_dve", 4), mix_turn0=("turned_act", 8), mix_turn1=("turned_dve", 8),
    a_v=("av", 1), a_u=("uT", 1), b_q=("bq", 1), b_kv=("bkv", 2), c_q=("cq", 1), c_k=("ck", 1), c_krow=("ckw", 1),
    a_mix=("ya_tmp", 4), c_v0=("cv", 1), c_v1=("cv", 2),
    **{f"scores{i}": ("biased", 2 * i + 2) for i in range(MAPS2)},
    **{f"turn{i}": ("turned", i + 1) for i in range(MAPS2)},
    **{f"values{i}": ("values", i + 1) for i in range(MAPS2)},
    c_g0=("cg", 1), c_g1=("cg", 2), c_scores=("scT", 4), c_state=("state", 1), c_out0=("o_n", 4), c_out1=("o_n", 8),
    gate_a0=("gate", 4), gate_a1=("gate", 8), branch_a0=("mT", 1), branch_a1=("mT", 2),
    gate_b0=("gate", 12), gate_b1=("gate", 16), branch_b0=("m_tmp", 1), branch_b1=("m_tmp", 2),
    gate_c0=("gate", 20), gate_c1=("gate", 24), c_turn0=("ycT", 4), c_turn1=("ycT", 8),
    branch_c0=("m_tmp", 3), branch_c1=("m_tmp", 4), mix0=("mix", 1), mix1=("mix", 2),
    ffn2_turn0=("turned_act", 12), ffn2_turn1=("turned_dve", 12))


class Signal:

    def __init__(self, sem, per):
        self.sem, self.per = sem, per

    def by(self, layer, n=None):
        return self.sem, layer * self.per + (self.per if n is None else n)


class Signals:

    def __init__(self, new, prefix, **per):
        self.named = {name: Signal(new(prefix + name), n) for name, n in per.items()}

    def __getitem__(self, name):
        return self.named[name]


def build(nc, a, out):
    with ExitStack() as ctx:
        def sb(name, words, dtype=F32):
            return ctx.enter_context(nc.sbuf_tensor(name, [P, words], dtype))

        ring = sb("weight_ring", SLOTS * UNIT)
        arena = sb("arena", 99 * 256)
        x_rows = sb("x_rows", HALVES * D)
        ident = sb("identity", P)
        cols1 = sb("columns_first", LAYERS * N_COLS1)
        cols2 = sb("columns_second", LAYERS * N_COLS2)
        stat = sb("statistics", 256)
        consts = sb("constants", 3 * 2 * HEADS)
        att = sb("softmax_statistics", 12 * 20)
        routing = sb("routing", HALVES * EXPERTS * 8)
        busiest = sb("busiest_expert", 1, I32)
        top_idx = sb("top_experts", HALVES * 8, U32)
        psum = ctx.enter_context(nc.psum_tensor("psum", [P, 8, 512], F32))

        def view(kb, words, pattern=None, **sizes):
            v = arena[:, int(kb * 256):int(kb * 256) + words]
            return v.rearrange(pattern, **sizes) if pattern else v

        X = x_rows[:].rearrange("p (h d) -> p h d", h=HALVES)

        xT = view(0, KT * SEQ, "p (k t) -> p k t", k=KT)
        xn = view(8, HALVES * D, "p (h d) -> p h d", h=HALVES)
        T = view(16, 2 * 2 * MAP, "p (b m k) -> p b m k", b=2, m=2)
        PT = view(22, 2 * 2 * MAP, "p (b m k) -> p b m k", b=2, m=2)
        hT = view(16, 4 * SEQ, "p (n t) -> p n t", n=4)
        sil = view(20, 2 * SEQ, "p (n t) -> p n t", n=2)
        latent = view(16, HALVES * LATENT, "p (h c) -> p h c", h=HALVES)
        qrow = view(22, HALVES * HEADS * MLA_QK, "p (h n c) -> p h n c", h=HALVES, n=HEADS)
        kcat = view(8, HALVES * HEADS * MLA_QK, "p (h n c) -> p h n c", h=HALVES, n=HEADS)
        squares = view(16, HALVES * D, "p (h d) -> p h d", h=HALVES)
        bias = view(28, HEADS * MAP, "p (h k) -> p h k", h=HEADS)
        dqT = view(40, HEADS * SEQ, "p (h t) -> p h t", h=HEADS)
        dkT = view(48, HEADS * SEQ, "p (h t) -> p h t", h=HEADS)
        dv = view(56, HALVES * D, "p (h c) -> p h c", h=HALVES)
        qT = view(64, HEADS * SEQ, "p (h t) -> p h t", h=HEADS)
        kT = view(72, HEADS * SEQ, "p (h t) -> p h t", h=HEADS)
        cqT = view(80, 3 * SEQ, "p (k t) -> p k t", k=3)
        ckvT = view(83, 2 * SEQ, "p (k t) -> p k t", k=2)
        obT = view(80, 4 * SEQ, "p (k t) -> p k t", k=4)
        vrow = view(85, HALVES * HEADS * MLA_V, "p (h n c) -> p h n c", h=HALVES, n=HEADS)
        norm_rows = view(89, 2 * D, "p (n d) -> p n d", n=2)
        rope_tmp = view(74, 4 * HEADS * HALF_ROPE, "p (n h c) -> p n h c", n=4, h=HEADS)
        neg_dist = view(89, MAP)
        step_pool = view(92.25, MAP)
        at_least = view(90.5, MAP)
        delta = view(94, BUCKETS * HEADS)
        table_rows = view(95, BUCKETS * HEADS)
        thresholds = view(96, BUCKETS)
        causal = view(97, MAP)
        trig = view(98.5, HALVES * 2 * HALF_ROPE, "p (n h c) -> p n h c", n=2, h=HALVES)
        lambdas = view(64, LAYERS * 4 * 64, "p (n q c) -> p n q c", n=2 * LAYERS, q=2)
        positions = view(66, SEQ + HALVES).bitcast(I32)
        pos = view(68, SEQ + HALVES)
        inv_freq = view(70, HALF_ROPE)
        angle = view(71, 6 * HALVES * HALF_ROPE, "p (n h c) -> p n h c", n=6, h=HALVES)
        oT = view(40, KT * SEQ, "p (k t) -> p k t", k=KT)
        gate1 = view(64, 2 * KT * SEQ, "p (n k t) -> p n k t", n=2, k=KT)
        m1T = view(48, KT * SEQ, "p (k t) -> p k t", k=KT)
        R = view(40, HALVES * D, "p (h d) -> p h d", h=HALVES)
        E = view(64, HALVES * D, "p (h d) -> p h d", h=HALVES)
        pT = view(56, 2 * SEQ, "p (k t) -> p k t", k=2)
        router = view(60, KT * EXPERTS + EXPERTS + 3 * P)
        chosen = view(0, 2 * KT * P, "p (b k t) -> p b k t", b=2, k=KT)
        slots_hot = view(48, 2 * HALVES * P, "p (b h t) -> p b h t", b=2, h=HALVES)
        tokens_hot = view(50, HALVES * P, "p (h t) -> p h t", h=HALVES)
        expert_rows = view(51, D)
        v2 = view(28, HALVES * 512, "p (h c) -> p h c", h=HALVES)
        uT = view(32, 4 * SEQ, "p (k t) -> p k t", k=4)
        m2T = view(28, KT * SEQ, "p (k t) -> p k t", k=KT)
        yaT = view(36, 4 * SEQ, "p (k t) -> p k t", k=4)
        bqT = view(40, 4 * SEQ, "p (k t) -> p k t", k=4)
        bkT = view(44, 2 * SEQ, "p (n t) -> p n t", n=2)
        bv = view(46, HALVES * P, "p (h c) -> p h c", h=HALVES)
        ybT = view(47, 4 * SEQ, "p (k t) -> p k t", k=4)
        c_qT = view(51, C_HEADS * SEQ, "p (h t) -> p h t", h=C_HEADS)
        c_kT = view(55, C_HEADS * SEQ, "p (h t) -> p h t", h=C_HEADS)
        c_qw = view(59, C_HEADS * P, "p (h t) -> p h t", h=C_HEADS)
        c_kw = view(61, C_HEADS * P, "p (h t) -> p h t", h=C_HEADS)
        cv = view(63, HALVES * D, "p (h c) -> p h c", h=HALVES)
        cg = view(71, HALVES * D, "p (h c) -> p h c", h=HALVES)
        scT = view(79, C_HEADS * SEQ, "p (h t) -> p h t", h=C_HEADS)
        state = view(83, C_HEADS * C_V, "p (h e) -> p h e", h=C_HEADS)
        ycT = view(16, KT * SEQ, "p (k t) -> p k t", k=KT)
        wsT = view(87, A_GROUPS * P, "p (g t) -> p g t", g=A_GROUPS)
        bs = view(89, A_GROUPS * P, "p (g t) -> p g t", g=A_GROUPS)
        tables = view(91, 2 * C_HEADS * P + MAP + C_HEADS + LAYERS * 2 * HEADS)
        t0 = 91 + 2 * C_HEADS * P / 256
        decayT = view(91, C_HEADS * P, "p (h t) -> p h t", h=C_HEADS)
        q_decay = view(93, C_HEADS * P, "p (h t) -> p h t", h=C_HEADS)
        swa_dist = view(t0, MAP)
        k_decay = view(t0 + 1.5, C_HEADS)
        neg_sinks = view(t0 + 1.5 + C_HEADS / 256, LAYERS * 2 * HEADS)
        gate2 = dict(a=view(63, KT * SEQ, "p (k t) -> p k t", k=KT),
                     b=view(51, KT * SEQ, "p (k t) -> p k t", k=KT),
                     c=view(63, KT * SEQ, "p (k t) -> p k t", k=KT))
        last_row = view(28, D)

        MAXS, NEGM, SUMS, INV, SINK = range(5)
        attv = att[:].rearrange("p (n s m b) -> p n s m b", n=12, s=5, m=2)
        neg_lambda = stat[:, 0:LAYERS]
        lam_work = stat[:, 4:4 + 4 * LAYERS]
        sq = stat[:, 16:32]
        rs = stat[:, 32:48]
        mean_var = stat[:, 48:80].rearrange("p (n v) -> p n v", v=2)
        bn = stat[:, 80:176].rearrange("p (n s) -> p n s", s=6)
        logit = routing[:, 0:16].rearrange("p (h e) -> p h e", h=HALVES)
        tops = routing[:, 16:32].rearrange("p (h e) -> p h e", h=HALVES)
        pick = routing[:, 32:48].rearrange("p (h e) -> p h e", h=HALVES)
        mask = routing[:, 64:80].rearrange("p (h e) -> p h e", h=HALVES)
        mask2 = routing[:, 80:96].rearrange("p (h e) -> p h e", h=HALVES)
        slot_of = routing[:, 96:96 + HALVES * (EXPERTS + 1)].rearrange("p (h e) -> p h e", h=HALVES)
        top_gate = routing[:, 48:64].rearrange("p (h e) -> p h e", h=HALVES)

        def new(name):
            return ctx.enter_context(nc.semaphore(name))

        loaded = [new(f"slot{i}_loaded") for i in range(SLOTS)]
        unit_used = new("unit_used")
        start_loaded = new("start_loaded")
        x_loaded = new("x_loaded")
        once = Signals(new, "once_", consts=3, eps_added=1, setup=18, lam_sum=1, lam_exp=1, angles=1, trig=2, bias=DVE_HEADS * BUCKETS, ind=BUCKETS - 1, pool_bias=(HEADS - DVE_HEADS) * BUCKETS, pool_step=(HEADS - DVE_HEADS) * (BUCKETS - 1), distances=3,
                       tables_loaded=16, sinks=1, routed=1, logits=1, tops=4, top_diff=1, top_exp=1, pick=9, masked=5, ranked=1, slotted=3, counted=1,
                       row_loaded=16, sq=2, rs=1, n=2, g=2, stored=16)

        def attention(jobs):
            return dict(biased=2 * jobs, maxed=2 * jobs, negated=jobs, exped=4 * jobs, inverse=jobs,
                        weighed=4 * jobs, turned=jobs, values=jobs)

        f = Signals(new, "first_", full=len(JOBS1), eps_added=5, **attention(MAPS1), lam_weight=8,
                    latent=2, latent_sq=4, latent_rs=2, latent_n=4, cqT=3, ckvT=2, q_rows=2, kv_rows=4, kr_tmp=8,
                    kcat=4, q_tmp=8, q_rot=4, qT=2, kT=2, dq=2, dk=2, dv=2, o_sq=2, o_sum=2, o_rs=1, o_n=2, oT=2,
                    gate=16, m_tmp=2, mT=4, mix=2, ln_stats=8, ln_aggr=4, ln_rs=2, ln_n=4, x=4,
                    norm_rows=32, turned_x=4, ple_loaded=32, ple_rows=2, ple_sig=2, ple_e=2, residual=1)
        s = Signals(new, "second_", full=len(JOBS2), eps_added=6, **attention(MAPS2), sink_diff=4, sink_exp=4, sink_added=4,
                    params=32, sq=6, rs=3, n=6, turned_act=12, turned_dve=12, av=1, av_sq=2, av_rs=1, av_n=2, ws=1, uT=1,
                    ya_tmp=4, yaT=1, bq=1, bkv=2, cq=1, cqw=1, ck=1, ckw=1, cv=2, cg=2, scT=4, state=1,
                    o_stats=8, o_aggr=8, o_rs=2, o_n=8, yc=2, ycT=8, gate=24, m_tmp=4, mT=6, mix=2)

        def ffn_signals(prefix, steps):
            return Signals(new, prefix, hidden=2 * steps, silu=2 * steps, gated=2 * steps, taken=4)

        dense, moe = ffn_signals("dense_", DENSE_STEPS), ffn_signals("expert_", EXPERT_STEPS)
        route = Signals(new, "route_", hot=2, turned=1, hot_taken=1, gathered=1, columns=1, y_act=1, y_dve=1, scattered=2)
        ffn = ffn_signals("ffn_", FFN_STEPS)

        def slot(c, k_tiles, width):
            base = (c % SLOTS) * UNIT
            return ring[:, base:base + k_tiles * width].rearrange("p (k n) -> p k n", k=k_tiles)

        def landed(c, turns):
            return loaded[c % SLOTS], 16 * (c // SLOTS + 1) + 16 * turns

        def pair(jobs, name):
            b = 2 * (jobs[name] % 4)
            return psum[:, b:b + 2].rearrange("p b n -> p (b n)")

        def banks(jobs, name):
            b = 2 * (jobs[name] % 4)
            return psum[:, b:b + 2]

        block = ctx.enter_context(nc.Block())

        @block.sync
        def _(sp):
            def load(c, turns, source, words=GEMM):
                if not (isinstance(turns, int) and c + SLOTS * turns < SLOTS):
                    sp.wait_ge(unit_used, c - SLOTS + 1 + SLOTS * turns)
                base = (c % SLOTS) * UNIT
                sp.dma_start(ring[:, base:base + words], source).then_inc(loaded[c % SLOTS], 16)

            def load_ffn(packed, first, steps, c0, turns):
                whole = steps // SLOTS
                with sp.Fori(0, whole) as g:
                    for q in range(SLOTS):
                        load(c0 + q, turns + g, packed[bass.ds((first + SLOTS * g + q) * P, P), :], UNIT)
                for q in range(SLOTS * whole, steps):
                    load(c0 + q, turns, packed[bass.ds((first + q) * P, P), :], UNIT)

            sp.dma_start(xT, a["xT"].rearrange("p (k t) -> p k t", k=KT)).then_inc(x_loaded, 16)
            narrow = {1: ("latent1", KT * (LATENT - 512)), 8: ("w_uq", 3 * 768), 9: ("w_ukv", 2 * D), MIX1: ("ple_proj", 2 * D)}
            c = 0
            for l in range(LAYERS):
                wide = 0
                for u in range(MIX1 + PLE):
                    if u in narrow:
                        name, words = narrow[u]
                        load(c, 0, a[name][l * P:(l + 1) * P, :], words)
                    else:
                        load(c, 0, a["first_wide"][(l * 18 + wide) * P:(l * 18 + wide + 1) * P, :])
                        wide += 1
                    c += 1
                    if c == 1:
                        sp.wait_ge(start_loaded, 16 * START_LOADS)
                    if c == SLOTS:
                        sp.dma_start(x_rows[:], a["x_rows"][:, :]).then_inc(start_loaded, 16)
                if l == 0:
                    load_ffn(a["dense"], 0, DENSE_STEPS, c, 0)
                    c += DENSE_STEPS
            with sp.Fori(0, EXPERTS * EXPERT_STEPS // SLOTS) as g:
                for q in range(SLOTS):
                    load(MOE_START + q, g, a["experts"][bass.ds((SLOTS * g + q) * P, P), :], UNIT)
            with sp.Fori(0, LAYERS) as l:
                turns = l * (LAYER2 // SLOTS)
                load_ffn(a["ffn1"], l * FFN_STEPS, FFN_STEPS, BLOCK2, turns)
                for view_, name in ((wsT, "spatial_w"), (bs, "spatial_b")):
                    sp.dma_start(view_, a[name][bass.ds(l * P, P), :].rearrange("p (g t) -> p g t", g=A_GROUPS)).then_inc(s["params"].sem, 16)
                wide = 0
                for u in range(MIX2):
                    c = BLOCK2 + FFN_STEPS + u
                    if u == 3:
                        load(c, turns, a["swa_kv"][bass.ds(l * P, P), :], KT * 256)
                    else:
                        load(c, turns, a["second_wide"][bass.ds((l * (MIX2 - 1) + wide) * P, P), :])
                        wide += 1
                load_ffn(a["ffn2"], l * FFN_STEPS, FFN_STEPS, FFN2_START, turns)
            sp.wait_ge(*once["g"].by(0))
            sp.dma_start(out.rearrange("(h p) d -> p h d", p=P), xn).then_inc(once["stored"].sem, 16)
            sp.wait_ge(*once["stored"].by(0))

        @block.gpsimd
        def _(pool):
            def root(sig, l, name, added, o, mean, eps):
                at = 2 * HEADS * (1 if eps == LN_EPS else 2)
                nc.gpsimd.tensor_tensor(out=o, in0=mean, in1=consts[:, at:at + o.shape[1]], op=ALU.add).then_inc(sig["eps_added"].sem, 1)
                pool.wait_ge(*sig["eps_added"].by(l, added))
                nc.gpsimd.tensor_tensor(out=o, in0=o, in1=consts[:, 0:o.shape[1]], op=ALU.pow).then_inc(sig[name].sem, 1)

            def latent_roots(l):
                for n in range(2):
                    pool.wait_ge(*f["latent_sq"].by(l, 2 * n + 2))
                    root(f, l, "latent_rs", n + 1, rs[:, 2 * n:2 * n + 2], sq[:, 2 * n:2 * n + 2], LN_EPS)

            for n, value in enumerate((-0.5, LN_EPS, RMS_EPS)):
                nc.gpsimd.memset(consts[:, 2 * HEADS * n:2 * HEADS * (n + 1)], value).then_inc(once["consts"].sem, 1)
            pool.wait_ge(*once["consts"].by(0))
            pool.wait_ge(start_loaded, 16 * START_LOADS)
            pool.wait_ge(*once["distances"].by(0))
            for h in range(DVE_HEADS, HEADS):
                nc.gpsimd.tensor_scalar(bias[:, h], causal, table_rows[:, h:h + 1], None, ALU.add).then_inc(once["pool_bias"].sem, 1)
            for b in range(BUCKETS - 1):
                if b == LATENT_BUCKET:
                    latent_roots(0)
                pool.wait_ge(*once["pool_bias"].by(0, (b + 1) * (HEADS - DVE_HEADS)))
                for n, h in enumerate(range(DVE_HEADS, HEADS)):
                    if n > 0:
                        pool.wait_ge(*once["pool_bias"].by(0, (b + 1) * (HEADS - DVE_HEADS) + n))
                    nc.gpsimd.tensor_scalar(step_pool, neg_dist, thresholds[:, b:b + 1], delta[:, b * HEADS + h:b * HEADS + h + 1],
                                            ALU.is_le, ALU.mult).then_inc(once["pool_step"].sem, 1)
                    pool.wait_ge(*once["pool_step"].by(0, b * (HEADS - DVE_HEADS) + n + 1))
                    nc.gpsimd.tensor_tensor(out=bias[:, h], in0=bias[:, h], in1=step_pool, op=ALU.add).then_inc(once["pool_bias"].sem, 1)
            for l in range(LAYERS):
                if l > 0:
                    latent_roots(l)
                if l == 0:
                    pool.wait_ge(*once["bias"].by(0))
                    pool.wait_ge(*once["pool_bias"].by(0))
                else:
                    pool.wait_ge(*f["x"].by(0))
                pool.dma_start(norm_rows, a["ln_mix"][l * P:(l + 1) * P, :].rearrange("p (n d) -> p n d", n=2)).then_inc(f["norm_rows"].sem, 16)
                pool.wait_ge(*f["o_sum"].by(l))
                root(f, l, "o_rs", 3, rs[:, 0:2 * HEADS], sq[:, 0:2 * HEADS], LN_EPS)
                pool.wait_ge(*f["values"].by(l))
                pool.dma_start(pT, a["pT"][l * P:(l + 1) * P, :].rearrange("p (k t) -> p k t", k=2)).then_inc(f["ple_loaded"].sem, 16)
                pool.dma_start(router, a["router"][:, :]).then_inc(f["ple_loaded"].sem, 16)
                pool.wait_ge(*f["ln_aggr"].by(l, 2))
                root(f, l, "ln_rs", 4, rs[:, 0:2], mean_var[:, 0:2, 1], LN_EPS)
                pool.wait_ge(*f["x"].by(l, 2))
                pool.dma_start(norm_rows, a["ln_ffn"][l * P:(l + 1) * P, :].rearrange("p (n d) -> p n d", n=2)).then_inc(f["norm_rows"].sem, 16)
                pool.wait_ge(*f["ln_aggr"].by(l))
                root(f, l, "ln_rs", 5, rs[:, 0:2], mean_var[:, 0:2, 1], LN_EPS)
            pool.wait_ge(*f["x"].by(1))
            pool.dma_start(tables, a["tables2"][:, :]).then_inc(once["tables_loaded"].sem, 16)
            with pool.Fori(0, LAYERS) as l:
                for n in range(2):
                    if n == 1:
                        pool.wait_ge(*s["params"].by(l))
                    pool.wait_ge(*s["sq"].by(l, 2 * n + 2))
                    root(s, l, "rs", n + 1, rs[:, 0:2], sq[:, 0:2], RMS_EPS)
                nc.gpsimd.affine_select(out=wsT, in_=wsT, compare_op=ALU.is_ge, fill=0.0, base=0,
                                        pattern=[[0, A_GROUPS], [1, P]], channel_multiplier=-1).then_inc(s["ws"].sem, 1)
                pool.wait_ge(*s["av_sq"].by(l))
                root(s, l, "av_rs", 3, rs[:, 4:6], sq[:, 4:6], RMS_EPS)
                for n in range(2):
                    pool.wait_ge(*s["o_aggr"].by(l, 4 * n + 4))
                    root(s, l, "o_rs", 4 + n, rs[:, 8 + 4 * n:12 + 4 * n], mean_var[:, 4 + 4 * n:8 + 4 * n, 1], LN_EPS)
                pool.wait_ge(*s["sq"].by(l))
                root(s, l, "rs", 6, rs[:, 0:2], sq[:, 0:2], RMS_EPS)
            pool.wait_ge(*s["mix"].by(1))
            pool.dma_start(last_row, a["final_norm"][:, :]).then_inc(once["row_loaded"].sem, 16)
            pool.wait_ge(*once["sq"].by(0))
            root(once, 0, "rs", 1, rs[:, 0:2], sq[:, 0:2], RMS_EPS)

        @block.tensor
        def _(pe):
            unit_open = [False]

            def count_unit(m):
                if unit_open[0]:
                    m.then_inc(unit_used, 1)
                    unit_open[0] = False

            def end_unit():
                unit_open[0] = True

            def product(terms):
                for i, (o, lhs, rhs) in enumerate(terms):
                    m = pe.matmul(o, lhs, rhs, start=i == 0, stop=i == len(terms) - 1)
                    if i == 0 and len(terms) > 1:
                        count_unit(m)
                return m

            def row_product(o, w, k_tiles, width, lhs, half, column=0):
                return product([(o, lhs[:, k, half * P:(half + 1) * P], w[:, k, column:column + width]) for k in range(k_tiles)])

            def rows(jobs, name, w, k_tiles, width, lhs=xT, column=0):
                for h in range(HALVES):
                    m = row_product(banks(jobs, name)[:, h, 0:width], w, k_tiles, width, lhs, h, column)
                return m

            def columns(jobs, name, w, k_tiles, rhs=xT, column=0):
                for n in range(4):
                    at = column + n * P
                    m = product([(pair(jobs, name)[:, n * SEQ:(n + 1) * SEQ], w[:, k, at:at + P], rhs[:, k, :]) for k in range(k_tiles)])
                return m

            def turn_rows(jobs, name, source, tiles, first):
                for n in range(tiles):
                    for h in range(HALVES):
                        m = pe.transpose(pair(jobs, name)[:, n * SEQ + h * P:n * SEQ + (h + 1) * P],
                                         source[:, h, first + n * P:first + (n + 1) * P], ident[:])
                        if n == 0 and h == 0:
                            count_unit(m)
                return m

            def map_scores(o, q, k):
                count_unit(pe.matmul(o[:, 0:P], q[:, 0:P], k[:, 0:P], start=True, stop=True))
                return pe.matmul(o[:, P:MAP], q[:, P:SEQ], k, start=True, stop=True)

            def turn_map(o, weights):
                for n in range(3):
                    m = pe.transpose(o[:, n * P:(n + 1) * P], weights[:, n * P:(n + 1) * P], ident[:])
                return m

            def pair_values(o, turned, values):
                for m in range(2):
                    om = o[64 * m:64 * m + 64]
                    pe.matmul(om[:, 0:P], values(m, 0), turned[:, m, 0:P], start=True, stop=True)
                    mm = product([(om[:, P:SEQ], values(m, 0), turned[:, m, P:2 * P]),
                                  (om[:, P:SEQ], values(m, 1), turned[:, m, 2 * P:MAP])])
                return mm

            def network(sig, l, steps, c0, turns):
                def up(step, q, t, guarded=True):
                    pe.wait_ge(*landed(c0 + q, t))
                    w = slot(c0 + q, 2 * KT, FF_STEP)
                    for i in range(2):
                        bank = (2 * q + i) % 4
                        if guarded:
                            pe.wait_ge(*sig["gated"].by(l, 2 * step + i - 3))
                        for m in range(2):
                            mm = product([(psum[:, bank, m * SEQ:(m + 1) * SEQ], w[:, m * KT + k, i * P:(i + 1) * P], xT[:, k, :])
                                          for k in range(KT)])
                        mm.then_inc(sig["hidden"].sem, 1)

                def down(step, q, first=False, last=False):
                    base = ((c0 + q) % SLOTS) * UNIT + UP
                    w = ring[:, base:base + 2 * D].rearrange("p (f n) -> p f n", f=2)
                    for i in range(2):
                        pe.wait_ge(*sig["gated"].by(l, 2 * step + i + 1))
                        for h in range(HALVES):
                            for n in range(2):
                                mm = pe.matmul(psum[:, 4 + 2 * h + n], hT[:, (2 * q + i) % 4, h * P:(h + 1) * P],
                                               w[:, i, n * 512:(n + 1) * 512], start=first and i == 0, stop=last and i == 1,
                                               skip_group_check=True)
                    mm.then_inc(unit_used, 1)

                up(0, 0, turns, guarded=False)
                up(1, 1, turns, guarded=False)
                down(0, 0, first=True)
                whole = (steps - 2) // SLOTS
                with pe.Fori(0, whole) as g:
                    for q in range(1, 1 + SLOTS):
                        up(SLOTS * g + q + 1, q + 1, turns + g)
                        down(SLOTS * g + q, q)
                for step in range(SLOTS * whole + 1, steps - 1):
                    up(step + 1, step + 1, turns)
                    down(step, step)
                down(steps - 1, steps - 1, last=True)

            def gather(e, parity):
                pe.wait_ge(*route["hot"].by(e))
                for k in range(KT):
                    mm = product([(psum[:, 6 + k // 4, (k % 4) * P:(k % 4 + 1) * P], X[:, h, k * P:(k + 1) * P], slots_hot[:, parity, h, 0:P])
                                  for h in range(HALVES)])
                mm.then_inc(route["gathered"].sem, 1)

            def chosen_network(e, parity, c0, turns):
                steps = EXPERT_STEPS

                def up(step, q, t, guarded=True):
                    pe.wait_ge(*landed(c0 + q, t))
                    w = slot(c0 + q, 2 * KT, FF_STEP)
                    for i in range(2):
                        bank = (2 * q + i) % 4
                        if guarded:
                            pe.wait_ge(*moe["gated"].by(e, 2 * step + i - 3))
                        for m in range(2):
                            mm = product([(psum[:, bank, m * P:(m + 1) * P], w[:, m * KT + k, i * P:(i + 1) * P], chosen[:, parity, k, 0:P])
                                          for k in range(KT)])
                        mm.then_inc(moe["hidden"].sem, 1)

                def down(step, q, first=False, last=False):
                    base = ((c0 + q) % SLOTS) * UNIT + UP
                    w = ring[:, base:base + 2 * D].rearrange("p (f n) -> p f n", f=2)
                    for i in range(2):
                        pe.wait_ge(*moe["gated"].by(e, 2 * step + i + 1))
                        for n in range(2):
                            mm = pe.matmul(psum[:, 4 + n], hT[:, (2 * q + i) % 4, 0:P], w[:, i, n * 512:(n + 1) * 512],
                                           start=first and i == 0, stop=last and i == 1, skip_group_check=True)
                    mm.then_inc(unit_used, 1)

                pe.wait_ge(*route["columns"].by(e))
                up(0, 0, turns, guarded=False)
                up(1, 1, turns, guarded=False)
                down(0, 0, first=True)
                for q in range(1, 1 + SLOTS):
                    up(q + 1, q + 1, turns)
                    down(q, q)
                    if q == 1:
                        pe.wait_ge(*route["hot"].by(e + 1))
                        for h in range(HALVES):
                            m = pe.transpose(psum[:, 6, h * P:(h + 1) * P], slots_hot[:, parity, h, 0:P], ident[:])
                        m.then_inc(route["turned"].sem, 1)
                    if q == 3:
                        pe.wait_ge(*route["hot_taken"].by(e))
                        gather(e + 1, 1 - parity)
                with pe.Fori(1, (steps - 2) // SLOTS) as g:
                    for q in range(1, 1 + SLOTS):
                        up(SLOTS * g + q + 1, q + 1, turns + g)
                        down(SLOTS * g + q, q)
                down(steps - 1, steps - 1, last=True)
                pe.wait_ge(*route["columns"].by(e + 1))
                pe.wait_ge(*route["y_act"].by(e))
                pe.wait_ge(*route["y_dve"].by(e))
                for h in range(HALVES):
                    for n in range(2):
                        m = pe.matmul(psum[:, (6, 4)[h] + n], tokens_hot[:, h, :], expert_rows[:, n * 512:(n + 1) * 512], start=True, stop=True)
                    m.then_inc(route["scattered"].sem, 1)

            pe.wait_ge(x_loaded, 16)
            c = 0

            for l in range(LAYERS):
                J = JOBS1

                def banks_free(name, l):
                    signal, count = FREED1[list(J)[J[name] - 4]]
                    return f[signal].by(l, count)

                if l == 1:
                    pe.wait_ge(*f["turned_x"].by(0))
                for i, width in enumerate((512, LATENT - 512)):
                    pe.wait_ge(*landed(c, 0))
                    rows(J, f"latent{i}", slot(c, KT, width), KT, width).then_inc(f["full"].sem, 1)
                    end_unit()
                    c += 1
                for name in ("dq0", "dq1", "dk0", "dk1", "dv0", "dv1"):
                    if J[name] >= 4:
                        pe.wait_ge(*banks_free(name, l))
                    pe.wait_ge(*landed(c, 0))
                    w = slot(c, KT, 512)
                    (rows(J, name, w, KT, 512) if name[:2] == "dv" else columns(J, name, w, KT)).then_inc(f["full"].sem, 1)
                    end_unit()
                    c += 1
                if l == 0:
                    pe.wait_ge(start_loaded, 16 * START_LOADS)
                pe.wait_ge(*banks_free("cq_turn", l))
                pe.wait_ge(*f["latent_n"].by(l))
                turn_rows(J, "cq_turn", latent, 3, 0).then_inc(f["full"].sem, 1)
                pe.wait_ge(*banks_free("ckv_turn", l))
                turn_rows(J, "ckv_turn", latent, 2, Q_RANK).then_inc(f["full"].sem, 1)
                for name, k_tiles, width, source in (("uq", 3, 384, cqT), ("ukv", 2, 512, ckvT)):
                    pe.wait_ge(*landed(c, 0))
                    w = slot(c, k_tiles, 2 * width)
                    for h in range(HALVES):
                        pe.wait_ge(*banks_free(f"{name}{h}", l))
                        pe.wait_ge(*f["cqT" if name == "uq" else "ckvT"].by(l))
                        for n in range(2):
                            m = row_product(banks(J, f"{name}{h}")[:, n, 0:width], w, k_tiles, width, source, h, n * width)
                        m.then_inc(f["full"].sem, 1)
                    end_unit()
                    c += 1
                for name, source, ready in (("q", qrow, "q_rot"), ("k", kcat, "kcat")):
                    if name == "k":
                        pe.wait_ge(*f["kv_rows"].by(l))
                    for i in range(2):
                        o = pair(J, f"{name}_turn{i}")
                        pe.wait_ge(*banks_free(f"{name}_turn{i}", l))
                        pe.wait_ge(*f[ready].by(l))
                        for n in range(4):
                            for h in range(HALVES):
                                m = pe.transpose(o[0:MLA_QK, n * SEQ + h * P:n * SEQ + (h + 1) * P], source[:, h, 4 * i + n, :], ident[:])
                                if n == h == 0:
                                    count_unit(m)
                        m.then_inc(f["full"].sem, 1)

                pe.wait_ge(*f["dv"].by(l))
                pe.wait_ge(*f["dk"].by(l))
                pe.wait_ge(*f["dq"].by(l))
                pe.wait_ge(*f["qT"].by(l))
                pe.wait_ge(*f["kT"].by(l))
                for i in range(MAPS1 + 3):
                    if i < MAPS1:
                        pe.wait_ge(*banks_free(f"scores{i}", l))
                        for m in range(2):
                            if i < HEADS:
                                q, k = dqT[64 * m:64 * m + 64, i, :], dkT[64 * m:64 * m + 64, i, :]
                            else:
                                q, k = qT[0:MLA_QK, 2 * (i - HEADS) + m, :], kT[0:MLA_QK, 2 * (i - HEADS) + m, :]
                            mm = map_scores(banks(J, f"scores{i}")[:, m], q, k)
                        mm.then_inc(f["full"].sem, 1)
                    if 0 <= i - 2 < MAPS1:
                        h = i - 2
                        pe.wait_ge(*banks_free(f"turn{h}", l))
                        pe.wait_ge(*f["weighed"].by(l, 4 * h + 4))
                        for m in range(1 if h < HEADS else 2):
                            mm = turn_map(banks(J, f"turn{h}")[:, m], T[:, h % 2, m])
                        mm.then_inc(f["full"].sem, 1)
                    if 0 <= i - 3 < MAPS1:
                        h = i - 3
                        o = pair(J, f"values{h}")
                        pe.wait_ge(*banks_free(f"values{h}", l))
                        pe.wait_ge(*f["turned"].by(l, h + 1))
                        if h < HEADS:
                            w, vh = PT[:, h % 2, 0], dv[:, :, h * P:(h + 1) * P]
                            pe.matmul(o[:, 0:P], w[:, 0:P], vh[:, 0], start=True, stop=True)
                            mm = product([(o[:, P:2 * P], w[:, P:2 * P], vh[:, 0]), (o[:, P:2 * P], w[:, 2 * P:MAP], vh[:, 1])])
                        else:
                            mm = pair_values(o, PT[:, h % 2], lambda m, half: vrow[:, half, 2 * (h - HEADS) + m, :])
                        mm.then_inc(f["full"].sem, 1)

                for i in range(2):
                    pe.wait_ge(*banks_free(f"gate_a{i}", l))
                    pe.wait_ge(*landed(c, 0))
                    columns(J, f"gate_a{i}", slot(c, KT, 512), KT).then_inc(f["full"].sem, 1)
                    end_unit()
                    c += 1
                for i in range(2):
                    pe.wait_ge(*banks_free(f"o_turn{i}", l))
                    pe.wait_ge(*f["o_n"].by(l))
                    turn_rows(J, f"o_turn{i}", xn, 4, 4 * i * P).then_inc(f["full"].sem, 1)
                for i in range(2):
                    pe.wait_ge(*banks_free(f"branch_a{i}", l))
                    pe.wait_ge(*f["oT"].by(l))
                    pe.wait_ge(*landed(c, 0))
                    columns(J, f"branch_a{i}", slot(c, KT, 512), KT, oT).then_inc(f["full"].sem, 1)
                    end_unit()
                    c += 1
                for i in range(2):
                    pe.wait_ge(*banks_free(f"gate_b{i}", l))
                    pe.wait_ge(*landed(c, 0))
                    columns(J, f"gate_b{i}", slot(c, KT, 512), KT).then_inc(f["full"].sem, 1)
                    end_unit()
                    c += 1
                pe.wait_ge(*landed(c, 0))
                for i in range(2):
                    pe.wait_ge(*banks_free(f"branch_b{i}", l))
                    pe.wait_ge(*f["values"].by(l))
                    columns(J, f"branch_b{i}", slot(c, 4, D), 4, obT, 512 * i).then_inc(f["full"].sem, 1)
                end_unit()
                c += 1
                for i in range(2):
                    pe.wait_ge(*banks_free(f"mix{i}", l))
                    pe.wait_ge(*f["mT"].by(l))
                    pe.wait_ge(*landed(c, 0))
                    rows(J, f"mix{i}", slot(c, KT, 512), KT, 512, m1T).then_inc(f["full"].sem, 1)
                    end_unit()
                    c += 1
                pe.wait_ge(*f["ple_loaded"].by(l))
                pe.wait_ge(*landed(c, 0))
                for i in range(2):
                    pe.wait_ge(*banks_free(f"ple_proj{i}", l))
                    rows(J, f"ple_proj{i}", slot(c, 2, D), 2, 512, pT, 512 * i).then_inc(f["full"].sem, 1)
                end_unit()
                c += 1
                for i in range(2):
                    pe.wait_ge(*banks_free(f"x_turn{i}", l))
                    pe.wait_ge(*f["x"].by(l, 2))
                    turn_rows(J, f"x_turn{i}", X, 4, 4 * i * P).then_inc(f["full"].sem, 1)
                for i in range(2):
                    pe.wait_ge(*banks_free(f"ple_gate{i}", l))
                    pe.wait_ge(*f["turned_x"].by(l, 2))
                    pe.wait_ge(*landed(c, 0))
                    rows(J, f"ple_gate{i}", slot(c, KT, 512), KT, 512).then_inc(f["full"].sem, 1)
                    end_unit()
                    c += 1
                pe.wait_ge(*f["ple_sig"].by(l))
                if l == 0:
                    assert c == DENSE_START
                    network(dense, 0, DENSE_STEPS, c, 0)
                    c += DENSE_STEPS
                    for i in range(2):
                        pe.wait_ge(*banks_free(f"end_turn{i}", l))
                        pe.wait_ge(*f["x"].by(l))
                        turn_rows(J, f"end_turn{i}", X, 4, 4 * i * P).then_inc(f["full"].sem, 1)
                else:
                    assert c == MOE_START
                    r = router[:, 0:KT * EXPERTS].rearrange("p (k e) -> p k e", k=KT)
                    for h in range(HALVES):
                        m = row_product(psum[:, 6, h * EXPERTS:(h + 1) * EXPERTS], r, KT, EXPERTS, xT, h)
                    m.then_inc(once["routed"].sem, 1)
                    earlier, ones = (router[:, KT * EXPERTS + EXPERTS + i * P:KT * EXPERTS + EXPERTS + (i + 1) * P] for i in range(2))
                    pe.wait_ge(*once["masked"].by(0))
                    pe.matmul(psum[:, 6, 0:EXPERTS], earlier, mask[:, 0, :], start=True, stop=True)
                    product([(psum[:, 6, EXPERTS:2 * EXPERTS], earlier, mask[:, 1, :]), (psum[:, 6, EXPERTS:2 * EXPERTS], ones, mask[:, 0, :])])
                    product([(psum[:, 6, 2 * EXPERTS:3 * EXPERTS], ones, mask[:, h, :]) for h in range(HALVES)]).then_inc(once["ranked"].sem, 1)
                    pe.wait_ge(*once["counted"].by(0))
                    most = pe.value_load(busiest[0:1, 0:1], min_val=0, max_val=SEQ)

                    def chosen_experts():
                        gather(0, 0)
                        with pe.Fori(0, EXPERTS // 2) as couple:
                            for e in range(2):
                                chosen_network(couple * 2 + e, e, MOE_START + e * EXPERT_STEPS, couple * (2 * EXPERT_STEPS // SLOTS))

                    with pe.If(most <= P):
                        chosen_experts()
                    with pe.Else():
                        with pe.Fori(0, EXPERTS // 2) as couple:
                            for e in range(2):
                                network(moe, couple * 2 + e, EXPERT_STEPS, MOE_START + e * EXPERT_STEPS, couple * (2 * EXPERT_STEPS // SLOTS))

            pe.wait_ge(*once["tables_loaded"].by(0))
            with pe.Fori(0, LAYERS) as l:
                J = JOBS2
                turns = l * (LAYER2 // SLOTS)
                unit = [BLOCK2 + FFN_STEPS]

                def banks_free(name, l):
                    signal, count = FREED2[list(J)[J[name] - 4]]
                    return s[signal].by(l, count)

                def weights(k_tiles, width):
                    pe.wait_ge(*landed(unit[0], turns))
                    return slot(unit[0], k_tiles, width)

                def end_of_unit():
                    end_unit()
                    unit[0] += 1

                def turn_normed(name, n):
                    for i in range(2):
                        if J[f"{name}_turn{i}"] >= 4:
                            pe.wait_ge(*banks_free(f"{name}_turn{i}", l))
                        pe.wait_ge(*s["n"].by(l, 2 * n))
                        turn_rows(J, f"{name}_turn{i}", xn, 4, 4 * i * P).then_inc(s["full"].sem, 1)
                    pe.wait_ge(*s["turned_act"].by(l, 4 * n))
                    pe.wait_ge(*s["turned_dve"].by(l, 4 * n))

                turn_normed("ffn1", 1)
                network(ffn, 2 * l, FFN_STEPS, BLOCK2, turns)
                turn_normed("mix", 2)
                for name in ("a_v", "a_u", "b_q"):
                    if J[name] >= 4:
                        pe.wait_ge(*banks_free(name, l))
                    w = weights(KT, 512)
                    (rows(J, name, w, KT, 512) if name == "a_v" else columns(J, name, w, KT)).then_inc(s["full"].sem, 1)
                    end_of_unit()
                pe.wait_ge(*banks_free("b_kv", l))
                w = weights(KT, 256)
                for n in range(2):
                    for half in range(2):
                        product([(banks(J, "b_kv")[64 * half:64 * half + 64, 0, n * SEQ:(n + 1) * SEQ],
                                  w[:, k, n * SWA_DIM:(n + 1) * SWA_DIM], xT[:, k, :]) for k in range(KT)])
                for h in range(HALVES):
                    m = row_product(banks(J, "b_kv")[:, 1, h * P:(h + 1) * P], w, KT, P, xT, h, P)
                m.then_inc(s["full"].sem, 1)
                end_of_unit()
                pe.wait_ge(*banks_free("c_q", l))
                columns(J, "c_q", weights(KT, 512), KT).then_inc(s["full"].sem, 1)
                end_of_unit()
                pe.wait_ge(*banks_free("c_k", l))
                w = weights(KT, 512)
                columns(J, "c_k", w, KT).then_inc(s["full"].sem, 1)
                o = pair(J, "c_krow")
                pe.wait_ge(*banks_free("c_krow", l))
                row_product(o[:, 0:512], w, KT, 512, xT, 0).then_inc(s["full"].sem, 1)
                end_of_unit()
                o = pair(J, "a_mix")
                pe.wait_ge(*banks_free("a_mix", l))
                pe.wait_ge(*s["av_n"].by(l))
                pe.wait_ge(*s["ws"].by(l))
                for g in range(A_GROUPS):
                    for h in range(HALVES):
                        m = pe.matmul(o[:, g * SEQ + h * P:g * SEQ + (h + 1) * P], v2[:, h, g * P:(g + 1) * P], wsT[:, g, :], start=True, stop=True)
                        if g == h == 0:
                            count_unit(m)
                m.then_inc(s["full"].sem, 1)
                for i in range(2):
                    pe.wait_ge(*banks_free(f"c_v{i}", l))
                    rows(J, f"c_v{i}", weights(KT, 512), KT, 512).then_inc(s["full"].sem, 1)
                    end_of_unit()
                pe.wait_ge(*s["bq"].by(l))
                pe.wait_ge(*s["bkv"].by(l))
                for i in range(MAPS2 + 3):
                    if i < MAPS2:
                        pe.wait_ge(*banks_free(f"scores{i}", l))
                        for m in range(2):
                            mm = map_scores(banks(J, f"scores{i}")[:, m], bqT[64 * m:64 * m + 64, i, :], bkT[64 * m:64 * m + 64, i // 2, :])
                        mm.then_inc(s["full"].sem, 1)
                    if 0 <= i - 2 < MAPS2:
                        h = i - 2
                        pe.wait_ge(*banks_free(f"turn{h}", l))
                        pe.wait_ge(*s["weighed"].by(l, 4 * h + 4))
                        for m in range(2):
                            mm = turn_map(banks(J, f"turn{h}")[:, m], T[:, h % 2, m])
                        mm.then_inc(s["full"].sem, 1)
                    if 0 <= i - 3 < MAPS2:
                        h = i - 3
                        o = pair(J, f"values{h}")
                        pe.wait_ge(*banks_free(f"values{h}", l))
                        pe.wait_ge(*s["turned"].by(l, h + 1))
                        pair_values(o, PT[:, h % 2], lambda m, half: bv[:, half, (h // 2) * 64:(h // 2) * 64 + 64]).then_inc(s["full"].sem, 1)
                for i in range(2):
                    pe.wait_ge(*banks_free(f"c_g{i}", l))
                    rows(J, f"c_g{i}", weights(KT, 512), KT, 512).then_inc(s["full"].sem, 1)
                    end_of_unit()
                o = pair(J, "c_scores")
                pe.wait_ge(*banks_free("c_scores", l))
                pe.wait_ge(*s["ck"].by(l))
                for h in range(C_HEADS):
                    for n in range(HALVES):
                        m = pe.matmul(o[:, h * SEQ + n * P:h * SEQ + (n + 1) * P], c_kT[:, h, n * P:(n + 1) * P], c_qT[:, h, n * P:(n + 1) * P], start=True, stop=True)
                        if h == n == 0:
                            count_unit(m)
                m.then_inc(s["full"].sem, 1)
                o = pair(J, "c_state")
                pe.wait_ge(*banks_free("c_state", l))
                pe.wait_ge(*s["ckw"].by(l))
                pe.wait_ge(*s["cv"].by(l))
                for h in range(C_HEADS):
                    m = pe.matmul(o[:, h * C_V:(h + 1) * C_V], c_kw[:, h, :], cv[:, 0, h * C_V:(h + 1) * C_V], start=True, stop=True)
                m.then_inc(s["full"].sem, 1)
                for n in range(HALVES):
                    o = pair(J, f"c_out{n}")
                    pe.wait_ge(*banks_free(f"c_out{n}", l))
                    pe.wait_ge(*s["scT"].by(l))
                    if n == 1:
                        pe.wait_ge(*s["state"].by(l))
                        pe.wait_ge(*s["cqw"].by(l))
                    for h in range(C_HEADS):
                        terms = [(o[:, h * C_V:(h + 1) * C_V], scT[:, h, n * P:(n + 1) * P], cv[:, n, h * C_V:(h + 1) * C_V])]
                        if n == 1:
                            terms.append((o[:, h * C_V:(h + 1) * C_V], c_qw[:, h, :], state[:, h, :]))
                        m = product(terms)
                    m.then_inc(s["full"].sem, 1)
                for branch, k_tiles, source, ready in (("a", 4, yaT, "yaT"), ("b", 4, ybT, "values"), ("c", KT, ycT, "ycT")):
                    for i in range(2):
                        pe.wait_ge(*banks_free(f"gate_{branch}{i}", l))
                        columns(J, f"gate_{branch}{i}", weights(KT, 512), KT).then_inc(s["full"].sem, 1)
                        end_of_unit()
                    if branch == "c":
                        for i in range(2):
                            pe.wait_ge(*banks_free(f"c_turn{i}", l))
                            pe.wait_ge(*s["yc"].by(l))
                            turn_rows(J, f"c_turn{i}", xn, 4, 4 * i * P).then_inc(s["full"].sem, 1)
                    for i in range(2):
                        pe.wait_ge(*banks_free(f"branch_{branch}{i}", l))
                        pe.wait_ge(*s[ready].by(l))
                        if branch == "c":
                            columns(J, f"branch_c{i}", weights(KT, 512), KT, source).then_inc(s["full"].sem, 1)
                            end_of_unit()
                        else:
                            columns(J, f"branch_{branch}{i}", weights(4, D), 4, source, 512 * i).then_inc(s["full"].sem, 1)
                            if i == 1:
                                end_of_unit()
                for i in range(2):
                    pe.wait_ge(*banks_free(f"mix{i}", l))
                    pe.wait_ge(*s["mT"].by(l))
                    rows(J, f"mix{i}", weights(KT, 512), KT, 512, m2T).then_inc(s["full"].sem, 1)
                    end_of_unit()
                assert unit[0] == FFN2_START
                turn_normed("ffn2", 3)
                network(ffn, 2 * l + 1, FFN_STEPS, FFN2_START, turns)

        @block.scalar
        def _(act):
            def exps(sig, l, i, b, scale):
                act.wait_ge(*sig["negated"].by(l, i + 1))
                for m in range(2):
                    for q, (lo, hi) in enumerate(((0, P), (P, MAP))):
                        nc.scalar.activation(T[:, b, m, lo:hi], T[:, b, m, lo:hi], ACT.Exp, bias=attv[:, i, NEGM, m, q:q + 1],
                                             scale=scale, accum_out=attv[:, i, SUMS, m, q:q + 1]).then_inc(sig["exped"].sem, 1)

            def silus(sig, l, steps):
                def tile(step, parity, i, guarded=True):
                    act.wait_ge(*sig["hidden"].by(l, 2 * step + i + 1))
                    if guarded:
                        act.wait_ge(*sig["gated"].by(l, 2 * step + i - 1))
                    nc.scalar.activation(sil[:, i, :], psum[:, 2 * parity + i, 0:SEQ], ACT.Silu).then_inc(sig["silu"].sem, 1)
                for step in range(2):
                    for i in range(2):
                        tile(step, step, i, guarded=step > 0)
                with act.Fori(1, steps // 2) as g:
                    for parity in range(2):
                        for i in range(2):
                            tile(2 * g + parity, parity, i)
                if steps % 2:
                    for i in range(2):
                        tile(steps - 1, 0, i)

            def chosen_silus(e, parity, c0, turns):
                def tile(step, q, i, guarded=True):
                    act.wait_ge(*moe["hidden"].by(e, 2 * step + i + 1))
                    if guarded:
                        act.wait_ge(*moe["gated"].by(e, 2 * step + i - 1))
                    nc.scalar.activation(sil[:, i, 0:P], psum[:, (2 * q + i) % 4, 0:P], ACT.Silu).then_inc(moe["silu"].sem, 1)

                for step in range(6):
                    for i in range(2):
                        tile(step, step, i, guarded=step > 0)
                    if step == 2:
                        act.wait_ge(*route["turned"].by(e))
                        nc.scalar.copy(tokens_hot, psum[:, 6, 0:SEQ].rearrange("p (h t) -> p h t", h=HALVES)).then_inc(route["hot_taken"].sem, 1)
                    if step == 4:
                        gathered_columns(e + 1, 1 - parity)
                with act.Fori(3, EXPERT_STEPS // 2) as g:
                    for q in range(2):
                        for i in range(2):
                            tile(2 * g + q, q, i)
                act.wait_ge(unit_used, c0 + EXPERT_STEPS + SLOTS * turns)
                nc.scalar.copy(expert_rows[:, 0:512], psum[:, 4]).then_inc(route["y_act"].sem, 1)

            def gathered_columns(e, parity):
                act.wait_ge(*route["gathered"].by(e))
                nc.scalar.copy(chosen[:, parity, :, 0:P], psum[:, 6:8].rearrange("p b (k t) -> p (b k) t", k=4)[:, :, 0:P]).then_inc(route["columns"].sem, 1)

            for place, name in ((ident[:], "identity"), (cols1[:], "columns_first"), (cols2[:], "columns_second"),
                                (causal, "causal"), (lambdas.rearrange("p n q c -> p (n q c)"), "lambdas"), (positions, "positions"),
                                (view(95, BUCKETS * HEADS + BUCKETS), "bias_tables"), (inv_freq, "inv_freq")):
                act.dma_start(place, a[name][:, :]).then_inc(start_loaded, 16)

            act.wait_ge(start_loaded, 16 * START_LOADS)
            for l in range(LAYERS):
                J = JOBS1
                for i, (lo, hi) in enumerate(((0, 512), (512, LATENT))):
                    act.wait_ge(*f["full"].by(l, J[f"latent{i}"] + 1))
                    nc.scalar.copy(latent[:, :, lo:hi], banks(J, f"latent{i}")[:, :, 0:hi - lo]).then_inc(f["latent"].sem, 1)
                act.wait_ge(*f["latent"].by(l))
                for n, (lo, hi) in enumerate(((0, Q_RANK), (Q_RANK, Q_RANK + KV_RANK))):
                    for h in range(HALVES):
                        nc.scalar.activation(xn[:, h, lo:hi], latent[:, h, lo:hi], ACT.Square, scale=(hi - lo) ** -0.5,
                                             accum_out=sq[:, 2 * n + h:2 * n + h + 1]).then_inc(f["latent_sq"].sem, 1)
                if l == 0:
                    act.wait_ge(*once["lam_sum"].by(0))
                    nc.scalar.activation(lam_work[:, 4:4 + 2 * LAYERS], lam_work[:, 0:2 * LAYERS], ACT.Exp).then_inc(once["lam_exp"].sem, 1)
                    act.wait_ge(*once["angles"].by(0))
                    for q in range(2):
                        nc.scalar.activation(trig[:, q], angle[:, 3 + q], ACT.Sin).then_inc(once["trig"].sem, 1)
                for name, place in (("dq", dqT), ("dk", dkT)):
                    for i in range(2):
                        act.wait_ge(*f["full"].by(l, J[f"{name}{i}"] + 1))
                        nc.scalar.copy(place[:, 4 * i:4 * i + 4, :], pair(J, f"{name}{i}").rearrange("p (h t) -> p h t", h=4)).then_inc(f[name].sem, 1)
                for i in range(2):
                    act.wait_ge(*f["full"].by(l, J[f"dv{i}"] + 1))
                    nc.scalar.copy(dv[:, :, 512 * i:512 * i + 512], banks(J, f"dv{i}")).then_inc(f["dv"].sem, 1)
                for h in range(HALVES):
                    act.wait_ge(*f["full"].by(l, J[f"uq{h}"] + 1))
                    nc.scalar.copy(qrow[:, h].rearrange("p (b n) c -> p b (n c)", b=2), banks(J, f"uq{h}")[:, :, 0:384]).then_inc(f["q_rows"].sem, 1)
                act.wait_ge(*f["latent_n"].by(l))
                for h in range(HALVES):
                    act.wait_ge(*f["full"].by(l, J[f"ukv{h}"] + 1))
                    o = pair(J, f"ukv{h}").rearrange("p (n c) -> p n c", n=HEADS)
                    nc.scalar.copy(kcat[:, h, :, 0:NOPE], o[:, :, 0:NOPE]).then_inc(f["kv_rows"].sem, 1)
                    nc.scalar.copy(vrow[:, h], o[:, :, NOPE:]).then_inc(f["kv_rows"].sem, 1)
                for name, place in (("q", qT), ("k", kT)):
                    for i in range(2):
                        act.wait_ge(*f["full"].by(l, J[f"{name}_turn{i}"] + 1))
                        nc.scalar.copy(place[0:MLA_QK, 4 * i:4 * i + 4, :], pair(J, f"{name}_turn{i}")[0:MLA_QK].rearrange("p (h t) -> p h t", h=4)).then_inc(f[name + "T"].sem, 1)
                for i in range(MAPS1 + 2):
                    if i < MAPS1:
                        exps(f, l, i, i % 2, 1.0)
                    if 0 <= i - 1 < MAPS1:
                        h = i - 1
                        maps = 1 if h < HEADS else 2
                        act.wait_ge(*f["full"].by(l, J[f"turn{h}"] + 1))
                        nc.scalar.copy(PT[:, h % 2, 0:maps], banks(J, f"turn{h}")[:, 0:maps, 0:MAP]).then_inc(f["turned"].sem, 1)
                    if 0 <= i - 2 < MAPS1:
                        h = i - 2
                        act.wait_ge(*f["full"].by(l, J[f"values{h}"] + 1))
                        o = pair(J, f"values{h}")[:, 0:SEQ]
                        if h < HEADS:
                            nc.scalar.copy(xn[:, :, h * P:(h + 1) * P], o.rearrange("p (h c) -> p h c", h=2)).then_inc(f["values"].sem, 1)
                        else:
                            nc.scalar.copy(obT[:, h - HEADS, :], o).then_inc(f["values"].sem, 1)

                def gate_tiles(n):
                    for i in range(2):
                        name = f"gate_{'ab'[n]}{i}"
                        act.wait_ge(*f["full"].by(l, J[name] + 1))
                        for t in range(4):
                            col = l * N_COLS1 + COLS1["b_gate"] + KT * n + 4 * i + t
                            nc.scalar.activation(gate1[:, n, 4 * i + t, :], pair(J, name)[:, t * SEQ:(t + 1) * SEQ], ACT.Sigmoid,
                                                 bias=cols1[:, col:col + 1]).then_inc(f["gate"].sem, 1)
                gate_tiles(0)
                gate_tiles(1)
                for i in range(2):
                    act.wait_ge(*f["full"].by(l, J[f"ple_proj{i}"] + 1))
                    nc.scalar.copy(E[:, :, 512 * i:512 * i + 512], banks(J, f"ple_proj{i}")).then_inc(f["ple_rows"].sem, 1)
                for i in range(2):
                    act.wait_ge(*f["full"].by(l, J[f"x_turn{i}"] + 1))
                    nc.scalar.copy(xT[:, 4 * i:4 * i + 4, :], pair(J, f"x_turn{i}").rearrange("p (k t) -> p k t", k=4)).then_inc(f["turned_x"].sem, 1)
                for i in range(2):
                    act.wait_ge(*f["full"].by(l, J[f"ple_gate{i}"] + 1))
                    nc.scalar.activation(xn[:, :, 512 * i:512 * i + 512], banks(J, f"ple_gate{i}"), ACT.Sigmoid).then_inc(f["ple_sig"].sem, 1)
                if l == 0:
                    silus(dense, 0, DENSE_STEPS)
                    for i in range(2):
                        act.wait_ge(*f["full"].by(l, J[f"end_turn{i}"] + 1))
                        nc.scalar.copy(xT[:, 4 * i:4 * i + 4, :], pair(J, f"end_turn{i}").rearrange("p (k t) -> p k t", k=4)).then_inc(f["turned_x"].sem, 1)
                else:
                    act.wait_ge(*once["top_diff"].by(0))
                    nc.scalar.activation(top_gate[:, :, 0:1], top_gate[:, :, 1:2], ACT.Exp).then_inc(once["top_exp"].sem, 1)
                    act.wait_ge(*once["counted"].by(0))
                    most = act.value_load(busiest[0:1, 0:1], min_val=0, max_val=SEQ)

                    def chosen_experts():
                        gathered_columns(0, 0)
                        with act.Fori(0, EXPERTS // 2) as couple:
                            for e in range(2):
                                chosen_silus(couple * 2 + e, e, MOE_START + e * EXPERT_STEPS, couple * (2 * EXPERT_STEPS // SLOTS))

                    with act.If(most <= P):
                        chosen_experts()
                    with act.Else():
                        with act.Fori(0, EXPERTS // 2) as couple:
                            for e in range(2):
                                silus(moe, couple * 2 + e, EXPERT_STEPS)

            def square_rows(sig, l, n, network=None):
                for h in range(HALVES):
                    if network is not None:
                        act.wait_ge(*ffn["taken"].by(network, 2 * h + 2))
                    nc.scalar.activation(xn[:, h], X[:, h], ACT.Square, scale=D ** -0.5, accum_out=sq[:, h:h + 1]).then_inc(sig["sq"].sem, 1)

            act.wait_ge(*f["x"].by(1))
            with act.Fori(0, LAYERS) as l:
                J = JOBS2

                def column(name, k):
                    return cols2[:, bass.ds(l * N_COLS2 + COLS2[name] + k, 1)]

                def turn_in(name, gain, n):
                    act.wait_ge(*s["full"].by(l, J[f"{name}_turn0"] + 1))
                    for k in range(4):
                        nc.scalar.activation(xT[:, k, :], pair(J, f"{name}_turn0")[:, k * SEQ:(k + 1) * SEQ], ACT.Copy,
                                             scale=column(gain, k)).then_inc(s["turned_act"].sem, 1)

                square_rows(s, l, 0)
                turn_in("ffn1", "ffn1", 0)
                silus(ffn, 2 * l, FFN_STEPS)
                square_rows(s, l, 1, 2 * l)
                turn_in("mix", "mix", 1)
                act.wait_ge(*s["full"].by(l, J["a_v"] + 1))
                nc.scalar.activation(v2, banks(J, "a_v"), ACT.Gelu_apprx_tanh).then_inc(s["av"].sem, 1)
                act.wait_ge(*s["av"].by(l))
                for h in range(HALVES):
                    nc.scalar.activation(T[:, h, 0:2].rearrange("p m k -> p (m k)")[:, 0:512], v2[:, h], ACT.Square, scale=512 ** -0.5,
                                         accum_out=sq[:, 4 + h:5 + h]).then_inc(s["av_sq"].sem, 1)
                act.wait_ge(*s["full"].by(l, J["a_u"] + 1))
                nc.scalar.activation(uT, pair(J, "a_u").rearrange("p (k t) -> p k t", k=4), ACT.Gelu_apprx_tanh).then_inc(s["uT"].sem, 1)
                for name, place, sig in (("b_q", bqT, "bq"), ("c_q", c_qT, "cq"), ("c_k", c_kT, "ck")):
                    act.wait_ge(*s["full"].by(l, J[name] + 1))
                    nc.scalar.copy(place, pair(J, name).rearrange("p (k t) -> p k t", k=4)).then_inc(s[sig].sem, 1)
                for i in range(2):
                    act.wait_ge(*s["full"].by(l, J[f"c_v{i}"] + 1))
                    nc.scalar.copy(cv[:, :, 512 * i:512 * i + 512], banks(J, f"c_v{i}")).then_inc(s["cv"].sem, 1)
                for i in range(MAPS2 + 2):
                    if i < MAPS2:
                        exps(s, l, i, i % 2, SWA_DIM ** -0.5)
                        act.wait_ge(*s["sink_diff"].by(l, i + 1))
                        nc.scalar.activation(attv[:, i, SINK], attv[:, i, SINK], ACT.Exp).then_inc(s["sink_exp"].sem, 1)
                    if 0 <= i - 1 < MAPS2:
                        h = i - 1
                        act.wait_ge(*s["full"].by(l, J[f"turn{h}"] + 1))
                        nc.scalar.copy(PT[:, h % 2], banks(J, f"turn{h}")[:, :, 0:MAP]).then_inc(s["turned"].sem, 1)
                    if 0 <= i - 2 < MAPS2:
                        h = i - 2
                        act.wait_ge(*s["full"].by(l, J[f"values{h}"] + 1))
                        nc.scalar.copy(ybT[:, h, :], pair(J, f"values{h}")[:, 0:SEQ]).then_inc(s["values"].sem, 1)
                for i in range(2):
                    act.wait_ge(*s["full"].by(l, J[f"c_g{i}"] + 1))
                    nc.scalar.activation(cg[:, :, 512 * i:512 * i + 512], banks(J, f"c_g{i}"), ACT.Silu).then_inc(s["cg"].sem, 1)
                act.wait_ge(*s["full"].by(l, J["c_state"] + 1))
                nc.scalar.copy(state, pair(J, "c_state").rearrange("p (h e) -> p h e", h=C_HEADS)).then_inc(s["state"].sem, 1)
                for n, branch in enumerate("abc"):
                    if branch == "c":
                        act.wait_ge(*s["mT"].by(l, 2))
                    for i in range(2):
                        name = f"gate_{branch}{i}"
                        act.wait_ge(*s["full"].by(l, J[name] + 1))
                        for t in range(4):
                            nc.scalar.activation(gate2[branch][:, 4 * i + t, :], pair(J, name)[:, t * SEQ:(t + 1) * SEQ], ACT.Sigmoid,
                                                 bias=column("b_gate", KT * n + 4 * i + t)).then_inc(s["gate"].sem, 1)
                for i in range(2):
                    act.wait_ge(*s["full"].by(l, J[f"c_turn{i}"] + 1))
                    for t in range(4):
                        nc.scalar.activation(ycT[:, 4 * i + t, :], pair(J, f"c_turn{i}")[:, t * SEQ:(t + 1) * SEQ], ACT.Copy,
                                             scale=column("ret", 4 * i + t)).then_inc(s["ycT"].sem, 1)
                act.wait_ge(*s["mix"].by(l))
                square_rows(s, l, 2)
                turn_in("ffn2", "ffn2", 2)
                silus(ffn, 2 * l + 1, FFN_STEPS)
                act.wait_ge(*ffn["taken"].by(2 * l + 1))
            square_rows(once, 0, 0)

        @block.vector
        def _(dve):
            v = nc.vector

            def score_max(sig, l, i, b, jobs, biased):
                dve.wait_ge(*sig["full"].by(l, jobs[f"scores{i}"] + 1))
                if i >= 2:
                    dve.wait_ge(*sig["full"].by(l, jobs[f"turn{i - 2}"] + 1))
                for m in range(2):
                    biased(T[:, b, m], banks(jobs, f"scores{i}")[:, m, 0:MAP], m).then_inc(sig["biased"].sem, 1)
                dve.wait_ge(*sig["biased"].by(l, 2 * i + 2))
                for q, (lo, hi) in enumerate(((0, P), (P, MAP))):
                    v.tensor_reduce(attv[:, i, MAXS, :, q], T[:, b, :, lo:hi], AX, ALU.max).then_inc(sig["maxed"].sem, 1)
                dve.wait_ge(*sig["maxed"].by(l, 2 * i + 2))

            def divide(sig, l, i, b):
                dve.wait_ge(*sig["inverse"].by(l, i + 1))
                for m in range(2):
                    for q, (lo, hi) in enumerate(((0, P), (P, MAP))):
                        v.tensor_scalar(T[:, b, m, lo:hi], T[:, b, m, lo:hi], attv[:, i, INV, m, q:q + 1], None, ALU.mult).then_inc(sig["weighed"].sem, 1)

            def gated_tiles(sig, l, steps, c0, turns):
                def tile(step, parity, i, guarded=True):
                    dve.wait_ge(*sig["silu"].by(l, 2 * step + i + 1))
                    if guarded:
                        dve.wait_ge(unit_used, c0 - 1 + step + SLOTS * turns)
                    v.tensor_tensor(hT[:, 2 * parity + i, :], sil[:, i, :], psum[:, 2 * parity + i, SEQ:2 * SEQ], ALU.mult).then_inc(sig["gated"].sem, 1)
                for step in range(2):
                    for i in range(2):
                        tile(step, step, i, guarded=False)
                with dve.Fori(1, steps // 2) as g:
                    for parity in range(2):
                        for i in range(2):
                            tile(2 * g + parity, parity, i)
                if steps % 2:
                    for i in range(2):
                        tile(steps - 1, 0, i)
                dve.wait_ge(unit_used, c0 + steps + SLOTS * turns)

            def map_slots(e, parity):
                slot_number = router[:, KT * EXPERTS + EXPERTS + 2 * P:]
                for h in range(HALVES):
                    v.tensor_scalar(slots_hot[:, parity, h, :], slot_number, slot_of[:, h, bass.ds(e, 1)], None, ALU.is_equal).then_inc(route["hot"].sem, 1)

            def chosen_tiles(e, parity, c0, turns):
                def tile(step, q, i, guarded=True):
                    dve.wait_ge(*moe["silu"].by(e, 2 * step + i + 1))
                    if guarded:
                        dve.wait_ge(unit_used, c0 - 1 + step + SLOTS * turns)
                    v.tensor_tensor(hT[:, (2 * q + i) % 4, 0:P], sil[:, i, 0:P], psum[:, (2 * q + i) % 4, P:2 * P], ALU.mult).then_inc(moe["gated"].sem, 1)

                for step in range(2):
                    for i in range(2):
                        tile(step, step, i, guarded=False)
                map_slots(e + 1, 1 - parity)
                with dve.Fori(1, EXPERT_STEPS // 2) as g:
                    for q in range(2):
                        for i in range(2):
                            tile(2 * g + q, q, i)
                dve.wait_ge(unit_used, c0 + EXPERT_STEPS + SLOTS * turns)
                v.tensor_copy(expert_rows[:, 512:], psum[:, 5]).then_inc(route["y_dve"].sem, 1)
                for h in range(HALVES):
                    dve.wait_ge(*route["scattered"].by(e, h + 1))
                    for n in range(2):
                        part = R[:, h, 512 * n:512 * n + 512]
                        v.scalar_tensor_tensor(out=part, in0=psum[:, (6, 4)[h] + n], scalar=pick[:, h, bass.ds(e, 1)],
                                               in1=part, op0=ALU.mult, op1=ALU.add).then_inc(moe["taken"].sem, 1)
                dve.wait_ge(*moe["taken"].by(e))

            dve.wait_ge(start_loaded, 16 * START_LOADS)
            v.tensor_copy(pos, positions).then_inc(once["setup"].sem, 1)
            v.tensor_tensor(lambdas[:, :, 0, :], lambdas[:, :, 0, :], lambdas[:, :, 1, :], ALU.mult).then_inc(once["setup"].sem, 1)
            dve.wait_ge(once["setup"].sem, 2)
            v.tensor_reduce(lam_work[:, 0:2 * LAYERS], lambdas[:, :, 0, :], AX, ALU.add).then_inc(once["lam_sum"].sem, 1)
            for h in range(HALVES):
                v.tensor_scalar(angle[:, 0, h], inv_freq, pos[:, SEQ + h:SEQ + h + 1], None, ALU.mult).then_inc(once["setup"].sem, 1)
            dve.wait_ge(once["setup"].sem, 4)
            for q in range(2):
                v.tensor_scalar(angle[:, 1 + q], angle[:, 0], 0.5 / math.pi, 0.25 * q, ALU.mult, ALU.add).then_inc(once["setup"].sem, 1)
            dve.wait_ge(once["setup"].sem, 6)
            for sign in (MAGIC, -MAGIC):
                v.tensor_scalar(angle[:, 1:3], angle[:, 1:3], sign, None, ALU.add).then_inc(once["setup"].sem, 1)
                dve.wait_ge(once["setup"].sem, 7 + (sign < 0))
            for part, term in enumerate(TWO_PI):
                for q in range(2):
                    v.scalar_tensor_tensor(out=angle[:, 3 + q], in0=angle[:, 1 + q], scalar=-term,
                                              in1=angle[:, 3 + q] if part else angle[:, 0], op0=ALU.mult, op1=ALU.add).then_inc(once["setup"].sem, 1)
                dve.wait_ge(once["setup"].sem, 10 + 2 * part)
            v.tensor_scalar(angle[:, 4], angle[:, 4], 0.5 * math.pi, None, ALU.add).then_inc(once["setup"].sem, 1)
            dve.wait_ge(once["setup"].sem, 15)
            v.tensor_scalar(angle[:, 3:5], angle[:, 3:5], PI_DOWN, -PI_DOWN, ALU.min, ALU.max).then_inc(once["angles"].sem, 1)
            for h in range(HALVES):
                lo, hi = (0, P) if h == 0 else (P, MAP)
                v.tensor_scalar(neg_dist[:, lo:hi], pos[:, 0:hi - lo], pos[:, SEQ + h:SEQ + h + 1], 0.0, ALU.subtract, ALU.min).then_inc(once["distances"].sem, 1)
            v.tensor_tensor(delta[:, 0:(BUCKETS - 1) * HEADS], table_rows[:, HEADS:], table_rows[:, 0:(BUCKETS - 1) * HEADS], ALU.subtract).then_inc(once["distances"].sem, 1)
            for h in range(DVE_HEADS):
                v.tensor_scalar(bias[:, h], causal, table_rows[:, h:h + 1], None, ALU.add).then_inc(once["bias"].sem, 1)
            dve.wait_ge(*once["distances"].by(0))

            def add_buckets(first, last):
                with dve.Fori(first, last) as b:
                    dve.wait_ge(*once["bias"].by(0, b * DVE_HEADS + DVE_HEADS))
                    v.tensor_scalar(at_least, neg_dist, thresholds[:, bass.ds(b, 1)], None, ALU.is_le).then_inc(once["ind"].sem, 1)
                    dve.wait_ge(*once["ind"].by(0, b + 1))
                    for h in range(DVE_HEADS):
                        v.scalar_tensor_tensor(out=bias[:, h], in0=at_least, scalar=delta[:, bass.ds(b * HEADS + h, 1)],
                                                      in1=bias[:, h], op0=ALU.mult, op1=ALU.add).then_inc(once["bias"].sem, 1)

            for l in range(LAYERS):
                J = JOBS1

                def rotate(x1, x2, y1, y2, h, tmp, base, rotated):
                    if h:
                        dve.wait_ge(*f[rotated].by(l, 2))
                    for n, (x, t) in enumerate(((x1, 1), (x2, 0), (x1, 0), (x2, 1))):
                        t_ = trig[:, t, h].unsqueeze(1).broadcast_to([P, HEADS, HALF_ROPE])
                        v.tensor_tensor(rope_tmp[:, n], x, t_, ALU.mult).then_inc(f[tmp].sem, 1)
                    dve.wait_ge(*f[tmp].by(l, base + 4))
                    return ((y1, rope_tmp[:, 0], rope_tmp[:, 1], ALU.subtract), (y2, rope_tmp[:, 2], rope_tmp[:, 3], ALU.add))

                if l == 0:
                    add_buckets(0, LATENT_BUCKET)
                    dve.wait_ge(*once["lam_exp"].by(0))
                    powers = lam_work[:, 4:4 + 2 * LAYERS].rearrange("p (l w) -> p l w", w=2)
                    v.tensor_tensor(neg_lambda, powers[:, :, 1], powers[:, :, 0], ALU.subtract).then_inc(once["setup"].sem, 1)
                    dve.wait_ge(once["setup"].sem, 16)
                    for n in range(LAYERS):
                        v.tensor_scalar(neg_lambda[:, n:n + 1], neg_lambda[:, n:n + 1], -LAM_INIT[n], None, ALU.add).then_inc(once["setup"].sem, 1)
                    dve.wait_ge(*once["setup"].by(0))
                dve.wait_ge(*f["latent_rs"].by(l))
                for n, (lo, hi) in enumerate(((0, Q_RANK), (Q_RANK, Q_RANK + KV_RANK))):
                    for h in range(HALVES):
                        v.tensor_scalar(latent[:, h, lo:hi], latent[:, h, lo:hi], rs[:, 2 * n + h:2 * n + h + 1], None, ALU.mult).then_inc(f["latent_n"].sem, 1)
                dve.wait_ge(*once["trig"].by(0))
                for h in range(HALVES):
                    lo = Q_RANK + KV_RANK
                    x1, x2 = (latent[:, h, lo + i:lo + i + HALF_ROPE].unsqueeze(1).broadcast_to([P, HEADS, HALF_ROPE]) for i in (0, HALF_ROPE))
                    y1, y2 = (kcat[:, h, :, NOPE + i:NOPE + i + HALF_ROPE] for i in (0, HALF_ROPE))
                    for y, t0_, t1_, op in rotate(x1, x2, y1, y2, h, "kr_tmp", 4 * h, "kcat"):
                        v.tensor_tensor(y, t0_, t1_, op).then_inc(f["kcat"].sem, 1)
                if l == 0:
                    add_buckets(LATENT_BUCKET, QUERY_BUCKET)
                dve.wait_ge(*f["full"].by(l, J["cq_turn"] + 1))
                for k in range(3):
                    col = l * N_COLS1 + COLS1["q_norm"] + k
                    v.tensor_scalar(cqT[:, k, :], pair(J, "cq_turn")[:, k * SEQ:(k + 1) * SEQ], cols1[:, col:col + 1], None, ALU.mult).then_inc(f["cqT"].sem, 1)
                dve.wait_ge(*f["full"].by(l, J["ckv_turn"] + 1))
                for k in range(2):
                    col = l * N_COLS1 + COLS1["kv_norm"] + k
                    v.tensor_scalar(ckvT[:, k, :], pair(J, "ckv_turn")[:, k * SEQ:(k + 1) * SEQ], cols1[:, col:col + 1], None, ALU.mult).then_inc(f["ckvT"].sem, 1)
                dve.wait_ge(*f["kcat"].by(l))
                for h in range(HALVES):
                    dve.wait_ge(*f["q_rows"].by(l, h + 1))
                    x1, x2 = (qrow[:, h, :, NOPE + i:NOPE + i + HALF_ROPE] for i in (0, HALF_ROPE))
                    for y, t0_, t1_, op in rotate(x1, x2, x1, x2, h, "q_tmp", 4 * h, "q_rot"):
                        v.tensor_tensor(y, t0_, t1_, op).then_inc(f["q_rot"].sem, 1)
                if l == 0:
                    add_buckets(QUERY_BUCKET, BUCKETS - 1)
                    dve.wait_ge(*once["bias"].by(0))
                    dve.wait_ge(*once["pool_bias"].by(0))

                def weigh_diff(h):
                    dve.wait_ge(*f["exped"].by(l, 4 * h + 4))
                    v.reciprocal(attv[:, h, INV], attv[:, h, SUMS]).then_inc(f["inverse"].sem, 1)
                    dve.wait_ge(*f["inverse"].by(l, h + 1))
                    v.tensor_scalar(attv[:, h, INV, 1], attv[:, h, INV, 1], neg_lambda[:, l:l + 1], None, ALU.mult).then_inc(f["lam_weight"].sem, 1)
                    for q, (lo, hi) in enumerate(((0, P), (P, MAP))):
                        v.tensor_scalar(T[:, h % 2, 0, lo:hi], T[:, h % 2, 0, lo:hi], attv[:, h, INV, 0, q:q + 1], None, ALU.mult).then_inc(f["weighed"].sem, 1)
                    dve.wait_ge(*f["lam_weight"].by(l, h + 1))
                    dve.wait_ge(*f["weighed"].by(l, 4 * h + 2))
                    for q, (lo, hi) in enumerate(((0, P), (P, MAP))):
                        v.scalar_tensor_tensor(out=T[:, h % 2, 0, lo:hi], in0=T[:, h % 2, 1, lo:hi], scalar=attv[:, h, INV, 1, q:q + 1],
                                                      in1=T[:, h % 2, 0, lo:hi], op0=ALU.mult, op1=ALU.add).then_inc(f["weighed"].sem, 1)

                for i in range(MAPS1 + 1):
                    if i < MAPS1:
                        scale, added = (64 ** -0.5, bias[:, i]) if i < HEADS else (MLA_QK ** -0.5, causal)
                        score_max(f, l, i, i % 2, J, lambda o, x, m: v.scalar_tensor_tensor(
                            out=o, in0=x, scalar=scale, in1=added, op0=ALU.mult, op1=ALU.add))
                        v.tensor_scalar(attv[:, i, NEGM], attv[:, i, MAXS], -1.0, None, ALU.mult).then_inc(f["negated"].sem, 1)
                    if 1 <= i <= HEADS:
                        weigh_diff(i - 1)
                    if i > HEADS:
                        h = i - 1
                        dve.wait_ge(*f["exped"].by(l, 4 * h + 4))
                        v.reciprocal(attv[:, h, INV], attv[:, h, SUMS]).then_inc(f["inverse"].sem, 1)
                        divide(f, l, h, (i - 1) % 2)

                dve.wait_ge(*f["values"].by(l))
                heads = xn.rearrange("p h (n c) -> p h n c", n=HEADS)
                for h in range(HALVES):
                    v.scalar_tensor_tensor(out=squares[:, h], in0=xn[:, h], scalar=1.0 / P, in1=xn[:, h], op0=ALU.mult, op1=ALU.mult).then_inc(f["o_sq"].sem, 1)
                dve.wait_ge(*f["o_sq"].by(l))
                for h in range(HALVES):
                    v.tensor_reduce(sq[:, HEADS * h:HEADS * h + HEADS], squares[:, h].rearrange("p (n c) -> p n c", n=HEADS), AX, ALU.add).then_inc(f["o_sum"].sem, 1)
                dve.wait_ge(*f["o_rs"].by(l))
                for h in range(HALVES):
                    v.tensor_tensor(heads[:, h], heads[:, h], rs[:, HEADS * h:HEADS * h + HEADS].unsqueeze(2).broadcast_to([P, HEADS, P]), ALU.mult).then_inc(f["o_n"].sem, 1)
                col = l * N_COLS1 + COLS1["subln"]
                for i in range(2):
                    dve.wait_ge(*f["full"].by(l, J[f"o_turn{i}"] + 1))
                    v.tensor_scalar(oT[:, 4 * i:4 * i + 4, :], pair(J, f"o_turn{i}").rearrange("p (k t) -> p k t", k=4),
                                           cols1[:, col:col + 1], 1.0 - LAM_INIT[l], ALU.mult, ALU.mult).then_inc(f["oT"].sem, 1)
                for i in range(2):
                    dve.wait_ge(*f["full"].by(l, J[f"branch_a{i}"] + 1))
                    dve.wait_ge(*f["gate"].by(l, 4 * i + 4))
                    v.tensor_tensor(m1T[:, 4 * i:4 * i + 4, :], pair(J, f"branch_a{i}").rearrange("p (k t) -> p k t", k=4),
                                           gate1[:, 0, 4 * i:4 * i + 4, :], ALU.mult).then_inc(f["mT"].sem, 1)
                for i in range(2):
                    dve.wait_ge(*f["full"].by(l, J[f"branch_b{i}"] + 1))
                    dve.wait_ge(*f["gate"].by(l, 12 + 4 * i))
                    g = gate1[:, 1, 4 * i:4 * i + 4, :]
                    v.tensor_tensor(g, pair(J, f"branch_b{i}").rearrange("p (k t) -> p k t", k=4), g, ALU.mult).then_inc(f["m_tmp"].sem, 1)
                    dve.wait_ge(*f["m_tmp"].by(l, i + 1))
                    dve.wait_ge(*f["mT"].by(l, i + 1))
                    m = m1T[:, 4 * i:4 * i + 4, :]
                    v.tensor_tensor(m, m, g, ALU.add).then_inc(f["mT"].sem, 1)
                if l == 0:
                    dve.wait_ge(start_loaded, 16 * (START_LOADS + 1))
                for i in range(2):
                    dve.wait_ge(*f["full"].by(l, J[f"mix{i}"] + 1))
                    part = slice(512 * i, 512 * i + 512)
                    v.scalar_tensor_tensor(out=R[:, :, part], in0=X[:, :, part], scalar=ALPHA, in1=banks(J, f"mix{i}"),
                                                  op0=ALU.mult, op1=ALU.add).then_inc(f["mix"].sem, 1)
                dve.wait_ge(*f["mix"].by(l))

                def layernorm(n):
                    for h in range(HALVES):
                        for j in range(2):
                            v.bn_stats(bn[:, 2 * h + j, :], R[:, h, 512 * j:512 * j + 512]).then_inc(f["ln_stats"].sem, 1)
                    dve.wait_ge(*f["ln_stats"].by(l, 4 * n + 4))
                    for h in range(HALVES):
                        v.bn_aggr(mean_var[:, h], bn[:, 2 * h:2 * h + 2, :]).then_inc(f["ln_aggr"].sem, 1)
                    dve.wait_ge(*f["norm_rows"].by(l, 16 * (n + 1)))
                    dve.wait_ge(*f["ln_aggr"].by(l, 2 * n + 2))
                    for h in range(HALVES):
                        v.scalar_tensor_tensor(out=xn[:, h], in0=R[:, h], scalar=mean_var[:, h, 0:1], in1=norm_rows[:, 0],
                                               op0=ALU.subtract, op1=ALU.mult).then_inc(f["ln_n"].sem, 1)
                    dve.wait_ge(*f["ln_n"].by(l, 2 * n + 2))
                    dve.wait_ge(*f["ln_rs"].by(l, n + 1))
                    for h in range(HALVES):
                        v.scalar_tensor_tensor(out=X[:, h], in0=xn[:, h], scalar=rs[:, h:h + 1], in1=norm_rows[:, 1],
                                               op0=ALU.mult, op1=ALU.add).then_inc(f["x"].sem, 1)
                    dve.wait_ge(*f["x"].by(l, 2 * n + 2))

                layernorm(0)
                for i in range(2):
                    dve.wait_ge(*f["ple_sig"].by(l, i + 1))
                    e = E[:, :, 512 * i:512 * i + 512]
                    v.tensor_tensor(e, xn[:, :, 512 * i:512 * i + 512], e, ALU.mult).then_inc(f["ple_e"].sem, 1)
                dve.wait_ge(*f["ple_e"].by(l))
                v.scalar_tensor_tensor(out=R, in0=X, scalar=ALPHA, in1=E, op0=ALU.mult, op1=ALU.add).then_inc(f["residual"].sem, 1)
                dve.wait_ge(*f["residual"].by(l))
                if l == 0:
                    gated_tiles(dense, 0, DENSE_STEPS, DENSE_START, 0)
                    for h in range(HALVES):
                        for n in range(2):
                            part = R[:, h, 512 * n:512 * n + 512]
                            v.tensor_tensor(part, psum[:, 4 + 2 * h + n], part, ALU.add).then_inc(dense["taken"].sem, 1)
                    dve.wait_ge(*dense["taken"].by(0))
                else:
                    dve.wait_ge(*once["routed"].by(0))
                    v.tensor_copy(logit, psum[:, 6, 0:HALVES * EXPERTS].rearrange("p (h e) -> p h e", h=HALVES)).then_inc(once["logits"].sem, 1)
                    dve.wait_ge(*once["logits"].by(0))
                    for h in range(HALVES):
                        v.max(tops[:, h], logit[:, h]).then_inc(once["tops"].sem, 1)
                    dve.wait_ge(*once["tops"].by(0, 2))
                    for h in range(HALVES):
                        v.max_index(top_idx[:, h * 8:h * 8 + 8], tops[:, h], logit[:, h]).then_inc(once["tops"].sem, 1)
                    v.tensor_tensor(top_gate[:, :, 1:2], tops[:, :, 1:2], tops[:, :, 0:1], ALU.subtract).then_inc(once["top_diff"].sem, 1)
                    dve.wait_ge(*once["tops"].by(0))
                    dve.wait_ge(*once["top_exp"].by(0))
                    v.tensor_copy(top_gate[:, :, 4:6], top_idx[:].rearrange("p (h e) -> p h e", h=HALVES)[:, :, 0:2]).then_inc(once["pick"].sem, 1)
                    v.tensor_scalar(top_gate[:, :, 1:2], top_gate[:, :, 0:1], 1.0, None, ALU.add).then_inc(once["pick"].sem, 1)
                    dve.wait_ge(*once["pick"].by(0, 2))
                    iota = router[:, KT * EXPERTS:KT * EXPERTS + EXPERTS]
                    for which, o in ((0, mask), (1, mask2)):
                        for h in range(HALVES):
                            v.tensor_scalar(o[:, h], iota, top_gate[:, h, 4 + which:5 + which], None, ALU.is_equal).then_inc(once["masked"].sem, 1)
                    dve.wait_ge(*once["masked"].by(0, 4))
                    v.tensor_tensor(mask, mask, mask2, ALU.add).then_inc(once["masked"].sem, 1)
                    dve.wait_ge(*once["masked"].by(0))
                    v.reciprocal(top_gate[:, :, 2:3], top_gate[:, :, 1:2]).then_inc(once["pick"].sem, 1)
                    dve.wait_ge(*once["pick"].by(0, 3))
                    v.tensor_tensor(top_gate[:, :, 3:4], top_gate[:, :, 0:1], top_gate[:, :, 2:3], ALU.mult).then_inc(once["pick"].sem, 1)
                    dve.wait_ge(*once["pick"].by(0, 4))
                    for h in range(HALVES):
                        for which, o in ((0, pick[:, h]), (1, logit[:, h])):
                            v.tensor_scalar(o, iota, top_gate[:, h, 4 + which:5 + which], top_gate[:, h, 2 + which:3 + which],
                                                   ALU.is_equal, ALU.mult).then_inc(once["pick"].sem, 1)
                    dve.wait_ge(*once["pick"].by(0, 8))
                    v.tensor_tensor(pick, pick, logit, ALU.add).then_inc(once["pick"].sem, 1)
                    dve.wait_ge(*once["ranked"].by(0))
                    v.scalar_tensor_tensor(out=slot_of[:, :, 0:EXPERTS], in0=psum[:, 6, 0:2 * EXPERTS].rearrange("p (h e) -> p h e", h=HALVES),
                                           scalar=1.0, in1=mask, op0=ALU.add, op1=ALU.mult).then_inc(once["slotted"].sem, 1)
                    v.memset(slot_of[:, :, EXPERTS:], 0.0).then_inc(once["slotted"].sem, 1)
                    v.tensor_reduce(top_gate[:, 0, 0:1], psum[:, 6, 2 * EXPERTS:3 * EXPERTS], AX, ALU.max).then_inc(once["slotted"].sem, 1)
                    dve.wait_ge(*once["pick"].by(0))
                    dve.wait_ge(*once["slotted"].by(0))
                    v.tensor_copy(busiest[:], top_gate[:, 0, 0:1]).then_inc(once["counted"].sem, 1)
                    dve.wait_ge(*once["counted"].by(0))
                    most = dve.value_load(busiest[0:1, 0:1], min_val=0, max_val=SEQ)

                    def chosen_experts():
                        map_slots(0, 0)
                        with dve.Fori(0, EXPERTS // 2) as couple:
                            for e in range(2):
                                chosen_tiles(couple * 2 + e, e, MOE_START + e * EXPERT_STEPS, couple * (2 * EXPERT_STEPS // SLOTS))

                    with dve.If(most <= P):
                        chosen_experts()
                    with dve.Else():
                        with dve.Fori(0, EXPERTS // 2) as couple:
                            for e in range(2):
                                expert = couple * 2 + e
                                gated_tiles(moe, expert, EXPERT_STEPS, MOE_START + e * EXPERT_STEPS, couple * (2 * EXPERT_STEPS // SLOTS))
                                for h in range(HALVES):
                                    for n in range(2):
                                        part = R[:, h, 512 * n:512 * n + 512]
                                        v.scalar_tensor_tensor(out=part, in0=psum[:, 4 + 2 * h + n], scalar=pick[:, h, bass.ds(expert, 1)],
                                                               in1=part, op0=ALU.mult, op1=ALU.add).then_inc(moe["taken"].sem, 1)
                                dve.wait_ge(*moe["taken"].by(expert))
                layernorm(1)

            dve.wait_ge(*once["tables_loaded"].by(0))
            v.tensor_scalar(neg_sinks, neg_sinks, -1.0, None, ALU.mult).then_inc(once["sinks"].sem, 1)
            dve.wait_ge(*once["sinks"].by(0))

            def norm_rows_of(sig, l, n):
                dve.wait_ge(*sig["rs"].by(l, n + 1))
                for h in range(HALVES):
                    v.tensor_scalar(xn[:, h], X[:, h], rs[:, h:h + 1], None, ALU.mult).then_inc(sig["n"].sem, 1)

            with dve.Fori(0, LAYERS) as l:
                J = JOBS2
                turns = l * (LAYER2 // SLOTS)

                def column(name, k):
                    return cols2[:, bass.ds(l * N_COLS2 + COLS2[name] + k, 1)]

                def turn_in(name, gain):
                    dve.wait_ge(*s["full"].by(l, J[f"{name}_turn1"] + 1))
                    for k in range(4):
                        v.tensor_scalar(xT[:, 4 + k, :], pair(J, f"{name}_turn1")[:, k * SEQ:(k + 1) * SEQ], column(gain, 4 + k), None, ALU.mult).then_inc(s["turned_dve"].sem, 1)

                def add_network(which, c0):
                    gated_tiles(ffn, 2 * l + which, FFN_STEPS, c0, turns)
                    for h in range(HALVES):
                        for n in range(2):
                            part = X[:, h, 512 * n:512 * n + 512]
                            v.scalar_tensor_tensor(out=part, in0=psum[:, 4 + 2 * h + n], scalar=0.5, in1=part, op0=ALU.mult, op1=ALU.add).then_inc(ffn["taken"].sem, 1)
                    dve.wait_ge(*ffn["taken"].by(2 * l + which))

                norm_rows_of(s, l, 0)
                turn_in("ffn1", "ffn1")
                add_network(0, BLOCK2)
                norm_rows_of(s, l, 1)
                turn_in("mix", "mix")
                dve.wait_ge(*s["av_rs"].by(l))
                for h in range(HALVES):
                    v.tensor_scalar(v2[:, h], v2[:, h], rs[:, 4 + h:5 + h], None, ALU.mult).then_inc(s["av_n"].sem, 1)
                dve.wait_ge(*s["full"].by(l, J["b_kv"] + 1))
                v.tensor_copy(bkT, banks(J, "b_kv")[:, 0].rearrange("p (n t) -> p n t", n=2)).then_inc(s["bkv"].sem, 1)
                v.tensor_copy(bv, banks(J, "b_kv")[:, 1, 0:SEQ].rearrange("p (h c) -> p h c", h=2)).then_inc(s["bkv"].sem, 1)
                dve.wait_ge(*s["cq"].by(l))
                v.tensor_tensor(c_qw, c_qT[:, :, P:SEQ], q_decay, ALU.mult).then_inc(s["cqw"].sem, 1)
                dve.wait_ge(*s["full"].by(l, J["c_krow"] + 1))
                v.tensor_tensor(c_kw, pair(J, "c_krow")[:, 0:512].rearrange("p (h d) -> p h d", h=C_HEADS),
                                       k_decay.unsqueeze(2).broadcast_to([P, C_HEADS, P]), ALU.mult).then_inc(s["ckw"].sem, 1)
                dve.wait_ge(*s["full"].by(l, J["a_mix"] + 1))
                for g in range(A_GROUPS):
                    v.scalar_tensor_tensor(out=yaT[:, g].rearrange("p (h t) -> p h t", h=2),
                                                  in0=pair(J, "a_mix")[:, g * SEQ:(g + 1) * SEQ].rearrange("p (h t) -> p h t", h=2),
                                                  scalar=column("v_norm", g), in1=bs[:, g:g + 1, :].broadcast_to([P, 2, P]),
                                                  op0=ALU.mult, op1=ALU.add).then_inc(s["ya_tmp"].sem, 1)
                dve.wait_ge(*s["ya_tmp"].by(l))
                dve.wait_ge(*s["uT"].by(l))
                v.tensor_tensor(yaT, yaT, uT, ALU.mult).then_inc(s["yaT"].sem, 1)
                for i in range(HEADS // 2 + 1):
                    if i < HEADS // 2:
                        score_max(s, l, i, i % 2, J, lambda o, x, m: v.scalar_tensor_tensor(
                            out=o, in0=swa_dist, scalar=-(2.0 ** -(2 * i + m + 1)) * SWA_DIM ** 0.5, in1=x, op0=ALU.mult, op1=ALU.add))
                        negs = neg_sinks[:, bass.ds(l * 2 * HEADS + 4 * i, 4)].rearrange("p (m b) -> p m b", m=2)
                        v.scalar_tensor_tensor(out=attv[:, i, NEGM], in0=attv[:, i, MAXS], scalar=-SWA_DIM ** -0.5, in1=negs,
                                                      op0=ALU.mult, op1=ALU.min).then_inc(s["negated"].sem, 1)
                        dve.wait_ge(*s["negated"].by(l, i + 1))
                        v.tensor_tensor(attv[:, i, SINK], attv[:, i, NEGM], negs, ALU.subtract).then_inc(s["sink_diff"].sem, 1)
                    if i >= 1:
                        h = i - 1
                        dve.wait_ge(*s["exped"].by(l, 4 * h + 4))
                        dve.wait_ge(*s["sink_exp"].by(l, h + 1))
                        v.tensor_tensor(attv[:, h, SUMS], attv[:, h, SUMS], attv[:, h, SINK], ALU.add).then_inc(s["sink_added"].sem, 1)
                        dve.wait_ge(*s["sink_added"].by(l, h + 1))
                        v.reciprocal(attv[:, h, INV], attv[:, h, SUMS]).then_inc(s["inverse"].sem, 1)
                        divide(s, l, h, h % 2)
                dve.wait_ge(*s["full"].by(l, J["c_scores"] + 1))
                for h in range(C_HEADS):
                    v.tensor_tensor(scT[:, h].rearrange("p (c t) -> p c t", c=2), pair(J, "c_scores")[:, h * SEQ:(h + 1) * SEQ].rearrange("p (c t) -> p c t", c=2),
                                           decayT[:, h:h + 1, :].broadcast_to([P, 2, P]), ALU.mult).then_inc(s["scT"].sem, 1)
                for n in range(HALVES):
                    o = pair(J, f"c_out{n}").rearrange("p (h e) -> p h e", h=C_HEADS)
                    dve.wait_ge(*s["full"].by(l, J[f"c_out{n}"] + 1))
                    for h in range(C_HEADS):
                        v.bn_stats(bn[:, 4 + 4 * n + h, :], o[:, h]).then_inc(s["o_stats"].sem, 1)
                    dve.wait_ge(*once["sinks"].by(0))
                    dve.wait_ge(*s["o_stats"].by(l, 4 * n + 4))
                    for h in range(C_HEADS):
                        v.bn_aggr(mean_var[:, 4 + 4 * n + h], bn[:, 4 + 4 * n + h:5 + 4 * n + h, :]).then_inc(s["o_aggr"].sem, 1)
                    at = 8 + 4 * n
                    dve.wait_ge(*s["o_rs"].by(l, n + 1))
                    for h in range(C_HEADS):
                        v.tensor_scalar(xn[:, n, h * C_V:(h + 1) * C_V], o[:, h], mean_var[:, 4 + 4 * n + h, 0:1], rs[:, at + h:at + h + 1],
                                               ALU.subtract, ALU.mult).then_inc(s["o_n"].sem, 1)
                    dve.wait_ge(*s["o_n"].by(l, 4 * n + 4))
                    dve.wait_ge(*s["cg"].by(l))
                    v.tensor_tensor(xn[:, n], xn[:, n], cg[:, n], ALU.mult).then_inc(s["yc"].sem, 1)
                for n, branch in enumerate("abc"):
                    for i in range(2):
                        dve.wait_ge(*s["full"].by(l, J[f"branch_{branch}{i}"] + 1))
                        dve.wait_ge(*s["gate"].by(l, 8 * n + 4 * i + 4))
                        g = gate2[branch][:, 4 * i:4 * i + 4, :]
                        m = m2T[:, 4 * i:4 * i + 4, :]
                        o = pair(J, f"branch_{branch}{i}").rearrange("p (k t) -> p k t", k=4)
                        if n == 0:
                            v.tensor_tensor(m, o, g, ALU.mult).then_inc(s["mT"].sem, 1)
                        else:
                            v.tensor_tensor(g, o, g, ALU.mult).then_inc(s["m_tmp"].sem, 1)
                            dve.wait_ge(*s["m_tmp"].by(l, 2 * (n - 1) + i + 1))
                            dve.wait_ge(*s["mT"].by(l, 2 * (n - 1) + i + 1))
                            v.tensor_tensor(m, m, g, ALU.add).then_inc(s["mT"].sem, 1)
                for i in range(2):
                    dve.wait_ge(*s["full"].by(l, J[f"mix{i}"] + 1))
                    part = X[:, :, 512 * i:512 * i + 512]
                    v.tensor_tensor(part, banks(J, f"mix{i}"), part, ALU.add).then_inc(s["mix"].sem, 1)
                dve.wait_ge(*s["mix"].by(l))
                norm_rows_of(s, l, 2)
                turn_in("ffn2", "ffn2")
                add_network(1, FFN2_START)

            norm_rows_of(once, 0, 0)
            dve.wait_ge(*once["n"].by(0))
            dve.wait_ge(*once["row_loaded"].by(0))
            for h in range(HALVES):
                v.tensor_tensor(xn[:, h], xn[:, h], last_row, ALU.mult).then_inc(once["g"].sem, 1)


def causal_map():
    q, k = np.arange(P)[:, None], np.arange(P)[None, :]
    own = np.where(k <= q, 0.0, NEG)
    return np.concatenate([own, np.zeros((P, P)), own], axis=1).astype(np.float32)


def window_map():
    q, k = np.arange(P)[:, None], np.arange(P)[None, :]
    own = np.where(k <= q, q - k, -NEG)
    before = np.where(q + P - k < P, q + P - k, -NEG)
    return np.concatenate([own, before, own], axis=1).astype(np.float32)


def retention_tables():
    log_gamma = np.log(1.0 - np.exp2(-5.0 - np.arange(C_HEADS, dtype=np.float32))).astype(np.float32)
    i = np.arange(P, dtype=np.float32)
    dist = i[None, :] - i[:, None]
    scale = P ** -0.5
    decay = np.where(dist[:, None, :] >= 0, np.exp(log_gamma[None, :, None] * np.maximum(dist, 0)[:, None, :]), 0.0) * scale
    queries = np.broadcast_to(np.exp(log_gamma[:, None] * (i + 1.0)[None, :]), (P, C_HEADS, P))
    keys = np.exp(log_gamma[None, :] * (P - 1.0 - i)[:, None]) * scale
    return [x.reshape(P, -1).astype(np.float32) for x in (decay, queries, keys)]


def tiles(w):
    k, n = w.shape
    return w.reshape(k // P, P, n).transpose(1, 0, 2).reshape(P, -1)


def column_blocks(w, width=512):
    return [tiles(w[:, i:i + width]) for i in range(0, w.shape[1], width)]


def network_units(w1, w3, w2):
    out = []
    for i in range(0, w1.shape[1], FF_STEP):
        out.append(np.concatenate([tiles(w1[:, i:i + FF_STEP]), tiles(w3[:, i:i + FF_STEP]), tiles(w2[i:i + FF_STEP])], axis=1))
    return out


def on_columns(vector):
    return vector.reshape(-1, P).T


def repeated(vector):
    return np.broadcast_to(np.asarray(vector).reshape(1, -1), (P, np.asarray(vector).size))


def arrange(i):
    x = i["x"][0]
    w_in, wide, latent1, uq, ukv = i["w_in"], [], [], [], []
    qkv = 3 * D
    for l in range(LAYERS):
        w = w_in[l]
        latent_cols = w[:, qkv:qkv + LATENT]
        gate = w[:, qkv + LATENT:]
        wide += [tiles(latent_cols[:, :512])] + column_blocks(w[:, :qkv])
        latent1.append(tiles(latent_cols[:, 512:]))
        uq.append(tiles(i["w_uq"][l]))
        ukv.append(tiles(i["w_ukv"][l]))
        wide += column_blocks(gate[:, :D]) + column_blocks(i["w_branch_diff"][l]) + column_blocks(gate[:, D:])
        wide += [tiles(i["w_branch_mla"][l])] + column_blocks(i["w_out"][l]) + column_blocks(i["w_ple_gate"][l])
    a = dict(
        xT=tiles(np.ascontiguousarray(x.T)), x_rows=tiles(x),
        first_wide=np.concatenate(wide), latent1=np.concatenate(latent1), w_uq=np.concatenate(uq), w_ukv=np.concatenate(ukv),
        ple_proj=np.concatenate([tiles(w) for w in i["w_ple_proj"]]),
        dense=np.concatenate(network_units(i["dense_w1"][0], i["dense_w3"][0], i["dense_w2"][0])),
        experts=np.concatenate([u for e in range(EXPERTS) for u in network_units(i["expert_w1"][0, e], i["expert_w3"][0, e], i["expert_w2"][0, e])]),
        pT=np.concatenate([tiles(np.ascontiguousarray(p[0].T)) for p in i["p"]]),
        ln_mix=np.concatenate([np.concatenate([repeated(i["ln_mix_g"][l]), repeated(i["ln_mix_b"][l])], axis=1) for l in range(LAYERS)]),
        ln_ffn=np.concatenate([np.concatenate([repeated(i["ln_ffn_g"][l]), repeated(i["ln_ffn_b"][l])], axis=1) for l in range(LAYERS)]),
        router=np.concatenate([tiles(i["router_w"][0]), repeated(np.arange(EXPERTS, dtype=np.float32)),
                               np.triu(np.ones((P, P), np.float32), 1), np.ones((P, P), np.float32),
                               repeated(np.arange(1, P + 1, dtype=np.float32))], axis=1),
        lambdas=np.concatenate([repeated(i[n][l]) for l in range(LAYERS) for n in ("lambda_q1", "lambda_k1", "lambda_q2", "lambda_k2")], axis=1),
        positions=np.concatenate([repeated(i["positions"][0]), on_columns(i["positions"][0])], axis=1),
        bias_tables=np.concatenate([repeated(i["rel_bias_table"]), repeated(np.array([-t for t in t5_thresholds()] + [0], np.float32))], axis=1),
        inv_freq=repeated(np.float32(10000.0) ** (-np.arange(HALF_ROPE, dtype=np.float32) / np.float32(HALF_ROPE))),
        columns_first=np.concatenate([on_columns(i[n][l]) for l in range(LAYERS) for n in ("b_gate", "diff_subln_g", "mla_q_norm_g", "mla_kv_norm_g")], axis=1),
        identity=np.eye(P, dtype=np.float32), causal=causal_map())

    wide, kv = [], []
    cuts = np.cumsum([512, 512, 512, 128, 128, 512, 512, 1024, 1024, 3072])[:-1]
    for l in range(LAYERS):
        a_u, a_v, b_q, b_k, b_v, c_q, c_k, c_v, c_g, gate = np.split(i["w_in_2"][l], cuts, axis=1)
        kv.append(tiles(np.concatenate([b_k, b_v], axis=1)))
        for w in (a_v, a_u, b_q, c_q, c_k, c_v, c_g, gate[:, :D]):
            wide += column_blocks(w)
        wide += [tiles(i["w_branch_a_2"][l])] + column_blocks(gate[:, D:2 * D]) + [tiles(i["w_branch_b_2"][l])]
        wide += column_blocks(gate[:, 2 * D:]) + column_blocks(i["w_branch_c_2"][l]) + column_blocks(i["w_out_2"][l])
    decay, queries, keys = retention_tables()
    a.update(
        second_wide=np.concatenate(wide), swa_kv=np.concatenate(kv),
        ffn1=np.concatenate([u for l in range(LAYERS) for u in network_units(i["ffn1_w_in_2"][l][:, :D_FF], i["ffn1_w_in_2"][l][:, D_FF:], i["ffn1_w_out_2"][l])]),
        ffn2=np.concatenate([u for l in range(LAYERS) for u in network_units(i["ffn2_w_in_2"][l][:, :D_FF], i["ffn2_w_in_2"][l][:, D_FF:], i["ffn2_w_out_2"][l])]),
        spatial_w=np.concatenate([np.ascontiguousarray(w.transpose(2, 0, 1)).reshape(P, -1) for w in i["gmlp_w_s_2"]]),
        spatial_b=np.concatenate([repeated(b) for b in i["gmlp_b_s_2"]]),
        columns_second=np.concatenate([on_columns(i[n][l]) for l in range(LAYERS) for n in ("ffn1_norm_2", "mix_norm_2", "b_gate_2", "gmlp_v_norm_2", "ret_gn_2", "ffn2_norm_2")], axis=1),
        tables2=np.concatenate([decay, queries, window_map(), keys, repeated(np.repeat(i["attn_sinks_2"].reshape(-1), 2))], axis=1),
        final_norm=repeated(i["final_norm_2"]))
    return {name: np.ascontiguousarray(array) for name, array in a.items()}


def kernel(**inputs):
    import concourse.bacc as bacc
    from concourse.bass_utils import run_bass_kernel_spmd

    arrays = arrange({name: np.asarray(value) for name, value in inputs.items()})
    nc = bacc.Bacc("TRN2", target_bir_lowering=False, num_devices=1)
    places = {name: nc.dram_tensor(f"in_{name}", x.shape, mybir.dt.from_np(x.dtype), kind="ExternalInput").ap() for name, x in arrays.items()}
    out = nc.dram_tensor("out", (SEQ, D), F32, kind="ExternalOutput").ap()
    build(nc, places, out)
    result = run_bass_kernel_spmd(nc, [{f"in_{name}": x for name, x in arrays.items()}], core_ids=[0])
    return result.results[0]["out"].reshape(1, SEQ, D)
```
